# Optimizing a Trainium2 kernel written in Bass

```python
import math
import jax, jax.numpy as jnp
from jax import lax
import numpy as np

"""Four-layer hybrid decoder trunk: interleaved RG-LRU (even layers) and mLSTM (odd layers)
token mixers, each layer followed by a SwiGLU channel mixer and a sigmoid-gated per-layer
input embedding. One inference step for a prompt group and a sample group sharing weights.

Inputs:
  x_prompt (BATCH, SEQ, D_MODEL), x_sample (DEC_BATCH, DEC_SEQ, D_MODEL)
  state_rglru_conv (N_LAYERS_A, DEC_BATCH, CONV_W-1, D_RNN)
  state_rglru_h    (N_LAYERS_A, DEC_BATCH, D_RNN)
  state_mlstm_conv (N_LAYERS_B, DEC_BATCH, CONV_W-1, INNER_M)
  state_mlstm_C    (N_LAYERS_B, DEC_BATCH, N_HEADS_M, HEAD_DIM_M, HEAD_DIM_M)
  state_mlstm_n    (N_LAYERS_B, DEC_BATCH, N_HEADS_M, HEAD_DIM_M)
  state_mlstm_m    (N_LAYERS_B, DEC_BATCH, N_HEADS_M)
  p_prompt (DEPTH, BATCH, SEQ, PLE_DIM), p_sample (DEPTH, DEC_BATCH, DEC_SEQ, PLE_DIM)
  then all weights.
Output tuple:
  (y_prompt (BATCH, SEQ, D_MODEL), y_sample (DEC_BATCH, DEC_SEQ, D_MODEL),
   rglru_conv_p, rglru_h_p, mlstm_conv_p, mlstm_C_p, mlstm_n_p, mlstm_m_p   [leading dim BATCH after layer axis],
   rglru_conv_s, rglru_h_s, mlstm_conv_s, mlstm_C_s, mlstm_n_s, mlstm_m_s   [leading dim DEC_BATCH after layer axis])
  each state in the layout of the corresponding state_ input.
"""

D_MODEL = 1024
BATCH = 1
SEQ = 512
DEPTH = 2
DEC_BATCH = 8
DEC_SEQ = 8
PAST_LEN = 4096
PAGE_SIZE = 128

N_MIXERS = 2
N_LAYERS_A = (DEPTH + 1) // 2
N_LAYERS_B = DEPTH // 2
PLE_DIM = 256
CONV_W = 4
D_RNN = 1536
N_BLOCKS_A = 6
BLOCK_A = D_RNN // N_BLOCKS_A
LRU_C = 8.0
INNER_M = 2 * D_MODEL
N_HEADS_M = 4
HEAD_DIM_M = INNER_M // N_HEADS_M
QKV_BLOCK = 4
N_QKV_BLOCKS = INNER_M // QKV_BLOCK
CHUNK_M = 64
D_FF = ((8 * D_MODEL + 3 * 256 - 1) // (3 * 256)) * 256
EPS = 1e-6

kernel_name = "hybrid_rglru_mlstm_decoder_step"

def rms_norm(x, g):
    xf = x.astype(jnp.float32)
    y = xf * lax.rsqrt(jnp.mean(xf * xf, axis=-1, keepdims=True) + EPS)
    return y.astype(x.dtype) * g

def causal_conv(x, buf, w, b):
    L = x.shape[1]
    xcat = jnp.concatenate([buf.astype(x.dtype), x], axis=1)
    y = b + sum(w[j] * xcat[:, j:j + L] for j in range(CONV_W))
    return y, xcat[:, L:]

def block_diag(x, w):
    nb, bi, bo = w.shape
    xs = x.reshape(*x.shape[:-1], nb, bi)
    return jnp.einsum('...ni,nio->...no', xs, w).reshape(*x.shape[:-1], nb * bo)

def _linear_combine(left, right):
    a_l, u_l = left
    a_r, u_r = right
    return a_l * a_r, a_r * u_l + u_r

def rglru_mixer(x, conv_buf, h0, w_in, conv_w, conv_b, w_r, b_r, w_i, b_i, lam, w_out):
    gate_branch, xb = jnp.split(x @ w_in, 2, axis=-1)
    xc, new_buf = causal_conv(xb, conv_buf, conv_w, conv_b)
    r = jax.nn.sigmoid((block_diag(xc, w_r) + b_r).astype(jnp.float32))
    ig = jax.nn.sigmoid((block_diag(xc, w_i) + b_i).astype(jnp.float32))
    log_a = -LRU_C * r * jax.nn.softplus(-lam.astype(jnp.float32))
    a = jnp.exp(log_a)
    u = jnp.sqrt(-jnp.expm1(2.0 * log_a)) * (ig * xc.astype(jnp.float32))
    u = u.at[:, 0].add(a[:, 0] * h0.astype(jnp.float32))
    _, h = lax.associative_scan(_linear_combine, (a, u), axis=1)
    y = (h.astype(x.dtype) * jax.nn.gelu(gate_branch)) @ w_out
    return y, new_buf, h[:, -1].astype(x.dtype)

def mlstm_chunkwise(q, k, v, log_i, log_f, C0, n0, m0):
    B, H, L, _ = q.shape
    c = CHUNK_M if L % CHUNK_M == 0 else L
    nc = L // c

    def to_chunks(t):
        return jnp.moveaxis(t.reshape(B, H, nc, c, *t.shape[3:]), 2, 0)

    causal = jnp.tril(jnp.ones((c, c), dtype=bool))

    def step(carry, xs):
        C, n, m = carry
        qc, kc, vc, li, lf = xs
        b = jnp.cumsum(lf, axis=-1)
        g = b + m[..., None]
        Dm = b[..., :, None] - b[..., None, :] + li[..., None, :]
        Dm = jnp.where(causal, Dm, -jnp.inf)
        m_t = jnp.maximum(g, jnp.max(Dm, axis=-1))
        inter = jnp.exp(g - m_t)
        S = jnp.einsum('bhtd,bhsd->bhts', qc, kc) * jnp.exp(Dm - m_t[..., None])
        num = inter[..., None] * jnp.einsum('bhtk,bhkv->bhtv', qc, C) + jnp.einsum('bhts,bhsv->bhtv', S, vc)
        den = inter * jnp.einsum('bhtk,bhk->bht', qc, n) + jnp.sum(S, axis=-1)
        h = num / jnp.maximum(jnp.abs(den), jnp.exp(-m_t))[..., None]
        b_last = b[..., -1]
        dec = b_last[..., None] - b + li
        m_new = jnp.maximum(b_last + m, jnp.max(dec, axis=-1))
        w_s = jnp.exp(dec - m_new[..., None])
        scale = jnp.exp(b_last + m - m_new)
        kw = kc * w_s[..., None]
        C_new = scale[..., None, None] * C + jnp.einsum('bhsk,bhsv->bhkv', kw, vc)
        n_new = scale[..., None] * n + jnp.sum(kw, axis=2)
        return (C_new, n_new, m_new), h

    init = (C0.astype(jnp.float32), n0.astype(jnp.float32), m0.astype(jnp.float32))
    (C, n, m), hs = lax.scan(step, init, (to_chunks(q), to_chunks(k), to_chunks(v), to_chunks(log_i), to_chunks(log_f)))
    h = jnp.moveaxis(hs, 0, 2).reshape(B, H, L, hs.shape[-1])
    return h, C, n, m

def mlstm_mixer(x, conv_buf, C0, n0, m0, w_in, conv_w, conv_b, w_q, w_k, w_v, w_gates, b_gates, norm_g, w_out):
    B, L, _ = x.shape
    xm, o_pre = jnp.split(x @ w_in, 2, axis=-1)
    xc, new_buf = causal_conv(xm, conv_buf, conv_w, conv_b)
    xc = jax.nn.silu(xc)
    q = block_diag(xc, w_q)
    k = block_diag(xc, w_k) * (HEAD_DIM_M ** -0.5)
    v = block_diag(xm, w_v)
    gates = (jnp.concatenate([q, k, v], axis=-1) @ w_gates + b_gates).astype(jnp.float32)
    log_i = jnp.moveaxis(gates[..., :N_HEADS_M], 1, 2)
    log_f = jnp.moveaxis(jax.nn.log_sigmoid(gates[..., N_HEADS_M:]), 1, 2)

    def to_heads(t):
        return t.reshape(B, L, N_HEADS_M, HEAD_DIM_M).transpose(0, 2, 1, 3).astype(jnp.float32)

    h, C, n, m = mlstm_chunkwise(to_heads(q), to_heads(k), to_heads(v), log_i, log_f, C0, n0, m0)
    h = h * lax.rsqrt(jnp.mean(h * h, axis=-1, keepdims=True) + EPS)
    h = h.transpose(0, 2, 1, 3).reshape(B, L, INNER_M).astype(x.dtype) * norm_g
    y = (jax.nn.sigmoid(o_pre) * h) @ w_out
    return y, new_buf, C.astype(x.dtype), n.astype(x.dtype), m.astype(x.dtype)

def swiglu(x, w_up, w_down):
    gate, up = jnp.split(x @ w_up, 2, axis=-1)
    return (jax.nn.silu(gate) * up) @ w_down

def trunk(x, p, rg_conv, rg_h, ml_conv, ml_C, ml_n, ml_m,
          norm_mix, norm_ffn, norm_final,
          rg_w_in, rg_conv_w, rg_conv_b, rg_w_r, rg_b_r, rg_w_i, rg_b_i, rg_lambda, rg_w_out,
          ml_w_in, ml_conv_w, ml_conv_b, ml_w_q, ml_w_k, ml_w_v, ml_w_gates, ml_b_gates, ml_norm, ml_w_out,
          ffn_w_up, ffn_w_down, ple_w_proj, ple_w_gate, ple_b_gate):
    new_rg_conv, new_rg_h = [], []
    new_ml_conv, new_ml_C, new_ml_n, new_ml_m = [], [], [], []
    for i in range(DEPTH):
        j = i // N_MIXERS
        xn = rms_norm(x, norm_mix[i])
        if i % N_MIXERS == 0:
            y, cb, hl = rglru_mixer(xn, rg_conv[j], rg_h[j], rg_w_in[j], rg_conv_w[j], rg_conv_b[j],
                                    rg_w_r[j], rg_b_r[j], rg_w_i[j], rg_b_i[j], rg_lambda[j], rg_w_out[j])
            new_rg_conv.append(cb)
            new_rg_h.append(hl)
        else:
            y, cb, Cn, nn_, mn = mlstm_mixer(xn, ml_conv[j], ml_C[j], ml_n[j], ml_m[j], ml_w_in[j], ml_conv_w[j],
                                             ml_conv_b[j], ml_w_q[j], ml_w_k[j], ml_w_v[j], ml_w_gates[j],
                                             ml_b_gates[j], ml_norm[j], ml_w_out[j])
            new_ml_conv.append(cb)
            new_ml_C.append(Cn)
            new_ml_n.append(nn_)
            new_ml_m.append(mn)
        x = x + y
        x = x + swiglu(rms_norm(x, norm_ffn[i]), ffn_w_up[i], ffn_w_down[i])
        gate = jax.nn.sigmoid(x @ ple_w_gate[i] + ple_b_gate[i])
        x = x + gate * (p[i] @ ple_w_proj[i])
    y = rms_norm(x, norm_final)
    return (y, jnp.stack(new_rg_conv), jnp.stack(new_rg_h), jnp.stack(new_ml_conv),
            jnp.stack(new_ml_C), jnp.stack(new_ml_n), jnp.stack(new_ml_m))

def setup_inputs(seed: int = 0) -> dict:
    key = jax.random.key(seed)
    keys = iter(jax.random.split(key, 48))

    def nrm(shape, scale):
        return jax.random.normal(next(keys), shape, jnp.float32) * scale

    def unif(shape, lo, hi):
        return jax.random.uniform(next(keys), shape, jnp.float32, minval=lo, maxval=hi)

    lam_a = unif((N_LAYERS_A, D_RNN), 0.9, 0.999)
    b_gates = jnp.concatenate([nrm((N_LAYERS_B, N_HEADS_M), 0.1),
                               unif((N_LAYERS_B, N_HEADS_M), 3.0, 6.0)], axis=-1)
    return {
        "x_prompt": nrm((BATCH, SEQ, D_MODEL), 1.0),
        "x_sample": nrm((DEC_BATCH, DEC_SEQ, D_MODEL), 1.0),
        "state_rglru_conv": nrm((N_LAYERS_A, DEC_BATCH, CONV_W - 1, D_RNN), 1.0),
        "state_rglru_h": nrm((N_LAYERS_A, DEC_BATCH, D_RNN), 0.5),
        "state_mlstm_conv": nrm((N_LAYERS_B, DEC_BATCH, CONV_W - 1, INNER_M), 1.0),
        "state_mlstm_C": nrm((N_LAYERS_B, DEC_BATCH, N_HEADS_M, HEAD_DIM_M, HEAD_DIM_M), 0.1),
        "state_mlstm_n": nrm((N_LAYERS_B, DEC_BATCH, N_HEADS_M, HEAD_DIM_M), 0.1),
        "state_mlstm_m": nrm((N_LAYERS_B, DEC_BATCH, N_HEADS_M), 1.0),
        "p_prompt": nrm((DEPTH, BATCH, SEQ, PLE_DIM), 1.0),
        "p_sample": nrm((DEPTH, DEC_BATCH, DEC_SEQ, PLE_DIM), 1.0),
        "norm_mix": 1.0 + nrm((DEPTH, D_MODEL), 0.01),
        "norm_ffn": 1.0 + nrm((DEPTH, D_MODEL), 0.01),
        "norm_final": 1.0 + nrm((D_MODEL,), 0.01),
        "rg_w_in": nrm((N_LAYERS_A, D_MODEL, 2 * D_RNN), D_MODEL ** -0.5),
        "rg_conv_w": nrm((N_LAYERS_A, CONV_W, D_RNN), CONV_W ** -0.5),
        "rg_conv_b": nrm((N_LAYERS_A, D_RNN), 0.01),
        "rg_w_r": nrm((N_LAYERS_A, N_BLOCKS_A, BLOCK_A, BLOCK_A), BLOCK_A ** -0.5),
        "rg_b_r": nrm((N_LAYERS_A, D_RNN), 0.01),
        "rg_w_i": nrm((N_LAYERS_A, N_BLOCKS_A, BLOCK_A, BLOCK_A), BLOCK_A ** -0.5),
        "rg_b_i": nrm((N_LAYERS_A, D_RNN), 0.01),
        "rg_lambda": jnp.log(lam_a) - jnp.log1p(-lam_a),
        "rg_w_out": nrm((N_LAYERS_A, D_RNN, D_MODEL), D_RNN ** -0.5),
        "ml_w_in": nrm((N_LAYERS_B, D_MODEL, 2 * INNER_M), D_MODEL ** -0.5),
        "ml_conv_w": nrm((N_LAYERS_B, CONV_W, INNER_M), CONV_W ** -0.5),
        "ml_conv_b": nrm((N_LAYERS_B, INNER_M), 0.01),
        "ml_w_q": nrm((N_LAYERS_B, N_QKV_BLOCKS, QKV_BLOCK, QKV_BLOCK), QKV_BLOCK ** -0.5),
        "ml_w_k": nrm((N_LAYERS_B, N_QKV_BLOCKS, QKV_BLOCK, QKV_BLOCK), QKV_BLOCK ** -0.5),
        "ml_w_v": nrm((N_LAYERS_B, N_QKV_BLOCKS, QKV_BLOCK, QKV_BLOCK), QKV_BLOCK ** -0.5),
        "ml_w_gates": nrm((N_LAYERS_B, 3 * INNER_M, 2 * N_HEADS_M), 0.1 * (3 * INNER_M) ** -0.5),
        "ml_b_gates": b_gates,
        "ml_norm": 1.0 + nrm((N_LAYERS_B, INNER_M), 0.01),
        "ml_w_out": nrm((N_LAYERS_B, INNER_M, D_MODEL), INNER_M ** -0.5),
        "ffn_w_up": nrm((DEPTH, D_MODEL, 2 * D_FF), D_MODEL ** -0.5),
        "ffn_w_down": nrm((DEPTH, D_FF, D_MODEL), D_FF ** -0.5),
        "ple_w_proj": nrm((DEPTH, PLE_DIM, D_MODEL), PLE_DIM ** -0.5),
        "ple_w_gate": nrm((DEPTH, D_MODEL, D_MODEL), D_MODEL ** -0.5),
        "ple_b_gate": nrm((DEPTH, D_MODEL), 0.01),
    }

def reference(x_prompt, x_sample, state_rglru_conv, state_rglru_h, state_mlstm_conv, state_mlstm_C,
              state_mlstm_n, state_mlstm_m, p_prompt, p_sample,
              norm_mix, norm_ffn, norm_final,
              rg_w_in, rg_conv_w, rg_conv_b, rg_w_r, rg_b_r, rg_w_i, rg_b_i, rg_lambda, rg_w_out,
              ml_w_in, ml_conv_w, ml_conv_b, ml_w_q, ml_w_k, ml_w_v, ml_w_gates, ml_b_gates, ml_norm, ml_w_out,
              ffn_w_up, ffn_w_down, ple_w_proj, ple_w_gate, ple_b_gate):
    dt = x_prompt.dtype
    Bp = x_prompt.shape[0]
    z_rg_conv = jnp.zeros((N_LAYERS_A, Bp, CONV_W - 1, D_RNN), dt)
    z_rg_h = jnp.zeros((N_LAYERS_A, Bp, D_RNN), dt)
    z_ml_conv = jnp.zeros((N_LAYERS_B, Bp, CONV_W - 1, INNER_M), dt)
    z_ml_C = jnp.zeros((N_LAYERS_B, Bp, N_HEADS_M, HEAD_DIM_M, HEAD_DIM_M), dt)
    z_ml_n = jnp.zeros((N_LAYERS_B, Bp, N_HEADS_M, HEAD_DIM_M), dt)
    z_ml_m = jnp.zeros((N_LAYERS_B, Bp, N_HEADS_M), dt)
    y_prompt, rg_conv_p, rg_h_p, ml_conv_p, ml_C_p, ml_n_p, ml_m_p = trunk(
        x_prompt, p_prompt, z_rg_conv, z_rg_h, z_ml_conv, z_ml_C, z_ml_n, z_ml_m,
        norm_mix, norm_ffn, norm_final,
        rg_w_in, rg_conv_w, rg_conv_b, rg_w_r, rg_b_r, rg_w_i, rg_b_i, rg_lambda, rg_w_out,
        ml_w_in, ml_conv_w, ml_conv_b, ml_w_q, ml_w_k, ml_w_v, ml_w_gates, ml_b_gates, ml_norm, ml_w_out,
        ffn_w_up, ffn_w_down, ple_w_proj, ple_w_gate, ple_b_gate)
    y_sample, rg_conv_s, rg_h_s, ml_conv_s, ml_C_s, ml_n_s, ml_m_s = trunk(
        x_sample, p_sample, state_rglru_conv, state_rglru_h, state_mlstm_conv, state_mlstm_C,
        state_mlstm_n, state_mlstm_m,
        norm_mix, norm_ffn, norm_final,
        rg_w_in, rg_conv_w, rg_conv_b, rg_w_r, rg_b_r, rg_w_i, rg_b_i, rg_lambda, rg_w_out,
        ml_w_in, ml_conv_w, ml_conv_b, ml_w_q, ml_w_k, ml_w_v, ml_w_gates, ml_b_gates, ml_norm, ml_w_out,
        ffn_w_up, ffn_w_down, ple_w_proj, ple_w_gate, ple_b_gate)
    return (y_prompt, y_sample,
            rg_conv_p, rg_h_p, ml_conv_p, ml_C_p, ml_n_p, ml_m_p,
            rg_conv_s, rg_h_s, ml_conv_s, ml_C_s, ml_n_s, ml_m_s)


_drawn_inputs = setup_inputs


def setup_inputs(seed=0):
    import zlib

    import numpy as np

    out = dict(_drawn_inputs(seed))
    spreads = {}
    factors = {'norm_mix': 3.552,
     'norm_ffn': 5.971,
     'norm_final': 32.756,
     'rg_b_r': 8.0,
     'rg_b_i': 8.0,
     'ml_conv_b': 15.436,
     'ml_norm': 64.0,
     'ple_b_gate': 64.0}
    for name, (base, spread) in spreads.items():
        noise = np.random.default_rng([zlib.crc32(name.encode()), seed]).standard_normal(out[name].shape)
        drawn = base * np.exp(spread * noise) if base else spread * noise
        out[name] = __import__('jax').numpy.asarray(drawn.astype(out[name].dtype))
    for name, factor in factors.items():
        out[name] = (out[name] * factor).astype(out[name].dtype)
    return out
```

```python
from contextlib import ExitStack, contextmanager

import concourse.bass as bass
from concourse import mybir

F32 = mybir.dt.float32
F32R = mybir.dt.float32r
ALU = mybir.AluOpType
ACT = mybir.ActivationFunctionType
ds = bass.ds

P = 128
D_MODEL, SEQ, DEC_B, DEC_S = 1024, 512, 8, 8
NS = DEC_B * DEC_S
T = SEQ + NS
H2 = T // 2
HP2 = SEQ - H2
D_RNN, INNER, D_FF, PLE = 1536, 2048, 2816, 256
CONV_W, TAIL = 4, 3
HEADS, HD = 4, 512
CX, CR, CI, CF = D_MODEL // P, D_RNN // P, INNER // P, D_FF // P
GROUPS = [(0, 8), (8, 8), (16, 6)]
EPS = 1e-6
SEG = TAIL + DEC_S
XB0 = TAIL + SEQ
WPAD = XB0 + DEC_B * SEG
WCONV = WPAD - TAIL
HSEG = 1 + DEC_S
WSCAN = SEQ + DEC_B * HSEG
NEG = -1.0e30
TOTAL = 484
RING = 4
FIRST = 1
UNITS = 2 + 2 * DEC_B
CSLOTS = 6
PPO = [0, 512, 896, 1152, 1280]
TT = [(i * P, min(P, T - i * P)) for i in range(-(-T // P))]


class Tally:
    looped = None

    def __init__(self, step=1):
        self.step, self.at, self.k, self.j, self.per = step, 0, 0, None, 0

    def adv(self, n=1):
        if self.j is None:
            assert Tally.looped is None, "a tally that the loop doesn't know"
            self.at += n
        else:
            self.k += n
        return self.now()

    def now(self):
        if self.j is None or not self.per:
            return (self.at + self.k) * self.step
        return self.j * (self.per * self.step) + (self.at + self.k) * self.step


def is_zero(count):
    return isinstance(count, int) and count == 0


@contextmanager
def loop(eng, n, per):
    with eng.Fori(0, n) as j:
        Tally.looped = per
        for t, p in per.items():
            t.j, t.per, t.k = j, p, 0
        yield j
        for t, p in per.items():
            assert t.k == p, (t.k, p)
            t.j, t.k, t.at = None, 0, t.at + p * n
        Tally.looped = None




def hybrid_trunk(nc, I, O):
    ctx = ExitStack()
    with ctx:
        def sb_in(stack, name, shape, dt=F32):
            return stack.enter_context(nc.sbuf_tensor(name, shape, dt))

        def sb(name, shape, dt=F32):
            return sb_in(ctx, name, shape, dt)

        credits = {}

        def sem(name, credit=0):
            s = ctx.enter_context(nc.semaphore(name))
            credits[id(s)] = credit
            return s

        waits_passed = {}

        def give_credit(eng, *sems):
            for s in sems:
                eng.nop().then_inc(s, credits[id(s)])

        def stand_alone(eng):
            if Tally.looped is not None:
                eng.sem_inc(waits_passed[id(eng)])

        X = sb("X", [P, CX, T])
        RAW = sb("RAW", [P, 4, 2, 256])
        WH = sb("WH", [P, 4, 2, 256], F32R)
        WL = sb("WL", [P, 4, 2, 256], F32R)
        RSTD = sb("RSTD", [P, T])
        ACC = sb("ACC", [P, 2, T])
        SQ = sb("SQ", [P, 2, T])
        IDN = sb("IDN", [P, P])
        ONES = sb("ONES", [P, P])
        V1 = sb("V1", [P, P])
        V2 = sb("V2", [P, P])
        SP8 = sb("SP8", [P, 2, CR])
        EPST = sb("EPST", [P, 1])
        RGSI = sb("RGSI", [P, CR, 32])
        RGSO = sb("RGSO", [P, CR, 36])
        MLSI = sb("MLSI", [P, CI, 24])
        MLSO = sb("MLSO", [P, CI, 27])
        NT = sb("NT", [P, DEC_B, HEADS, 4])
        NP = sb("NP", [P, HEADS, 4])
        WQKV = sb("WQKV", [P, 3, CI, 4])
        TRI = sb("TRI", [P, P])
        M64 = sb("M64", [NS, NS])
        BM8 = sb("BM8", [NS, DEC_B])
        BDM = sb("BDM", [P, 32])
        M0T = sb("M0T", [HEADS, DEC_B])
        BG = sb("BG", [HEADS, 2])
        MO = sb("MO", [HEADS, 1 + DEC_B])
        COLS = sb("COLS", [P, len(TT), 8])
        WM = sb("WM", [NS, HEADS, DEC_B])

        kb36 = [P, CX, T]
        with ExitStack() as p1:
            AH, AL = sb_in(p1, "AH", kb36, F32R), sb_in(p1, "AL", kb36, F32R)
            GH, GL = sb_in(p1, "GH", kb36, F32R), sb_in(p1, "GL", kb36, F32R)
            BH, BL = sb_in(p1, "BH", kb36, F32R), sb_in(p1, "BL", kb36, F32R)
            TG = sb_in(p1, "TG", [P, 2, T])
            TU = sb_in(p1, "TU", [P, 2, T])
            PTK = sb_in(p1, "PTK", [P, len(TT), PLE])
            YTK = sb_in(p1, "YTK", [P, 2, D_MODEL])
            SRO = sb_in(p1, "SRO", [36, D_RNN])
            SMO = sb_in(p1, "SMO", [27, INNER])
            NTO = sb_in(p1, "NTO", [P, 2, P])
        with ExitStack() as p0:
            sb_in(p0, "fill0", [P, 2, CX, T])
            YH, YL = sb_in(p0, "YH", [P, CR, T], F32R), sb_in(p0, "YL", [P, CR, T], F32R)
            XBP = sb_in(p0, "XBP", [P, 2, WPAD + 1])
            XCP = sb_in(p0, "XCP", [P, 2, WPAD + 1])
            XCH, XCL = sb_in(p0, "XCH", [P, 2, T], F32R), sb_in(p0, "XCL", [P, 2, T], F32R)
            GT = sb_in(p0, "GT", [P, 2, T])
            RT = sb_in(p0, "RT", [P, 2, T])
            IT = sb_in(p0, "IT", [P, 2, T])
            ST = sb_in(p0, "ST", [P, 2, T])
            AP_ = sb_in(p0, "APAD", [P, 2, WSCAN])
            UP = sb_in(p0, "UPAD", [P, 2, WSCAN])
            HPD = sb_in(p0, "HPAD", [P, 2, WSCAN])
            YF = sb_in(p0, "YF", [P, 2, T])
            DT = YF
        with ExitStack() as pl:
            sb_in(pl, "fill1", [P, 2, CX, T])
            XTK = sb_in(pl, "XTK", [P, len(TT), D_MODEL])
            VR = sb_in(pl, "VR", [P, 2, P])
            NR = sb_in(pl, "NR", [P, P])
            RSR = sb_in(pl, "RSR", [32, D_RNN])
            MSR = sb_in(pl, "MSR", [24, INNER])
        with ExitStack() as pj:
            fillj = sb_in(pj, "fillj", [P, 2, CX, T])
            PJ0 = sb_in(pj, "PJ0", [P, CX, T])
            PH0, PL0 = sb_in(pj, "PH0", [P, 2, T], F32R), sb_in(pj, "PL0", [P, 2, T], F32R)
        with ExitStack() as pk:
            PJ1 = sb_in(pk, "PJ1", [P, CX, T])
            PH1, PL1 = sb_in(pk, "PH1", [P, 2, T], F32R), sb_in(pk, "PL1", [P, 2, T], F32R)
        with ExitStack() as p2:
            XM = sb_in(p2, "XM", [P, CI, T])
            XC = sb_in(p2, "XC", [P, CI, T])
            with ExitStack() as p2a:
                sb_in(p2a, "fill2", [P, 2, CX, T])
                XMP = sb_in(p2a, "XMP", [P, 2, WPAD + 1])
                XCV = sb_in(p2a, "XCV", [P, 2, WPAD + 1])
                WGR = sb_in(p2a, "WGR", [P, 3 * CI, 4, 8])
                ET = sb_in(p2a, "ET", [P, 2 * CI, 36])
            with ExitStack() as p2r:
                rowt = lambda n: sb_in(p2r, n, [HEADS, T])
                LI, FF, AB, LF, BC, AS, A1, WS, T1, RM, NEGM = map(
                    rowt, ("LI", "FF", "AB", "LF", "BC", "AS", "A1", "WS", "T1", "RM", "NEGM"))
            HT = sb_in(p2, "HT", [P, 4, T])
            QT = sb_in(p2, "QT", [P, 4, T])
            VTK = sb_in(p2, "VTK", [P, len(TT), HD])
            KW = sb_in(p2, "KW", [P, 4, HD])
            KTK4 = sb_in(p2, "KTK4", [NS, HD])
            PP = sb_in(p2, "PP", [P, PPO[-1]])
            PSM = sb_in(p2, "PSM", [NS, NS])
            WBD = sb_in(p2, "WBD", [P, 3, 4, P])
            CS = sb_in(p2, "CS", [P, CSLOTS, 2, HD])
            KWM = sb_in(p2, "KWM", [NS, 2, HD])
            IWB = sb_in(p2, "IWB", [P, NS])
            ER = sb_in(p2, "ER", [HEADS, T])
            MR = sb_in(p2, "MR", [HEADS, T])
            IWR = sb_in(p2, "IWR", [HEADS, NS])
            SELH = sb_in(p2, "SELH", [HEADS, P])
        EM, RD, MB, FV = ACC[:, 0, :], ACC[:, 1, :], SQ[:, 0, :], SQ[:, 1, :]

        ps = ctx.enter_context(nc.psum_tensor("ps", [P, 8, 512], F32))
        psv = ps[:, :, :].rearrange("p (s m h) n -> p s m h n", s=2, m=2)

        raw_loaded = [sem(f"raw_loaded{i}") for i in range(4)]
        hi_ready = sem("hi_ready")
        lo_ready = sem("lo_ready", RING)
        slab_used = sem("slab_used", 2 * RING)
        psum_freed = [sem("psum0_freed"), sem("psum1_freed")]
        misc_done = sem("misc_done", FIRST)
        x_loaded = sem("x_loaded")
        rows_loaded = sem("rows_loaded")
        const_ready = sem("const_ready")
        act_step, dve_step, pool_step = sem("act_step"), sem("dve_step"), sem("pool_step")
        x_ready = sem("x_ready")
        xn_hi = sem("xn_hi")
        xn_ready = sem("xn_ready")
        sq_ready = sem("sq_ready")
        acc_ready = sem("acc_ready")
        acc_clear = sem("acc_clear")
        std_ready = sem("std_ready")
        lam_e = sem("lam_e")
        vecs_ready = sem("vecs_ready")
        pads_ready, conv_done, xc_hi, xc_ready = sem("pads_ready"), sem("conv_done", FIRST), sem("xc_hi", FIRST), sem("xc_ready")
        tails_out, h_out = sem("tails_out", FIRST), sem("h_out", FIRST)
        gelu_done, s_ready, a_ready = sem("gelu_done"), sem("s_ready"), sem("a_ready")
        v_in, v_ready, scan_done = sem("v_in"), sem("v_ready"), sem("scan_done", FIRST)
        y_ready, y_hi, y_lo = sem("y_ready"), sem("y_hi"), sem("y_lo", FIRST)
        gate_in, silu_done = sem("gate_in"), sem("silu_done")
        p_loaded, pt_hi, pt_ready, pj_ready = sem("p_loaded"), sem("pt_hi"), sem("pt_ready"), sem("pj_ready")
        sig_done = sem("sig_done")
        out_rows, stored, y_stored = sem("out_rows"), sem("stored"), [sem("y_stored0"), sem("y_stored1")]
        wqkv_loaded, wgr_loaded, et_ready = sem("wqkv_loaded"), sem("wgr_loaded"), sem("et_ready")
        xm_copied, xc_silu = sem("xm_copied"), sem("xc_silu")
        f_ready, ln_ready, t1_ready, er_ready, iws_in = sem("f_ready"), sem("ln_ready"), sem("t1_ready"), sem("er_ready"), sem("iws_in")
        rows_ready, cols_ready = sem("rows_ready"), sem("cols_ready")
        ht_ready, wbd_ready, sel_ready = sem("ht_ready"), sem("wbd_ready"), sem("sel_ready")
        nq_ready, e_ready, exp_done, masked = sem("nq_ready"), sem("e_ready"), sem("exp_done"), sem("masked")
        kt4_done, kwm_ready, rd_in, n_done = sem("kt4_done"), sem("kwm_ready"), sem("rd_in"), sem("n_done")
        unit_done, unit_freed = sem("unit_done", 2 * FIRST), sem("unit_freed", 2 * FIRST)
        c_loaded = [sem(f"c_loaded{i}") for i in range(CSLOTS)]
        c_stored = [sem(f"c_stored{i}", 16 * FIRST) for i in range(CSLOTS)]
        sqh_ready, fv_ready, sd_ready, h_done = sem("sqh_ready"), sem("fv_ready"), sem("sd_ready"), sem("h_done", FIRST)
        states_out = sem("states_out")

        G_MIX, G_FFN, C_RCW, C_RCB, C_BR, C_BI, C_LAM = 0, 16, 32, 80, 92, 104, 116
        C_MCW, C_MCB, C_MN, C_PB, C_NF = 0, 64, 80, 96, 112

        def pair4(t):
            return t.rearrange("p m (h n) -> p (m h) n", h=2)

        def pair5(t):
            return t.rearrange("p m (h n) -> p m h n", h=2)

        def psum4(s):
            return ps[:, 4 * s:4 * s + 4, 0:H2]

        RB = RSTD[:, :].rearrange("p (h n) -> p h n", h=2).unsqueeze(1).broadcast_to([P, 2, 2, H2])

        def padded(t, width, seg, lead, pre):
            return (t[:, :, pre:pre + SEQ],
                    t[:, :, pre + SEQ:pre + SEQ + DEC_B * seg].rearrange("p m (b t) -> p m b t", b=DEC_B)[:, :, :, lead:lead + DEC_S])

        def tight(t):
            return t[:, :, 0:SEQ], t[:, :, SEQ:T].rearrange("p m (b t) -> p m b t", b=DEC_B)

        block = ctx.enter_context(nc.Block())

        def w_slab(w, k, col):
            return w[k * 256:k * 256 + 256, col].rearrange("(k p) n -> p k n", p=P)

        @block.sync
        def _(sp):
            lo_t = Tally()
            phase = [0]
            waits_passed[id(sp)] = sem("sp_waits_passed")
            give_credit(sp, *c_stored)

            def slab(src):
                sp.wait_ge(lo_ready, lo_t.adv() - 4 + RING)
                stand_alone(sp)
                s = phase[0] % 4
                phase[0] += 1
                sp.dma_start(RAW[:, s], src).then_inc(raw_loaded[s], 16)

            for i, (t0, n) in enumerate(TT):
                src = I["x_prompt"][0, t0:t0 + n, :] if t0 < SEQ else I["x_sample"].rearrange("b t d -> (b t) d")
                sp.dma_start(XTK[0:n, i, :], src).then_inc(x_loaded, 16)
            rg_in, rg_wr, rg_wi, rg_out = I["rg_w_in"][0], I["rg_w_r"][0], I["rg_w_i"][0], I["rg_w_out"][0]
            with loop(sp, 3, {lo_t: 20}) as j:
                for jj in range(2):
                    b = 2 * j + jj
                    for k in range(4):
                        slab(w_slab(rg_in, k, ds(b * 256 + D_RNN, 256)))
                    for k in range(4):
                        slab(w_slab(rg_in, k, ds(b * 256, 256)))
                    for w in (rg_wr, rg_wi):
                        slab(w[ds(b, 1), :, :].rearrange("o (k p) n -> p (o k) n", p=P))
            with loop(sp, 2, {lo_t: 12}) as j:
                for m in range(2):
                    for k in range(6):
                        slab(w_slab(rg_out, k, ds(j * 512 + m * 256, 256)))

            def load_p(layer, dead_sem, dead):
                sp.wait_ge(dead_sem, dead)
                sp.dma_start(PTK[:, 0:4, :], I["p_prompt"][layer, 0].rearrange("(i p) d -> p i d", p=P)).then_inc(p_loaded, 16)
                sp.dma_start(PTK[0:NS, 4, :], I["p_sample"][layer].rearrange("b t d -> (b t) d")).then_inc(p_loaded, 16)

            def ffn(layer):
                up, down = I["ffn_w_up"][layer], I["ffn_w_down"][layer]
                for g0, gn in GROUPS:
                    with loop(sp, gn // 2, {lo_t: 8}) as j:
                        for off in (0, D_FF):
                            for k in range(4):
                                slab(w_slab(up, k, ds(j * 256 + off + g0 * P, 256)))
                    ks = gn // 2
                    with loop(sp, 1 if ks % 2 else 2, {lo_t: ks * (4 if ks % 2 else 2)}) as j:
                        for m in range(4 if ks % 2 else 2):
                            for k in range(ks):
                                slab(w_slab(down, g0 // 2 + k, ds(j * 512 + m * 256, 256)))

            def ple(layer):
                for m in range(4):
                    slab(w_slab(I["ple_w_proj"][layer], 0, slice(m * 256, m * 256 + 256)))
                with loop(sp, 2, {lo_t: 8}) as j:
                    for m in range(2):
                        for k in range(4):
                            slab(w_slab(I["ple_w_gate"][layer], k, ds(j * 512 + m * 256, 256)))

            load_p(0, y_lo, 6)
            ffn(0)
            ple(0)

            ml_in, ml_out = I["ml_w_in"][0], I["ml_w_out"][0]
            sp.wait_ge(misc_done, 9 + FIRST)
            with nc.allow_non_contiguous_dma(reason="small weights and gate vectors, once"):
                for i, name in enumerate(("ml_w_q", "ml_w_k", "ml_w_v")):
                    sp.dma_start(WQKV[:, i], I[name][0].rearrange("(c b) i o -> (b i) c o", c=CI)).then_inc(wqkv_loaded, 16)
                for i in range(4):
                    for m in range(3):
                        sp.dma_start(WGR[i:P:4, m * CI:m * CI + CI],
                                     I["ml_w_gates"][0, m * INNER:m * INNER + INNER].rearrange("(c b o) g -> b c (o g)", c=CI, o=4)
                                     .rearrange("b c (o g) -> b c o g", o=4)).then_inc(wgr_loaded, 16)
                sp.dma_start(M0T[:, :], I["state_mlstm_m"][0].rearrange("b h -> h b")).then_inc(wgr_loaded, 16)
                sp.dma_start(BG[:, :], I["ml_b_gates"][0].rearrange("(g h) -> h g", g=2)).then_inc(wgr_loaded, 16)
            with loop(sp, 4, {lo_t: 8}) as j:
                for m in range(2):
                    for k in range(4):
                        slab(w_slab(ml_in, k, ds(j * 512 + m * 256, 256)))

            def o_job(m):
                for k in range(4):
                    slab(w_slab(ml_in, k, slice(INNER + m * 256, INNER + m * 256 + 256)))

            o_job(0)
            freed = Tally()
            stored_t = [Tally(16) for _ in range(CSLOTS)]
            per_slot = UNITS // CSLOTS
            sp.wait_ge(rows_ready, 1)
            with loop(sp, HEADS, {freed: UNITS, **{t: per_slot for t in stored_t}}) as h:
                ahead = CSLOTS - 2
                for v in range(UNITS + ahead):
                    if v < UNITS:
                        slot = v % CSLOTS
                        sp.wait_ge(c_stored[slot], stored_t[slot].adv() - 16 + 16 * FIRST)
                        stand_alone(sp)
                        if v >= 2:
                            b, half = (v - 2) // 2, v % 2
                            sp.dma_start(CS[:, slot], I["state_mlstm_C"][0, b, ds(h, 1), half * 256:half * 256 + 256, :]
                                         .rearrange("o (k p) v -> p (o k) v", p=P)).then_inc(c_loaded[slot], 16)
                        else:
                            sp.nop().then_inc(c_loaded[slot], 16)
                    if v >= ahead:
                        w = v - ahead
                        slot, half = w % CSLOTS, w % 2
                        sp.wait_ge(unit_freed, freed.adv() + 2 * FIRST)
                        stand_alone(sp)
                        dst = (O["ml_C_p"][0, 0] if w < 2 else O["ml_C_s"][0, (w - 2) // 2])[ds(h, 1), half * 256:half * 256 + 256, :]
                        sp.dma_start(dst.rearrange("o (k p) v -> p (o k) v", p=P), CS[:, slot]).then_inc(c_stored[slot], 16)
            load_p(1, h_done, HEADS)
            for m in range(1, 4):
                o_job(m)
            for g in range(2):
                if g:
                    for m in range(4, 8):
                        o_job(m)
                with loop(sp, 2, {lo_t: 8}) as j:
                    for m in range(2):
                        for k in range(4):
                            slab(w_slab(ml_out, 4 * g + k, ds(j * 512 + m * 256, 256)))
            ffn(1)
            ple(1)
            sp.wait_ge(states_out, 4)
            for dst, src in ((O["rg_conv_s"].rearrange("l b t d -> (l b t) d"), SRO[0:24, :]),
                             (O["rg_h_s"].rearrange("l b d -> (l b) d"), SRO[24:32, :]),
                             (O["rg_conv_p"].rearrange("l b t d -> (l b t) d"), SRO[32:35, :]),
                             (O["rg_h_p"].rearrange("l b d -> (l b) d"), SRO[35:36, :]),
                             (O["ml_conv_s"].rearrange("l b t d -> (l b t) d"), SMO[0:24, :]),
                             (O["ml_conv_p"].rearrange("l b t d -> (l b t) d"), SMO[24:27, :]),
                             (O["ml_n_s"].rearrange("l b h (k p) -> (l b h k) p", p=P), NTO[:, 0, :]),
                             (O["ml_n_p"].rearrange("l b h (k p) -> (l b h k) p", p=P), NTO[0:16, 1, :])):
                sp.dma_start(dst, src).then_inc(stored, 16)
            with nc.allow_non_contiguous_dma(reason="m, 36 numbers"):
                sp.dma_start(O["ml_m_p"].rearrange("l b h -> h (l b)"), MO[:, 0:1]).then_inc(stored, 16)
                sp.dma_start(O["ml_m_s"].rearrange("l b h -> h (l b)"), MO[:, 1:1 + DEC_B]).then_inc(stored, 16)
            for i, (t0, n) in enumerate(TT):
                sp.wait_ge(out_rows, i + 1)
                dst = O["y_prompt"][0, t0:t0 + n, :] if t0 < SEQ else O["y_sample"].rearrange("b t d -> (b t) d")
                sp.dma_start(dst, YTK[0:n, i % 2, :]).then_inc(y_stored[i % 2], 16)
            sp.wait_ge(stored, 16 * 10)
            sp.wait_ge(y_stored[0], 16 * 3)
            sp.wait_ge(y_stored[1], 16 * 2)
            for slot in range(CSLOTS):
                sp.wait_ge(c_stored[slot], 16 * HEADS * per_slot + 16 * FIRST)

        @block.gpsimd
        def _(pool):
            slabs, step, conv_t, sq_t, misc = Tally(), Tally(), Tally(), Tally(), Tally()
            uses = [Tally(), Tally()]
            scans, ys = Tally(), Tally()
            phase = [0]

            def split_lo():
                n = slabs.adv()
                if isinstance(n, int) and n > TOTAL:
                    return
                pool.wait_ge(hi_ready, n)
                s = phase[0] % 4
                phase[0] += 1
                pool.tensor_tensor(WL[:, s], RAW[:, s], WH[:, s].bitcast(F32), ALU.subtract).then_inc(lo_ready, 1)

            def clear_acc():
                pool.memset(ACC[:, :, :], 0.0).then_inc(acc_clear, 1)

            def add_sq():
                pool.wait_ge(sq_ready, sq_t.adv())
                pool.tensor_tensor(ACC[:, :, :], ACC[:, :, :], SQ[:, :, :], ALU.add).then_inc(acc_ready, 1)

            give_credit(pool, lo_ready, tails_out, h_out, y_lo)
            pool.memset(IDN[:, :], 0.0).then_inc(pool_step, 1)
            pool.wait_ge(pool_step, step.adv())
            pool.affine_select(out=IDN[:, :], in_=IDN[:, :], compare_op=ALU.not_equal, fill=1.0, base=0,
                               pattern=[[-1, P]], channel_multiplier=1)
            pool.memset(ONES[:, :], 1.0)
            pool.memset(XBP[:, :, 0:TAIL], 0.0)
            pool.memset(AP_[:, :, SEQ:WSCAN], 0.0)
            for t in (TRI, M64, BM8, BDM):
                pool.memset(t[:, :], 1.0)
            pool.memset(EPST[:, :], EPS).then_inc(const_ready, 1)
            pool.wait_ge(const_ready, 1)

            def keep(t, pattern, base, mult):
                pool.affine_select(out=t, in_=t, compare_op=ALU.is_ge, fill=0.0, base=base, pattern=pattern,
                                   channel_multiplier=mult).then_inc(pool_step, 1)
                pool.wait_ge(pool_step, step.adv())

            keep(TRI[:, :], [[1, P]], 0, -1)
            keep(M64[:, :], [[1, NS]], 0, -1)
            keep(M64[:, :].rearrange("p (b t) -> p b t", b=DEC_B), [[-DEC_S, DEC_B], [0, DEC_S]], 0, 1)
            keep(BM8[:, :], [[-DEC_S, DEC_B]], 0, 1)
            keep(BM8[:, :], [[DEC_S, DEC_B]], DEC_S - 1, -1)
            keep(BDM[:, :], [[-4, 32]], 0, 1)
            keep(BDM[:, :], [[4, 32]], 3, -1)
            clear_acc()
            for k in range(4):
                split_lo()
            pool.wait_ge(acc_clear, 1)
            for m in range(4):
                add_sq()
            pool.wait_ge(vecs_ready, 1)
            with loop(pool, 3, {slabs: 20, uses[0]: 4, uses[1]: 4, conv_t: 2, scans: 2, ys: 2}) as j:
                for jj in range(2):
                    c0 = 4 * j + 2 * jj
                    u0 = uses[0].adv()
                    pool.wait_ge(conv_done, conv_t.adv() - 1 + FIRST)
                    pool.tensor_copy(
                        XBP[:, :, XB0:XB0 + DEC_B * SEG].rearrange("p m (b t) -> p m b t", b=DEC_B)[:, :, :, 0:TAIL],
                        RGSI[:, ds(c0, 2), 0:24].rearrange("p m (b t) -> p m b t", b=DEC_B)).then_inc(pads_ready, 1)
                    for k in range(8):
                        split_lo()
                    pool.wait_ge(conv_done, conv_t.now() + FIRST)
                    pool.tensor_copy(
                        RGSO[:, ds(c0, 2), 0:24].rearrange("p m (b t) -> p m b t", b=DEC_B),
                        XBP[:, :, XB0:XB0 + DEC_B * SEG].rearrange("p m (b t) -> p m b t", b=DEC_B)[:, :, :, DEC_S:SEG])
                    pool.tensor_copy(RGSO[:, ds(c0, 2), 32:35], XBP[:, :, XB0 - TAIL:XB0]).then_inc(tails_out, 1)
                    for k in range(2):
                        split_lo()
                    uses[0].adv()
                    uses[1].adv(2)
                    pool.wait_ge(scan_done, scans.adv() + FIRST)
                    pool.tensor_copy(
                        RGSO[:, ds(c0, 2), 24:32],
                        HPD[:, :, SEQ:WSCAN].rearrange("p m (b t) -> p m b t", b=DEC_B)[:, :, :, DEC_S])
                    pool.tensor_copy(RGSO[:, ds(c0, 2), 35:36], HPD[:, :, SEQ - 1:SEQ]).then_inc(h_out, 1)
                    pool.wait_ge(y_hi, ys.adv())
                    pool.tensor_tensor(YL[:, ds(c0, 2), :], YF[:, :, :], YH[:, ds(c0, 2), :].bitcast(F32),
                                       ALU.subtract).then_inc(y_lo, 1)

            def next_norm():
                pool.wait_ge(misc_done, misc.adv() + FIRST)
                clear_acc()

            misc.adv(6)
            next_norm()
            pool.wait_ge(acc_clear, 2)
            with loop(pool, 2, {slabs: 12, sq_t: 2}) as j:
                for m in range(2):
                    for k in range(6):
                        split_lo()
                    add_sq()

            def ffn1():
                ffn(AH, AL)

            def g_lo(j, dst_h, dst_l, src):
                pool.tensor_tensor(dst_l[:, ds(j * 2, 2), :], src[:, :, :], dst_h[:, ds(j * 2, 2), :].bitcast(F32),
                                   ALU.subtract).then_inc(y_lo, 1)

            def ffn(gh=GH, gl=GL):
                for g, (g0, gn) in enumerate(GROUPS):
                    with loop(pool, gn // 2, {slabs: 8, ys: 1}) as j:
                        for k in range(8):
                            split_lo()
                        pool.wait_ge(y_hi, ys.adv())
                        g_lo(j, gh, gl, TU)
                    ks = gn // 2
                    n = 4 if ks % 2 else 2
                    with loop(pool, 4 // n, {slabs: ks * n}) as j:
                        for k in range(ks * n):
                            split_lo()

            def ple(clear, last):
                for k in range(4):
                    split_lo()
                misc.adv()
                next_norm()
                pool.wait_ge(acc_clear, clear)
                for j in (range(2) if last else (None,)):
                    if last:
                        body(j)
                    else:
                        with loop(pool, 2, {slabs: 8, sq_t: 2}) as j:
                            body(j)

            def body(j):
                for m in range(2):
                    for k in range(4):
                        split_lo()
                    add_sq()

            ffn()
            ple(3, False)
            pool.memset(XMP[:, :, 0:TAIL], 0.0)

            def link(ins):
                ins.then_inc(pool_step, 1)
                pool.wait_ge(pool_step, step.adv())

            def ml_in():
                with loop(pool, 2, {slabs: 8, conv_t: 2}) as j:
                    for m in range(2):
                        c0 = 4 * j + 2 * m + ml_c[0]
                        pool.wait_ge(conv_done, conv_t.adv() - 1 + FIRST)
                        pool.tensor_copy(
                            XMP[:, :, XB0:XB0 + DEC_B * SEG].rearrange("p m (b t) -> p m b t", b=DEC_B)[:, :, :, 0:TAIL],
                            MLSI[:, ds(c0, 2), :].rearrange("p m (b t) -> p m b t", b=DEC_B)).then_inc(pads_ready, 1)
                        for k in range(4):
                            split_lo()
                        pool.wait_ge(conv_done, conv_t.now() + FIRST)
                        pool.tensor_copy(
                            MLSO[:, ds(c0, 2), 0:24].rearrange("p m (b t) -> p m b t", b=DEC_B),
                            XMP[:, :, XB0:XB0 + DEC_B * SEG].rearrange("p m (b t) -> p m b t", b=DEC_B)[:, :, :, DEC_S:SEG])
                        pool.tensor_copy(MLSO[:, ds(c0, 2), 24:27], XMP[:, :, XB0 - TAIL:XB0]).then_inc(tails_out, 1)
                ml_c[0] += 8

            ml_c = [0]
            ml_in()
            pool.wait_ge(wqkv_loaded, 48)
            pool.wait_ge(wgr_loaded, 16 * 14)
            link(pool.tensor_scalar(WQKV[:, 1], WQKV[:, 1], float(HD) ** -0.5, None, ALU.mult))
            link(pool.memset(ET[:, :, :], 0.0))
            for i in range(3):
                g = WGR[:, i * CI:i * CI + CI]
                link(pool.tensor_tensor(g, g, WQKV[:, i].unsqueeze(3).broadcast_to([P, CI, 4, 8]), ALU.mult))
            link(pool.tensor_tensor(WGR[:, :, 0:2, :], WGR[:, :, 0:2, :], WGR[:, :, 2:4, :], ALU.add))
            link(pool.tensor_tensor(WGR[:, :, 0, :], WGR[:, :, 0, :], WGR[:, :, 1, :], ALU.add))
            for g in range(2):
                e = ET[:, :, 32 * g:32 * g + 4]
                w = WGR[:, :, 0, 4 * g:4 * g + 4]
                pool.tensor_tensor(e[:, 0:CI], w[:, 0:CI], w[:, CI:2 * CI], ALU.add)
                pool.tensor_copy(e[:, CI:2 * CI], w[:, 2 * CI:3 * CI]).then_inc(et_ready, 1)
            ml_in()
            heads, misc_h = Tally(), Tally()
            misc_h.adv(12)
            with loop(pool, HEADS, {heads: 1, misc_h: 13}) as h:
                n = heads.adv()
                pool.wait_ge(misc_done, misc_h.now() + FIRST)
                for i in range(3):
                    ins = pool.tensor_tensor(
                        WBD[:, i].rearrange("p c (b o) -> p c b o", o=4),
                        WQKV[:, i, ds(4 * h, 4), :].unsqueeze(2).broadcast_to([P, 4, 32, 4]),
                        BDM[:, :].unsqueeze(1).unsqueeze(3).broadcast_to([P, 4, 32, 4]), ALU.mult)
                ins.then_inc(wbd_ready, 1)
                pool.wait_ge(exp_done, n)
                for sbk in range(4):
                    pool.tensor_tensor(PP[:, PPO[sbk]:PPO[sbk] + P], PP[:, PPO[sbk]:PPO[sbk] + P], TRI[:, :], ALU.mult)
                pool.tensor_tensor(PSM[:, :], PSM[:, :], M64[:, :], ALU.mult).then_inc(masked, 1)
                misc_h.adv(13)

            def small_lo(j, dst_h, dst_l):
                pool.wait_ge(y_hi, ys.adv())
                pool.tensor_tensor(dst_l[:, ds(j, 2), :], TU[:, :, :], dst_h[:, ds(j, 2), :].bitcast(F32),
                                   ALU.subtract).then_inc(y_lo, 1)

            misc.adv(2 + 13 * HEADS + STATE_JOBS)
            next_norm_at = [None]
            for g in range(2):
                with loop(pool, 2, {slabs: 8, ys: 2}) as j:
                    for m in range(2):
                        for k in range(4):
                            split_lo()
                        small_lo(4 * j + 2 * m, AH, AL)
                if g:
                    next_norm()
                    pool.wait_ge(acc_clear, 4)
                with loop(pool, 2, {slabs: 8, **({sq_t: 2} if g else {})}) as j:
                    for m in range(2):
                        for k in range(4):
                            split_lo()
                        if g:
                            add_sq()
            ffn1()
            ple(5, True)

        @block.scalar
        def _(act):
            slabs, step, sq_t, misc, jobs = Tally(), Tally(), Tally(), Tally(), Tally()
            raw_t = [Tally(16) for _ in range(4)]
            uses = [Tally(), Tally()]
            xr, blk, conv_t = Tally(), Tally(), Tally()
            phase = [0]

            def link(ins):
                ins.then_inc(act_step, 1)
                act.wait_ge(act_step, step.adv())

            def split_hi():
                n = slabs.adv()
                if isinstance(n, int) and n > TOTAL:
                    return
                s = phase[0] % 4
                phase[0] += 1
                act.wait_ge(raw_loaded[s], raw_t[s].adv())
                stand_alone(act)
                act.wait_ge(slab_used, n - 4 + 2 * RING)
                stand_alone(act)
                act.activation(WH[:, s], RAW[:, s], ACT.Copy).then_inc(hi_ready, 1)

            def split_per(n):
                return {slabs: n, **{t: n // 4 for t in raw_t}}

            def prep(c0, gain, hi, norm=True):
                act.wait_ge(x_ready, xr.adv())
                stand_alone(act)
                for m in range(2):
                    if gain is None:
                        ins = act.activation(hi[:, ds(c0 + m, 1), :], X[:, ds(c0 + m, 1), :], ACT.Copy)
                    else:
                        ins = act.activation(hi[:, ds(c0 + m, 1), :], X[:, ds(c0 + m, 1), :], ACT.Copy,
                                             scale=V1[:, ds(gain + c0 + m, 1)])
                ins.then_inc(xn_hi, 1)
                if norm:
                    before = sq_t.adv() - 1
                    if not is_zero(before):
                        act.wait_ge(acc_ready, before)
                        stand_alone(act)
                    act.activation(SQ[:, :, :], X[:, ds(c0, 2), :], ACT.Square).then_inc(sq_ready, 1)

            def std(s):
                uses[s].adv()
                act.wait_ge(misc_done, misc.adv() + FIRST)
                act.activation(RSTD[:, :].rearrange("p (h n) -> p h n", h=2), ps[:, 4 * s:4 * s + 2, 0:H2], ACT.Sqrt,
                               bias=EPST[:, :], scale=1.0 / D_MODEL).then_inc(psum_freed[s], 1)

            def rows(t, i):
                t0, n = TT[i]
                return t[0:n, i, :]

            waits_passed[id(act)] = sem("act_waits_passed")
            give_credit(act, xc_hi)
            r = lambda name, pat, **k: I[name].rearrange(pat, **k)
            vec_rows = [
                (VR[0:16, 0, :], r("norm_mix", "l (c p) -> (l c) p", p=P)),
                (VR[16:32, 0, :], r("norm_ffn", "l (c p) -> (l c) p", p=P)),
                (VR[32:80, 0, :], r("rg_conv_w", "l w (c p) -> (l w c) p", p=P)),
                (VR[80:92, 0, :], r("rg_conv_b", "l (c p) -> (l c) p", p=P)),
                (VR[92:104, 0, :], r("rg_b_r", "l (c p) -> (l c) p", p=P)),
                (VR[104:116, 0, :], r("rg_b_i", "l (c p) -> (l c) p", p=P)),
                (VR[116:128, 0, :], r("rg_lambda", "l (c p) -> (l c) p", p=P)),
                (VR[0:64, 1, :], r("ml_conv_w", "l w (c p) -> (l w c) p", p=P)),
                (VR[64:80, 1, :], r("ml_conv_b", "l (c p) -> (l c) p", p=P)),
                (VR[80:96, 1, :], r("ml_norm", "l (c p) -> (l c) p", p=P)),
                (VR[96:112, 1, :], r("ple_b_gate", "l (c p) -> (l c) p", p=P)),
                (VR[112:120, 1, :], r("norm_final", "(c p) -> c p", p=P)),
                (NR[:, :], r("state_mlstm_n", "l b h (k p) -> (l b h k) p", p=P)),
                (RSR[0:24, :], r("state_rglru_conv", "l b t d -> (l b t) d")),
                (RSR[24:32, :], r("state_rglru_h", "l b d -> (l b) d")),
                (MSR[:, :], r("state_mlstm_conv", "l b t d -> (l b t) d")),
            ]
            for dst, src in vec_rows:
                act.dma_start(dst, src).then_inc(rows_loaded, 16)
            assert 16 * len(vec_rows) == ROWS_LOADED
            for k in range(4):
                split_hi()
            act.wait_ge(vecs_ready, 1)
            link(act.activation(SP8[:, 0, :], V1[:, C_LAM:C_LAM + CR], ACT.Abs))
            act.activation(SP8[:, 1, :], SP8[:, 0, :], ACT.Exp, scale=-1.0).then_inc(lam_e, 1)
            act.wait_ge(acc_clear, 1)
            misc.adv(6)
            uses[0].adv(3)
            uses[1].adv(3)
            for m in range(4):
                prep(2 * m, G_MIX, AH)
            std(1)
            with loop(act, 3, {**split_per(20), jobs: 20, uses[0]: 4, uses[1]: 4, blk: 2}) as j:
                for jj in range(2):
                    c0 = 4 * j + 2 * jj
                    for k in range(6):
                        split_hi()
                    jobs.adv(8)
                    b = blk.adv()
                    act.wait_ge(conv_done, b + FIRST)
                    stand_alone(act)
                    act.wait_ge(slab_used, jobs.now() - 8 + 2 * RING)
                    stand_alone(act)
                    (src_p, src_s), (dst_p, dst_s) = padded(XCP, WPAD, SEG, 0, 0), tight(XCH)
                    src_s = XCP[:, :, XB0:XB0 + DEC_B * SEG].rearrange("p m (b t) -> p m b t", b=DEC_B)[:, :, :, 0:DEC_S]
                    act.activation(dst_p, XCP[:, :, 0:SEQ], ACT.Copy)
                    act.activation(dst_s, src_s, ACT.Copy).then_inc(xc_hi, 1)
                    split_hi()
                    split_hi()
                    uses[0].adv()
                    act.wait_ge(psum_freed[1], uses[1].adv())
                    stand_alone(act)
                    act.activation(GT[:, :, :], GT[:, :, :], ACT.Gelu_apprx_tanh).then_inc(gelu_done, 1)
                    split_hi()
                    act.wait_ge(slab_used, jobs.adv() + 2 * RING)
                    stand_alone(act)
                    for m in range(2):
                        ins = act.activation(RT[:, m].rearrange("p (h n) -> p h n", h=2), psv[:, 0, m, :, 0:H2],
                                             ACT.Sigmoid, bias=V1[:, ds(C_BR + m + c0, 1)])
                    ins.then_inc(psum_freed[0], 1)
                    split_hi()
                    act.wait_ge(slab_used, jobs.adv() + 2 * RING)
                    stand_alone(act)
                    act.wait_ge(scan_done, b - 1 + FIRST)
                    stand_alone(act)
                    for m in range(2):
                        ins = act.activation(IT[:, m].rearrange("p (h n) -> p h n", h=2), psv[:, 1, m, :, 0:H2],
                                             ACT.Sigmoid, bias=V1[:, ds(C_BI + m + c0, 1)])
                    ins.then_inc(psum_freed[1], 1)
                    act.wait_ge(psum_freed[0], uses[0].adv())
                    stand_alone(act)
                    for m in range(2):
                        ins = act.activation(ST[:, m, :], RT[:, m, :], ACT.Tanh, scale=SP8[:, 0, ds(c0 + m, 1)])
                    ins.then_inc(s_ready, 1)
                    for m in range(2):
                        act.activation(AP_[:, m, 0:SEQ], RT[:, m, 0:SEQ], ACT.Exp, scale=SP8[:, 1, ds(c0 + m, 1)])
                        ins = act.activation(
                            AP_[:, m, SEQ:WSCAN].rearrange("p (b t) -> p b t", b=DEC_B)[:, :, 1:HSEG],
                            RT[:, m, SEQ:T].rearrange("p (b t) -> p b t", b=DEC_B), ACT.Exp,
                            scale=SP8[:, 1, ds(c0 + m, 1)])
                    ins.then_inc(a_ready, 1)
                    act.wait_ge(v_in, b)
                    stand_alone(act)
                    act.activation(ST[:, :, :], ST[:, :, :], ACT.Sqrt, scale=2.0).then_inc(v_ready, 1)
                    uses[1].adv()
                    act.wait_ge(y_ready, b)
                    stand_alone(act)
                    act.activation(YH[:, ds(c0, 2), :], YF[:, :, :], ACT.Copy).then_inc(y_hi, 1)
            act.wait_ge(acc_clear, 2)
            with loop(act, 2, {**split_per(12), jobs: 12, uses[0]: 1, uses[1]: 1, xr: 2, sq_t: 2}) as j:
                for m in range(2):
                    for k in range(6):
                        split_hi()
                    jobs.adv(6)
                    uses[m].adv()
                    prep(4 * j + 2 * m, G_FFN, AH)
            std(1)

            def ffn(last_out, gh):
                for g, (g0, gn) in enumerate(GROUPS):
                    with loop(act, gn // 2, {**split_per(8), jobs: 8, uses[0]: 1, uses[1]: 1, blk: 1}) as j:
                        for k in range(4):
                            split_hi()
                        b = blk.adv()
                        act.wait_ge(psum_freed[0], uses[0].adv())
                        stand_alone(act)
                        act.activation(TG[:, :, :], TG[:, :, :], ACT.Silu).then_inc(silu_done, 1)
                        for k in range(4):
                            split_hi()
                        jobs.adv(8)
                        uses[1].adv()
                        act.wait_ge(y_ready, b)
                        stand_alone(act)
                        act.activation(gh[:, ds(2 * j, 2), :], TU[:, :, :], ACT.Copy).then_inc(y_hi, 1)
                    ks = gn // 2
                    n = 4 if ks % 2 else 2
                    lastg = g == len(GROUPS) - 1
                    with loop(act, 4 // n, {**split_per(ks * n), jobs: ks * n, uses[0]: n // 2, uses[1]: n // 2,
                                            xr: n if lastg else 0}) as j:
                        for m in range(n):
                            for k in range(ks):
                                split_hi()
                            jobs.adv(ks)
                            uses[m % 2].adv()
                            if lastg:
                                prep(4 * j + 2 * m, None, last_out, norm=False)

            def ple(layer, PH, PJ, gain, dst, acc0):
                act.wait_ge(misc_done, misc.adv() + FIRST)
                act.activation(PH[:, :, 0:SEQ], ps[:, 0:4:2, 0:SEQ], ACT.Copy)
                act.activation(PH[:, :, SEQ:T], ps[:, 1:4:2, 0:NS], ACT.Copy).then_inc(pt_hi, 1)
                uses[0].adv()
                for m in range(4):
                    split_hi()
                    s = (m + 1) % 2
                    uses[s].adv()
                    act.wait_ge(slab_used, jobs.adv() + 2 * RING)
                    act.activation(pair4(PJ[:, 2 * m:2 * m + 2, :]), psum4(s), ACT.Copy).then_inc(psum_freed[s], 1)
                act.wait_ge(acc_clear, acc0)

                def body(j):
                    for m in range(2):
                        for k in range(4):
                            split_hi()
                        act.wait_ge(slab_used, jobs.adv(4) + 2 * RING)
                        stand_alone(act)
                        s = (m + 1) % 2
                        uses[s].adv()
                        act.wait_ge(x_ready, xr.now())
                        stand_alone(act)
                        for c in range(2):
                            ins = act.activation(TG[:, c].rearrange("p (h n) -> p h n", h=2), psv[:, s, c, :, 0:H2],
                                                 ACT.Sigmoid, bias=V2[:, ds(C_PB + 8 * layer + 2 * m + c + 4 * j, 1)])
                        ins.then_inc(psum_freed[s], 1)
                        if dst is None:
                            act.wait_ge(x_ready, xr.adv())
                            act.wait_ge(acc_ready, sq_t.adv() - 1)
                            act.activation(SQ[:, :, :], X[:, ds(4 * j + 2 * m, 2), :], ACT.Square).then_inc(sq_ready, 1)
                        else:
                            prep(4 * j + 2 * m, gain, dst)

                if layer:
                    for j in range(2):
                        body(j)
                else:
                    with loop(act, 2, {**split_per(8), jobs: 8, uses[0]: 1, uses[1]: 1, xr: 2, sq_t: 2}) as j:
                        body(j)
                std(1)

            ffn(AH, GH)
            ple(0, PH0, PJ0, G_MIX + 8, BH, 3)

            with loop(act, 4, {**split_per(8), jobs: 8, uses[0]: 1, uses[1]: 1, conv_t: 2}) as j:
                for m in range(2):
                    c0 = 4 * j + 2 * m
                    for k in range(4):
                        split_hi()
                    jobs.adv(4)
                    act.wait_ge(psum_freed[m], uses[m].adv())
                    stand_alone(act)
                    mp, ms = tight(XM[:, ds(c0, 2), :])
                    act.activation(mp, XMP[:, :, TAIL:XB0], ACT.Copy)
                    act.activation(ms, XMP[:, :, XB0:XB0 + DEC_B * SEG].rearrange("p m (b t) -> p m b t", b=DEC_B)[:, :, :, TAIL:SEG],
                                   ACT.Copy).then_inc(xm_copied, 1)
                    act.wait_ge(conv_done, 6 + conv_t.adv() + FIRST)
                    stand_alone(act)
                    cp, cs = tight(XC[:, ds(c0, 2), :])
                    act.activation(cp, XCV[:, :, 0:SEQ], ACT.Silu)
                    act.activation(cs, XCV[:, :, XB0:XB0 + DEC_B * SEG].rearrange("p m (b t) -> p m b t", b=DEC_B)[:, :, :, 0:DEC_S],
                                   ACT.Silu).then_inc(xc_silu, 1)
            misc.adv()
            uses[0].adv()
            act.wait_ge(f_ready, 1)
            link(act.activation(AB[:, :], FF[:, :], ACT.Abs))
            link(act.activation(AB[:, :], AB[:, :], ACT.Exp, scale=-1.0))
            act.activation(AB[:, :], AB[:, :], ACT.Ln, bias=1.0).then_inc(ln_ready, 1)
            act.wait_ge(t1_ready, 1)
            act.activation(ER[:, :], T1[:, :], ACT.Exp, scale=-1.0)
            act.activation(IWR[:, :], IWR[:, :], ACT.Exp)
            act.activation(WS[:, :], WS[:, :], ACT.Exp).then_inc(rows_ready, 1)
            misc.adv()
            uses[1].adv()
            heads, units = Tally(), Tally()
            with loop(act, HEADS, {misc: 13, uses[0]: 6, uses[1]: 6, heads: 1, units: UNITS}) as h:
                n = heads.adv()
                act.wait_ge(misc_done, misc.now() + FIRST)
                stand_alone(act)
                act.activation(HT[:, :, :], XM[:, ds(4 * h, 4), :], ACT.Copy).then_inc(ht_ready, 1)
                act.wait_ge(misc_done, misc.adv() + FIRST)
                stand_alone(act)
                act.activation(VTK[:, 0:4, :], ps[:, 0:4, :], ACT.Copy).then_inc(psum_freed[0], 1)
                uses[0].adv()
                act.wait_ge(misc_done, misc.adv() + FIRST)
                stand_alone(act)
                act.wait_ge(h_done, n - 1 + FIRST)
                stand_alone(act)
                act.activation(VTK[0:NS, 4, :], ps[0:NS, 4, :], ACT.Copy)
                act.activation(MB[:, 0:SEQ], ps[:, 5, :], ACT.Copy)
                act.activation(EM[:, 0:SEQ], ps[:, 6, :], ACT.Copy)
                act.activation(MB[:, SEQ:T], ps[:, 7, 0:NS], ACT.Copy)
                act.activation(EM[:, SEQ:T], ps[:, 7, NS:2 * NS], ACT.Copy)
                act.activation(IWB[:, :], ps[:, 7, 2 * NS:3 * NS], ACT.Copy).then_inc(psum_freed[1], 1)
                uses[1].adv()
                for t in (QT, HT):
                    for s in range(2):
                        act.wait_ge(misc_done, misc.adv() + FIRST)
                        stand_alone(act)
                        act.activation(pair4(t[:, 2 * s:2 * s + 2, :]), psum4(s), ACT.Copy).then_inc(psum_freed[s], 1)
                        uses[s].adv()
                act.wait_ge(e_ready, n)
                stand_alone(act)
                act.activation(PP[:, :], PP[:, :], ACT.Exp, scale=-1.0)
                act.activation(PSM[:, :], PSM[:, :], ACT.Exp, scale=-1.0).then_inc(exp_done, 1)
                act.wait_ge(misc_done, misc.adv() + FIRST)
                stand_alone(act)
                for i in range(4):
                    ins = act.activation(KW[:, i, :], ps[:, i, :], ACT.Copy, scale=COLS[:, i, ds(h + 4, 1)])
                ins.then_inc(psum_freed[0], 1)
                uses[0].adv()
                act.wait_ge(misc_done, misc.adv() + FIRST)
                stand_alone(act)
                act.activation(KTK4[:, :], ps[0:NS, 4, :], ACT.Copy).then_inc(kt4_done, 1)
                uses[1].adv()
                act.wait_ge(kt4_done, n)
                stand_alone(act)

                def kwm(b):
                    if b >= 2:
                        act.wait_ge(unit_done, units.now() + 2 * b + 2 * FIRST)
                        stand_alone(act)
                    act.activation(KWM[:, b % 2, :], KTK4[:, :], ACT.Copy, scale=WM[:, ds(h, 1), b]).then_inc(kwm_ready, 1)

                kwm(0)
                kwm(1)
                misc.adv()
                uses[0].adv()
                act.wait_ge(misc_done, misc.adv() + FIRST)
                stand_alone(act)
                act.activation(XC[:, ds(4 * h, 4), 0:SEQ], ps[:, 4:8, :], ACT.Copy).then_inc(psum_freed[1], 1)
                uses[1].adv()
                act.wait_ge(misc_done, misc.adv() + FIRST)
                stand_alone(act)
                act.activation(RD[:, 0:SEQ], ps[:, 0, :], ACT.Abs)
                act.activation(RD[:, SEQ:T], ps[:, 2, 0:NS], ACT.Abs).then_inc(rd_in, 1)
                for b in range(2, DEC_B):
                    kwm(b)
                units.adv(UNITS)
                act.wait_ge(misc_done, misc.adv() + FIRST)
                stand_alone(act)
                act.wait_ge(n_done, n)
                stand_alone(act)
                act.activation(XC[:, ds(4 * h, 4), SEQ:T], ps[:, 1, 0:4 * NS].rearrange("p (v t) -> p v t", v=4),
                               ACT.Copy).then_inc(psum_freed[0], 1)
                act.wait_ge(psum_freed[0], uses[0].adv())
                stand_alone(act)
                act.activation(XM[:, ds(4 * h, 4), :], XC[:, ds(4 * h, 4), :], ACT.Square).then_inc(sqh_ready, 1)
                misc.adv()
                uses[1].adv()
                act.wait_ge(fv_ready, n)
                stand_alone(act)
                act.activation(FV[:, :], FV[:, :], ACT.Sqrt, bias=EPST[:, :], scale=1.0 / HD).then_inc(sd_ready, 1)
            misc.adv(STATE_JOBS)
            uses[0].adv(2)
            uses[1].adv(2)
            act.wait_ge(misc_done, misc.now() + FIRST)
            act.wait_ge(h_done, HEADS + FIRST)
            for m in range(4):
                for c in range(2 * m, 2 * m + 2):
                    ins = act.activation(BH[:, c, :], X[:, c, :], ACT.Copy, scale=V1[:, G_MIX + 8 + c:G_MIX + 9 + c])
                ins.then_inc(xn_hi, 1)
            for g in range(2):
                with loop(act, 2, {**split_per(8), jobs: 8, uses[0]: 1, uses[1]: 1, blk: 2}) as j:
                    for m in range(2):
                        for k in range(4):
                            split_hi()
                        jobs.adv(4)
                        b = blk.adv()
                        act.wait_ge(psum_freed[m], uses[m].adv())
                        stand_alone(act)
                        act.activation(TG[:, :, :], TG[:, :, :], ACT.Sigmoid).then_inc(silu_done, 1)
                        act.wait_ge(y_ready, b)
                        stand_alone(act)
                        act.activation(AH[:, ds(4 * j + 2 * m, 2), :], TU[:, :, :], ACT.Copy).then_inc(y_hi, 1)
                if g:
                    act.wait_ge(acc_clear, 4)
                with loop(act, 2, {**split_per(8), jobs: 8, uses[0]: 1, uses[1]: 1,
                                   **({xr: 2, sq_t: 2} if g else {})}) as j:
                    for m in range(2):
                        for k in range(4):
                            split_hi()
                        jobs.adv(4)
                        uses[m].adv()
                        if g:
                            prep(4 * j + 2 * m, G_FFN + 8, BH)
            std(1)
            ffn(BH, AH)
            ple(1, PH1, PJ1, None, None, 5)

        @block.vector
        def _(dve):
            step, misc, jobs, hi_t, blk = Tally(), Tally(), Tally(), Tally(), Tally()
            uses = [Tally(), Tally()]
            ys = Tally()

            def link(ins):
                ins.then_inc(dve_step, 1)
                dve.wait_ge(dve_step, step.adv())

            def xn_lo(c0, gain, hi, lo):
                dve.wait_ge(xn_hi, hi_t.adv())
                if gain is None:
                    dve.tensor_tensor(lo[:, ds(c0, 2), :], X[:, ds(c0, 2), :], hi[:, ds(c0, 2), :].bitcast(F32),
                                      ALU.subtract).then_inc(xn_ready, 1)
                    return
                for m in range(2):
                    ins = dve.scalar_tensor_tensor(
                        lo[:, ds(c0 + m, 1), :], X[:, ds(c0 + m, 1), :], V1[:, ds(gain + c0 + m, 1)],
                        hi[:, ds(c0 + m, 1), :].bitcast(F32), ALU.mult, ALU.subtract)
                ins.then_inc(xn_ready, 1)

            def evac_padded(dst, s):
                R = RSTD[:, :]
                dve.tensor_tensor(dst[:, :, TAIL:TAIL + H2], psv[:, s, :, 0, 0:H2],
                                  R[:, 0:H2].unsqueeze(1).broadcast_to([P, 2, H2]), ALU.mult)
                dve.tensor_tensor(dst[:, :, TAIL + H2:XB0], psv[:, s, :, 1, 0:HP2],
                                  R[:, H2:SEQ].unsqueeze(1).broadcast_to([P, 2, HP2]), ALU.mult)
                dve.tensor_tensor(
                    dst[:, :, XB0:XB0 + DEC_B * SEG].rearrange("p m (b t) -> p m b t", b=DEC_B)[:, :, :, TAIL:SEG],
                    psv[:, s, :, 1, HP2:H2].rearrange("p m (b t) -> p m b t", b=DEC_B),
                    R[:, SEQ:T].rearrange("p (b t) -> p b t", b=DEC_B).unsqueeze(1).broadcast_to([P, 2, DEC_B, DEC_S]),
                    ALU.mult).then_inc(psum_freed[s], 1)

            def conv(src, dst, c0, V, cw, cb, per):
                for k in range(CONV_W):
                    for m in range(2):
                        o = dst[:, m, 0:WCONV]
                        wk = V[:, ds(cw + k * per + c0 + m, 1)]
                        if k == 0:
                            ins = dve.tensor_scalar(o, src[:, m, 0:WCONV], wk, V[:, ds(cb + c0 + m, 1)], ALU.mult, ALU.add)
                        else:
                            ins = dve.scalar_tensor_tensor(o, src[:, m, k:k + WCONV], wk, o, ALU.mult, ALU.add)
                    if k < CONV_W - 1:
                        link(ins)
                ins.then_inc(conv_done, 1)

            so = [0]
            cl = [Tally(16), Tally(16)]

            def rstd(s):
                dve.wait_ge(psum_freed[s], uses[s].adv())
                misc.adv()
                dve.reciprocal(RSTD[:, :], RSTD[:, :]).then_inc(std_ready, 1)

            stds = Tally()
            give_credit(dve, conv_done, scan_done, unit_freed, h_done)
            dve.wait_ge(misc_done, misc.adv() + FIRST)
            for dst, src in ((V1[:, :], ps[:, 4, 0:P]), (V2[:, 0:120], ps[:, 4, P:P + 120]),
                             (NT[:, :, :, :].rearrange("p b h k -> p (b h k)"), ps[:, 4, 256:384]),
                             (RGSI[:, :, :].rearrange("p c r -> p (c r)"), ps[:, 5, 0:CR * 32]),
                             (MLSI[:, :, :].rearrange("p c r -> p (c r)"), ps[:, 6, 0:CI * 24])):
                ins = dve.tensor_copy(dst, src)
                ins.then_inc(dve_step, 1)
                step.adv()
            uses[1].adv()
            dve.wait_ge(dve_step, step.now())
            dve.nop().then_inc(vecs_ready, 1)
            dve.nop().then_inc(psum_freed[1], 1)
            for i, (t0, n) in enumerate(TT):
                s = i % 2
                dve.wait_ge(misc_done, misc.adv() + FIRST)
                uses[s].adv()
                dve.tensor_copy(X[:, :, t0:t0 + n],
                                ps[:, 4 * s:4 * s + 2, :].rearrange("p b (c t) -> p (b c) t", t=P)[:, :, 0:n])\
                    .then_inc(psum_freed[s], 1)
            dve.wait_ge(psum_freed[0], 3)
            dve.wait_ge(psum_freed[1], 3)
            for m in range(4):
                dve.nop().then_inc(x_ready, 1)
            for m in range(4):
                xn_lo(2 * m, G_MIX, AH, AL)
            dve.wait_ge(lam_e, 1)
            e_, z, z2, p = SP8[:, 1, :], DT[:, 0, 0:CR], DT[:, 0, 16:16 + CR], DT[:, 0, 32:32 + CR]
            link(dve.tensor_scalar(z2, e_, 2.0, None, ALU.add))
            link(dve.reciprocal(z2, z2))
            link(dve.tensor_tensor(z, e_, z2, ALU.mult))
            link(dve.tensor_tensor(z2, z, z, ALU.mult))
            link(dve.tensor_scalar(p, z2, 1.0 / 17, None, ALU.mult))
            for k in (15, 13, 11, 9, 7, 5, 3):
                link(dve.scalar_tensor_tensor(p, p, 1.0 / k, z2, ALU.add, ALU.mult))
            link(dve.scalar_tensor_tensor(p, p, 1.0, z, ALU.add, ALU.mult))
            link(dve.tensor_scalar(z, V1[:, C_LAM:C_LAM + CR], -1.0, 0.0, ALU.mult, ALU.max))
            link(dve.scalar_tensor_tensor(p, p, 2.0, z, ALU.mult, ALU.add))
            link(dve.tensor_scalar(SP8[:, 0, :], p, 8.0, None, ALU.mult))
            link(dve.tensor_scalar(SP8[:, 1, :], p, -8.0, None, ALU.mult))
            rstd(1)
            dve.wait_ge(std_ready, stds.adv())
            with loop(dve, 3, {jobs: 20, uses[0]: 4, uses[1]: 4, blk: 2, step: 2 * 10}) as j:
                for jj in range(2):
                    c0 = 4 * j + 2 * jj
                    b = blk.adv()
                    dve.wait_ge(slab_used, jobs.adv(4) + 2 * RING)
                    dve.wait_ge(tails_out, b - 1 + FIRST)
                    evac_padded(XBP, 0)
                    dve.wait_ge(psum_freed[0], uses[0].adv())
                    dve.wait_ge(pads_ready, b)
                    dve.wait_ge(xc_hi, b - 1 + FIRST)
                    conv(XBP, XCP, c0, V1, C_RCW, C_RCB, CR)
                    dve.wait_ge(xc_hi, b + FIRST)
                    src_s = XCP[:, :, XB0:XB0 + DEC_B * SEG].rearrange("p m (b t) -> p m b t", b=DEC_B)[:, :, :, 0:DEC_S]
                    hp, hs = tight(XCH)
                    lp, ls = tight(XCL)
                    dve.tensor_tensor(lp, XCP[:, :, 0:SEQ], hp.bitcast(F32), ALU.subtract)
                    dve.tensor_tensor(ls, src_s, hs.bitcast(F32), ALU.subtract).then_inc(xc_ready, 1)
                    dve.wait_ge(slab_used, jobs.adv(4) + 2 * RING)
                    dve.tensor_tensor(pair5(GT[:, :, :]), psv[:, 1, :, :, 0:H2], RB, ALU.mult).then_inc(psum_freed[1], 1)
                    uses[1].adv()
                    jobs.adv(2)
                    uses[0].adv()
                    uses[1].adv()
                    dve.wait_ge(s_ready, b)
                    dve.wait_ge(y_lo, b - 1 + FIRST)
                    link(dve.tensor_scalar(DT[:, :, :], ST[:, :, :], 1.0, None, ALU.add))
                    link(dve.reciprocal(DT[:, :, :], DT[:, :, :]))
                    dve.tensor_tensor(ST[:, :, :], ST[:, :, :], DT[:, :, :], ALU.mult).then_inc(v_in, 1)
                    ip, is_ = tight(IT)
                    dve.tensor_tensor(ip, ip, XCP[:, :, 0:SEQ], ALU.mult)
                    link(dve.tensor_tensor(is_, is_, src_s, ALU.mult))
                    up_p = UP[:, :, 0:SEQ]
                    up_s = UP[:, :, SEQ:WSCAN].rearrange("p m (b t) -> p m b t", b=DEC_B)
                    dve.tensor_copy(up_s[:, :, :, 0], RGSI[:, ds(c0, 2), 24:32])
                    dve.wait_ge(v_ready, b)
                    vp, vs = tight(ST)
                    dve.tensor_tensor(up_p, vp, ip, ALU.mult)
                    link(dve.tensor_tensor(up_s[:, :, :, 1:HSEG], vs, is_, ALU.mult))
                    dve.wait_ge(a_ready, b)
                    dve.wait_ge(h_out, b - 1 + FIRST)
                    for m in range(2):
                        ins = dve.tensor_tensor_scan(HPD[:, m, :], AP_[:, m, :], UP[:, m, :], 0.0, ALU.mult, ALU.add)
                        if m == 0:
                            link(ins)
                    ins.then_inc(scan_done, 1)
                    dve.wait_ge(scan_done, b + FIRST)
                    dve.wait_ge(gelu_done, b)
                    dve.wait_ge(y_lo, b - 1 + FIRST)
                    gp, gs = tight(GT)
                    yp, ys_ = tight(YF)
                    dve.tensor_tensor(yp, HPD[:, :, 0:SEQ], gp, ALU.mult)
                    dve.tensor_tensor(ys_, HPD[:, :, SEQ:WSCAN].rearrange("p m (b t) -> p m b t", b=DEC_B)[:, :, :, 1:HSEG],
                                      gs, ALU.mult).then_inc(y_ready, 1)
                    link(dve.nop())
                    link(dve.nop())

            def add_to_x(n_slabs, s, c0, ready):
                dve.wait_ge(slab_used, jobs.adv(n_slabs) + 2 * RING)
                xx = pair4(X[:, ds(c0, 2), :])
                dve.tensor_tensor(xx, xx, psum4(s), ALU.add).then_inc(psum_freed[s], 1)
                u = uses[s].adv()
                if ready:
                    dve.wait_ge(psum_freed[s], u)
                    dve.nop().then_inc(x_ready, 1)

            with loop(dve, 2, {jobs: 12, uses[0]: 1, uses[1]: 1, hi_t: 2}) as j:
                for m in range(2):
                    add_to_x(6, m, 4 * j + 2 * m, True)
                    xn_lo(4 * j + 2 * m, G_FFN, AH, AL)
            rstd(1)
            dve.wait_ge(std_ready, stds.adv())

            def ffn(hi, lo):
                for g, (g0, gn) in enumerate(GROUPS):
                    with loop(dve, gn // 2, {jobs: 8, uses[0]: 1, uses[1]: 1, blk: 1, ys: 1, step: 1}) as j:
                        b = blk.adv()
                        y = ys.adv()
                        dve.wait_ge(slab_used, jobs.adv(4) + 2 * RING)
                        dve.tensor_tensor(pair5(TG[:, :, :]), psv[:, 0, :, :, 0:H2], RB, ALU.mult).then_inc(psum_freed[0], 1)
                        uses[0].adv()
                        dve.wait_ge(slab_used, jobs.adv(4) + 2 * RING)
                        dve.wait_ge(silu_done, y)
                        dve.wait_ge(y_lo, b - 1 + FIRST)
                        link(dve.tensor_tensor(pair5(TU[:, :, :]), psv[:, 1, :, :, 0:H2], pair5(TG[:, :, :]), ALU.mult))
                        dve.nop().then_inc(psum_freed[1], 1)
                        uses[1].adv()
                        dve.tensor_tensor(pair5(TU[:, :, :]), pair5(TU[:, :, :]), RB, ALU.mult).then_inc(y_ready, 1)
                    ks = gn // 2
                    n = 4 if ks % 2 else 2
                    last = g == len(GROUPS) - 1
                    with loop(dve, 4 // n, {jobs: ks * n, uses[0]: n // 2, uses[1]: n // 2, hi_t: n if last else 0}) as j:
                        for m in range(n):
                            add_to_x(ks, m % 2, 4 * j + 2 * m, last)
                            if last:
                                xn_lo(4 * j + 2 * m, None, hi, lo)

            def ple(layer, PH, PL, PJ, gain, hi, lo):
                dve.wait_ge(misc_done, misc.adv() + FIRST)
                dve.wait_ge(pt_hi, layer + 1)
                dve.tensor_tensor(PL[:, :, 0:SEQ], ps[:, 0:4:2, 0:SEQ], PH[:, :, 0:SEQ].bitcast(F32), ALU.subtract)
                link(dve.tensor_tensor(PL[:, :, SEQ:T], ps[:, 1:4:2, 0:NS], PH[:, :, SEQ:T].bitcast(F32), ALU.subtract))
                dve.nop().then_inc(pt_ready, 1)
                dve.nop().then_inc(psum_freed[0], 1)
                uses[0].adv()
                jobs.adv(4)
                uses[0].adv(2)
                uses[1].adv(2)
                with loop(dve, 2, {jobs: 8, uses[0]: 1, uses[1]: 1, hi_t: 0 if hi is None else 2, step: 2}) as j:
                    for m in range(2):
                        s = (m + 1) % 2
                        jobs.adv(4)
                        dve.wait_ge(psum_freed[s], uses[s].adv())
                        c0 = 4 * j + 2 * m
                        link(dve.tensor_tensor(TG[:, :, :], TG[:, :, :], PJ[:, ds(c0, 2), :], ALU.mult))
                        dve.tensor_tensor(X[:, ds(c0, 2), :], X[:, ds(c0, 2), :], TG[:, :, :], ALU.add).then_inc(x_ready, 1)
                        if hi is not None:
                            xn_lo(c0, gain, hi, lo)
                rstd(1)
                dve.wait_ge(std_ready, stds.adv())

            ffn(AH, AL)
            ple(0, PH0, PL0, PJ0, G_MIX + 8, BH, BL)
            ml = Tally()
            with loop(dve, 4, {jobs: 8, uses[0]: 1, uses[1]: 1, ml: 2, step: 6}) as j:
                for m in range(2):
                    c0 = 4 * j + 2 * m
                    n = ml.adv()
                    dve.wait_ge(slab_used, jobs.adv(4) + 2 * RING)
                    dve.wait_ge(tails_out, 6 + n - 1 + FIRST)
                    dve.wait_ge(xm_copied, n - 1)
                    evac_padded(XMP, m)
                    dve.wait_ge(psum_freed[m], uses[m].adv())
                    dve.wait_ge(pads_ready, 6 + n)
                    dve.wait_ge(xc_silu, n - 1)
                    conv(XMP, XCV, c0, V2, C_MCW, C_MCB, CI)
            dve.wait_ge(misc_done, misc.adv() + FIRST)
            pg = ps[:, 0:2, 0:H2]
            link(dve.memset(RM[:, :], 1.0))
            dve.memset(RM[:, 0:1], 0.0)
            dve.memset(RM[:, SEQ:T:DEC_S], 0.0)
            dve.wait_ge(wgr_loaded, 16 * 14)
            dve.tensor_scalar(LI[:, :].rearrange("p (h n) -> p h n", h=2), pg[0:4], BG[:, 0:1], None, ALU.add)
            dve.tensor_copy(FF[:, :].rearrange("p (h n) -> p h n", h=2), pg[32:36]).then_inc(psum_freed[0], 1)
            dve.wait_ge(psum_freed[0], uses[0].adv())
            dve.tensor_scalar(FF[:, :], FF[:, :], BG[:, 1:2], None, ALU.add).then_inc(f_ready, 1)
            dve.tensor_scalar(NEGM[:, :], RM[:, :], 1.0, -NEG, ALU.subtract, ALU.mult)
            dve.wait_ge(ln_ready, 1)
            link(dve.scalar_tensor_tensor(LF[:, :], FF[:, :], 0.0, AB[:, :], ALU.min, ALU.subtract))
            link(dve.tensor_tensor_scan(BC[:, :], RM[:, :], LF[:, :], 0.0, ALU.mult, ALU.add))
            link(dve.tensor_tensor(AS[:, :], LI[:, :], BC[:, :], ALU.subtract))
            link(dve.tensor_copy(A1[:, :], AS[:, :]))
            dve.tensor_scalar(A1[:, 0:1], AS[:, 0:1], 0.0, None, ALU.max)
            link(dve.tensor_tensor(A1[:, SEQ:T:DEC_S], AS[:, SEQ:T:DEC_S], M0T[:, :], ALU.max))
            link(dve.tensor_tensor_scan(MR[:, :], NEGM[:, :], A1[:, :], 0.0, ALU.add, ALU.max))
            link(dve.tensor_tensor(T1[:, :], BC[:, :], MR[:, :], ALU.add))
            dve.tensor_copy(MO[:, 0:1], T1[:, SEQ - 1:SEQ])
            dve.tensor_copy(MO[:, 1:1 + DEC_B], T1[:, SEQ + DEC_S - 1:T:DEC_S])
            b8 = lambda t: t.rearrange("p (b t) -> p b t", b=DEC_B)
            bc8 = lambda t: t.unsqueeze(2).broadcast_to([HEADS, DEC_B, DEC_S])
            dve.tensor_tensor(b8(IWR[:, :]), bc8(M0T[:, :]), b8(MR[:, SEQ:T]), ALU.subtract)
            dve.tensor_scalar(WS[:, 0:SEQ], AS[:, 0:SEQ], MR[:, SEQ - 1:SEQ], None, ALU.subtract)
            dve.tensor_tensor(b8(WS[:, SEQ:T]), b8(AS[:, SEQ:T]), bc8(MR[:, SEQ + DEC_S - 1:T:DEC_S]),
                              ALU.subtract).then_inc(t1_ready, 1)
            dve.wait_ge(misc_done, misc.adv() + FIRST)
            dve.tensor_copy(COLS[:, 0:4, :], ps[:, 4, 0:32].rearrange("p (i g) -> p i g", g=8))
            dve.tensor_copy(COLS[0:NS, 4, :], ps[0:NS, 4, 32:40]).then_inc(psum_freed[1], 1)
            dve.wait_ge(psum_freed[1], uses[1].adv())
            dve.tensor_tensor(WM[:, :, :], COLS[0:NS, 4, 4:8].unsqueeze(2).broadcast_to([NS, HEADS, DEC_B]),
                              BM8[:, :].unsqueeze(1).broadcast_to([NS, HEADS, DEC_B]), ALU.mult).then_inc(cols_ready, 1)
            dve.wait_ge(rows_ready, 1)
            heads, units = Tally(), Tally()
            with loop(dve, HEADS, {misc: 13, uses[0]: 6, uses[1]: 6, heads: 1, units: UNITS, step: 8, cl[0]: 3, cl[1]: 3}) as h:
                n = heads.adv()
                dve.wait_ge(misc_done, misc.now() + FIRST)
                dve.tensor_scalar(SELH[:, :], ONES[0:HEADS, :], IDN[0:HEADS, ds(h, 1)], None, ALU.mult).then_inc(sel_ready, 1)
                misc.adv(4)
                uses[0].adv(2)
                dve.wait_ge(psum_freed[1], uses[1].adv())
                for i in range(4):
                    dve.tensor_scalar(PP[:, PPO[i]:PPO[i + 1]], MB[:, i * P:SEQ], COLS[:, i, ds(h, 1)], 0.0,
                                      ALU.subtract, ALU.max)
                dve.tensor_scalar(PSM[:, :], MB[0:NS, SEQ:T], COLS[0:NS, 4, ds(h, 1)], 0.0,
                                  ALU.subtract, ALU.max).then_inc(e_ready, 1)
                dve.wait_ge(psum_freed[1], uses[1].adv())
                qi = XM[:, ds(4 * h, 1), 0:4 * NS].rearrange("p o (k t) -> p (o k) t", k=4)
                nq = XM[:, ds(4 * h + 1, 1), 0:4 * NS].rearrange("p o (k b t) -> p (o k) b t", k=4, b=DEC_B)
                link(dve.tensor_tensor(qi, QT[:, :, SEQ:T], IWB[:, :].unsqueeze(1).broadcast_to([P, 4, NS]), ALU.mult))
                dve.tensor_tensor(nq, qi.rearrange("p k (b t) -> p k b t", b=DEC_B),
                                  NT[:, :, ds(h, 1), :].rearrange("p b o k -> p (o k) b").unsqueeze(3)
                                  .broadcast_to([P, 4, DEC_B, DEC_S]), ALU.mult).then_inc(nq_ready, 1)
                misc.adv(3)
                uses[0].adv(2)
                uses[1].adv()
                dve.wait_ge(misc_done, misc.adv() + FIRST)
                dve.wait_ge(masked, n)
                dve.wait_ge(kt4_done, n)
                dve.tensor_tensor(PSM[:, :], PSM[:, :], ps[0:NS, 5, 0:NS], ALU.mult).then_inc(psum_freed[1], 1)
                uses[1].adv()
                dve.wait_ge(misc_done, misc.adv() + FIRST)
                for i in range(4):
                    ins = dve.tensor_tensor(PP[:, PPO[i]:PPO[i + 1]], PP[:, PPO[i]:PPO[i + 1]],
                                            ps[:, i, i * P:SEQ], ALU.mult)
                ins.then_inc(psum_freed[0], 1)
                uses[0].adv()
                misc.adv()
                uses[1].adv()
                dve.wait_ge(misc_done, misc.adv() + FIRST)
                nt = NT[:, :, ds(h, 1), :].rearrange("p b o k -> p (o k) b")
                dve.tensor_copy(NP[:, ds(h, 1), :], ps[:, 3, 0:4].unsqueeze(1))
                link(dve.tensor_tensor(nt, nt, IWB[:, DEC_S - 1:NS:DEC_S].unsqueeze(1).broadcast_to([P, 4, DEC_B]), ALU.mult))
                dve.tensor_tensor(nt, nt, ps[:, 3, 8:40].rearrange("p (k b) -> p k b", k=4), ALU.add).then_inc(n_done, 1)
                dve.wait_ge(rd_in, n)
                link(dve.tensor_tensor(RD, RD, EM, ALU.max))
                link(dve.reciprocal(RD, RD))
                dve.tensor_tensor(FV, RD, RD, ALU.mult)
                for v in range(UNITS):
                    dve.wait_ge(unit_done, units.adv() + 2 * FIRST)
                    bank = 4 + 2 * (v % 2)
                    c = CS[:, v % CSLOTS]
                    if v < 2:
                        dve.wait_ge(c_loaded[v], cl[v].adv())
                        cl[v].adv(UNITS // CSLOTS - 1)
                        ins = dve.tensor_copy(c, ps[:, bank:bank + 2, :])
                    else:
                        b = (v - 2) // 2
                        cc = c.rearrange("p k v -> p (k v)")
                        ins = dve.scalar_tensor_tensor(cc, cc, IWB[:, DEC_S * b + DEC_S - 1:DEC_S * b + DEC_S],
                                                       ps[:, bank:bank + 2, :].rearrange("p k v -> p (k v)"), ALU.mult, ALU.add)
                    ins.then_inc(unit_freed, 1)
                misc.adv()
                uses[0].adv()
                dve.wait_ge(misc_done, misc.adv() + FIRST)
                link(dve.tensor_tensor(FV[:, 0:SEQ], FV[:, 0:SEQ], ps[:, 4, :], ALU.mult))
                dve.tensor_tensor(FV[:, SEQ:T], FV[:, SEQ:T], ps[:, 5, 0:NS], ALU.mult).then_inc(psum_freed[1], 1)
                dve.wait_ge(psum_freed[1], uses[1].adv())
                link(dve.nop())
                dve.nop().then_inc(fv_ready, 1)
                dve.wait_ge(sd_ready, n)
                link(dve.reciprocal(FV, FV))
                link(dve.tensor_tensor(FV, FV, RD, ALU.mult))
                for c in range(4):
                    hh = XC[:, ds(4 * h + c, 1), :].rearrange("p o t -> p (o t)")
                    ins = dve.scalar_tensor_tensor(hh, hh, V2[:, ds(C_MN + c + 4 * h, 1)], FV, ALU.mult, ALU.mult)
                ins.then_inc(h_done, 1)
            for s, srcs in ((0, ((SRO[:, :].rearrange("p (b n) -> p b n", b=3), ps[0:36, 0:3, :]),)),
                            (1, ((SMO[:, :].rearrange("p (b n) -> p b n", b=4), ps[0:27, 4:8, :]),)),
                            (0, ((NTO[:, 0, :], ps[:, 0, 0:P]),)),
                            (1, ((NTO[0:16, 1, :], ps[0:16, 4, 0:P]),))):
                dve.wait_ge(misc_done, misc.adv() + FIRST)
                uses[s].adv()
                for dst, src in srcs:
                    if s == 0:
                        for slot in range(CSLOTS):
                            dve.wait_ge(c_stored[slot], 16 * HEADS * UNITS // CSLOTS + 16 * FIRST)
                    dve.tensor_copy(dst, src).then_inc(states_out, 1)
                dve.wait_ge(states_out, 1 + so[0])
                so[0] += 1
                dve.nop().then_inc(psum_freed[s], 1)
            for m in range(4):
                xn_lo(2 * m, G_MIX + 8, BH, BL)
            for g in range(2):
                with loop(dve, 2, {jobs: 8, uses[0]: 1, uses[1]: 1, blk: 2, ys: 2}) as j:
                    for m in range(2):
                        b = blk.adv()
                        y = ys.adv()
                        dve.wait_ge(slab_used, jobs.adv(4) + 2 * RING)
                        dve.wait_ge(y_ready, b - 1)
                        dve.tensor_tensor(pair5(TG[:, :, :]), psv[:, m, :, :, 0:H2], RB, ALU.mult).then_inc(psum_freed[m], 1)
                        uses[m].adv()
                        dve.wait_ge(silu_done, y)
                        dve.wait_ge(y_lo, b - 1 + FIRST)
                        dve.tensor_tensor(TU[:, :, :], TG[:, :, :], XC[:, ds(8 * g + 4 * j + 2 * m, 2), :], ALU.mult)\
                            .then_inc(y_ready, 1)
                with loop(dve, 2, {jobs: 8, uses[0]: 1, uses[1]: 1, **({hi_t: 2} if g else {})}) as j:
                    for m in range(2):
                        add_to_x(4, m, 4 * j + 2 * m, bool(g))
                        if g:
                            xn_lo(4 * j + 2 * m, G_FFN + 8, BH, BL)
            rstd(1)
            dve.wait_ge(std_ready, stds.adv())
            ffn(BH, BL)
            ple(1, PH1, PL1, PJ1, None, None, None)
            for c in range(CX):
                dve.scalar_tensor_tensor(X[:, c, :], X[:, c, :], V2[:, C_NF + c:C_NF + c + 1], RSTD[:, :],
                                         ALU.mult, ALU.mult).then_inc(x_ready, 1)
            for i, (t0, n) in enumerate(TT):
                s = i % 2
                dve.wait_ge(misc_done, misc.adv() + FIRST)
                if i >= 2:
                    dve.wait_ge(y_stored[s], 16 * (i // 2))
                dve.tensor_copy(YTK[0:n, s, :].rearrange("p (b c) -> p b c", b=2), ps[0:n, 4 * s:4 * s + 2, :]).then_inc(out_rows, 1)
                dve.wait_ge(out_rows, i + 1)
                dve.nop().then_inc(psum_freed[s], 1)

        @block.tensor
        def _(pe):
            slabs, blk, xn, ys = Tally(), Tally(), Tally(), Tally()
            uses = [Tally(), Tally()]
            phase = [0]

            def use(s):
                before = uses[s].adv() - 1
                if not is_zero(before):
                    pe.wait_ge(psum_freed[s], before)

            def job(s, pairs, operand, before=None):
                use(s)
                for i in range(pairs):
                    if before:
                        before(i)
                    pe.wait_ge(lo_ready, slabs.adv() + RING)
                    w = phase[0] % 4
                    phase[0] += 1
                    for k in range(2):
                        hi, lo = operand(2 * i + k)
                        for m in range(2):
                            wc = slice(m * P, m * P + P)
                            for q, (a, x) in enumerate(((WH, hi), (WH, lo), (WL, hi))):
                                for h in range(2):
                                    ins = pe.matmul(ps[:, 4 * s + 2 * m + h, 0:H2], a[:, w, k, wc], x[:, h * H2:h * H2 + H2],
                                                    start=i == 0 and k == 0 and q == 0,
                                                    stop=i == pairs - 1 and k == 1 and q == 2)
                    ins.then_inc(slab_used, 1)

            def norm(s, acc):
                use(s)
                pe.wait_ge(acc_ready, acc)
                for h in range(2):
                    for k in range(2):
                        ins = pe.matmul(ps[:, 4 * s + h, 0:H2], ONES[:, :], ACC[:, k, h * H2:h * H2 + H2], start=k == 0, stop=k == 1)
                ins.then_inc(misc_done, 1)

            def chunks(hi, lo):
                return lambda k: (hi[:, k, :], lo[:, k, :])

            give_credit(pe, slab_used, misc_done, unit_done)
            pe.wait_ge(const_ready, 1)
            pe.wait_ge(rows_loaded, ROWS_LOADED)
            use(1)
            pe.transpose(ps[:, 4, 0:P], VR[:, 0, :], IDN[:, :])
            pe.transpose(ps[:, 4, P:P + 120], VR[0:120, 1, :], IDN[0:120, 0:120])
            pe.transpose(ps[:, 4, 256:384], NR[:, :], IDN[:, :])
            for c in range(CR):
                pe.transpose(ps[:, 5, c * 32:c * 32 + 32], RSR[:, c * P:c * P + P], IDN[0:32, 0:32])
            for c in range(CI):
                ins = pe.transpose(ps[:, 6, c * 24:c * 24 + 24], MSR[:, c * P:c * P + P], IDN[0:24, 0:24])
            ins.then_inc(misc_done, 1)
            pe.wait_ge(x_loaded, 16 * len(TT))
            for i, (t0, n) in enumerate(TT):
                s = i % 2
                use(s)
                for c in range(CX):
                    ins = pe.transpose(ps[:, 4 * s + c // 4, (c % 4) * P:(c % 4) * P + n], XTK[0:n, i, c * P:c * P + P],
                                       IDN[0:n, 0:n])
                ins.then_inc(misc_done, 1)
            norm(1, 4)
            pe.wait_ge(xn_ready, 4)
            with loop(pe, 3, {slabs: 20, uses[0]: 4, uses[1]: 4, blk: 2}) as j:
                for jj in range(2):
                    b = blk.adv()
                    job(0, 4, chunks(AH, AL))
                    job(1, 4, chunks(AH, AL))
                    pe.wait_ge(xc_ready, b)
                    job(0, 1, chunks(XCH, XCL))
                    job(1, 1, chunks(XCH, XCL))
            pe.wait_ge(y_lo, 6 + FIRST)
            with loop(pe, 2, {slabs: 12, uses[0]: 1, uses[1]: 1}) as j:
                for m in range(2):
                    job(m, 6, chunks(YH, YL))
            norm(1, 8)
            pe.wait_ge(xn_ready, 8)
            y_done = [6]

            def ffn(hi, lo, gh, gl):
                for g, (g0, gn) in enumerate(GROUPS):
                    with loop(pe, gn // 2, {slabs: 8, uses[0]: 1, uses[1]: 1}) as j:
                        for s in range(2):
                            job(s, 4, chunks(hi, lo))
                    ks = gn // 2
                    n = 4 if ks % 2 else 2
                    with loop(pe, 4 // n, {slabs: ks * n, uses[0]: n // 2, uses[1]: n // 2}) as j:
                        for m in range(n):
                            job(m % 2, ks, chunks(gh, gl), lambda i: pe.wait_ge(y_lo, y_done[0] + i + 1 + FIRST))
                    y_done[0] += ks

            def ple(layer, PH, PL, hi, lo, acc, xn0):
                pe.wait_ge(p_loaded, 32 * (layer + 1))
                use(0)
                for c in range(2):
                    for i, (t0, n) in enumerate(TT):
                        dst = ps[:, 2 * c, t0:t0 + n] if t0 < SEQ else ps[:, 2 * c + 1, 0:n]
                        ins = pe.transpose(dst, PTK[0:n, i, c * P:c * P + P], IDN[0:n, 0:n])
                ins.then_inc(misc_done, 1)
                pe.wait_ge(pt_ready, layer + 1)
                for m in range(4):
                    job((m + 1) % 2, 1, chunks(PH, PL))
                with loop(pe, 2, {slabs: 8, uses[0]: 1, uses[1]: 1}) as j:
                    for m in range(2):
                        job((m + 1) % 2, 4, chunks(hi, lo), lambda i: pe.wait_ge(xn_ready, xn0 + i + 1))
                norm(1, acc)
                if not layer:
                    pe.wait_ge(xn_ready, xn0 + 8)

            ffn(AH, AL, GH, GL)
            ple(0, PH0, PL0, AH, AL, 12, 8)
            with loop(pe, 4, {slabs: 8, uses[0]: 1, uses[1]: 1}) as j:
                for s in range(2):
                    job(s, 4, chunks(BH, BL))
            use(0)
            pe.wait_ge(et_ready, 2)
            pe.wait_ge(xm_copied, 8)
            order = [CI + c for c in range(CI)] + list(range(CI))
            for i, c in enumerate(order):
                if c < CI and c % 2 == 0:
                    pe.wait_ge(xc_silu, c // 2 + 1)
                for hf in range(2):
                    src = (XC if c < CI else XM)[:, c % CI, hf * H2:hf * H2 + H2]
                    ins = pe.matmul(ps[0:36, hf, 0:H2], ET[:, c, :], src, start=i == 0, stop=i == 2 * CI - 1)
            ins.then_inc(misc_done, 1)
            use(1)
            pe.wait_ge(rows_ready, 1)
            for i, (t0, n) in enumerate(TT):
                for k, t in enumerate((AS, WS)):
                    ins = pe.transpose(ps[0:n, 4, i * 8 + 4 * k:i * 8 + 4 * k + 4], t[:, t0:t0 + n], IDN[0:4, 0:4])
            ins.then_inc(misc_done, 1)
            pe.wait_ge(cols_ready, 1)
            heads, units, kws = Tally(), Tally(), Tally()
            cl = [Tally(16) for _ in range(CSLOTS)]
            with loop(pe, HEADS, {uses[0]: 6, uses[1]: 6, heads: 1, units: UNITS, kws: DEC_B,
                                  **{t: UNITS // CSLOTS for t in cl}}) as h:
                n = heads.adv()
                done = lambda ins: ins.then_inc(misc_done, 1)
                use(0)
                pe.wait_ge(ht_ready, n)
                pe.wait_ge(wbd_ready, n)

                def v_rows(i, bank):
                    t0, nt = TT[i]
                    for c in range(4):
                        ins = pe.matmul(ps[0:nt, bank, c * P:c * P + P], HT[:, c, t0:t0 + nt], WBD[:, 2, c, :],
                                        start=True, stop=True)
                    return ins

                for i in range(4):
                    ins = v_rows(i, i)
                done(ins)
                use(1)
                v_rows(4, 4)
                pe.wait_ge(sel_ready, n)
                pe.matmul(ps[:, 5, :], SELH[:, :], MR[:, 0:SEQ], start=True, stop=True)
                pe.matmul(ps[:, 6, :], SELH[:, :], ER[:, 0:SEQ], start=True, stop=True)
                for k, t in enumerate((MR[:, SEQ:T], ER[:, SEQ:T], IWR[:, :])):
                    ins = pe.matmul(ps[:, 7, k * NS:k * NS + NS], SELH[:, :], t, start=True, stop=True)
                done(ins)
                for i in range(2):
                    for s in range(2):
                        use(s)
                        for m in range(2):
                            c = 2 * s + m
                            for hf in range(2):
                                ins = pe.matmul(ps[:, 4 * s + 2 * m + hf, 0:H2], WBD[:, i, c, :],
                                                XC[:, ds(4 * h + c, 1), hf * H2:hf * H2 + H2].rearrange("p o t -> p (o t)"),
                                                start=True, stop=True)
                        done(ins)
                pe.wait_ge(psum_freed[1], uses[1].now())
                use(0)

                def k_rows(i, bank):
                    t0, nt = TT[i]
                    for c in range(4):
                        ins = pe.transpose(ps[0:nt, bank, c * P:c * P + P], HT[:, c, t0:t0 + nt], IDN[:, :])
                    return ins

                for i in range(4):
                    ins = k_rows(i, i)
                done(ins)
                use(1)
                for c in range(4):
                    pe.matmul(ps[0:NS, 5, 0:NS], HT[:, c, SEQ:T], QT[:, c, SEQ:T], start=c == 0, stop=c == 3)
                done(k_rows(4, 4))
                use(0)
                for i in range(4):
                    for c in range(4):
                        ins = pe.matmul(ps[:, i, i * P:SEQ], HT[:, c, i * P:i * P + P], QT[:, c, i * P:SEQ],
                                        start=c == 0, stop=c == 3)
                done(ins)
                use(1)
                pe.wait_ge(psum_freed[0], uses[0].now())
                for vb in range(4):
                    for i in range(4):
                        ins = pe.matmul(ps[:, 4 + vb, i * P:SEQ], VTK[:, i, vb * P:vb * P + P], PP[:, PPO[i]:PPO[i + 1]],
                                        start=i == 0, stop=i == 3)
                done(ins)
                use(0)
                for i in range(4):
                    pe.matmul(ps[:, 0, i * P:SEQ], ONES[:, :], PP[:, PPO[i]:PPO[i + 1]], start=i == 0, stop=i == 3)
                pe.wait_ge(nq_ready, n)
                pe.matmul(ps[:, 2, 0:NS], ONES[0:NS, :], PSM[:, :], start=True, stop=False)
                for c in range(4):
                    pe.matmul(ps[:, 2, 0:NS], ONES[:, :],
                              XM[:, ds(4 * h + 1, 1), c * NS:c * NS + NS].rearrange("p o t -> p (o t)"), start=False, stop=c == 3)
                for kb in range(4):
                    for i in range(4):
                        pe.matmul(ps[:, 3, kb:kb + 1], KW[:, i, kb * P:kb * P + P], ONES[:, 0:1], start=i == 0, stop=i == 3)
                pe.wait_ge(kt4_done, n)
                for kb in range(4):
                    pe.matmul(ps[:, 3, 8 + 8 * kb:16 + 8 * kb], KTK4[:, kb * P:kb * P + P],
                              WM[:, ds(h, 1), :].rearrange("p o b -> p (o b)"), start=True, stop=True)
                for vb in range(4):
                    ins = pe.matmul(ps[:, 1, vb * NS:vb * NS + NS], VTK[0:NS, 4, vb * P:vb * P + P], PSM[:, :],
                                    start=vb == 0, stop=False, skip_group_check=True)
                done(ins)
                pe.wait_ge(psum_freed[1], uses[1].now())
                for v in range(UNITS):
                    u = units.adv()
                    bank, slot = 4 + 2 * (v % 2), v % CSLOTS
                    pe.wait_ge(unit_freed, u - 2 + 2 * FIRST)
                    cl[slot].adv()
                    if v < 2:
                        for kb in range(2):
                            for i in range(4):
                                kc = 2 * v + kb
                                ins = pe.matmul(ps[:, bank + kb, :], KW[:, i, kc * P:kc * P + P], VTK[:, i, :],
                                                start=i == 0, stop=i == 3)
                    else:
                        b, half = (v - 2) // 2, v % 2
                        pe.wait_ge(c_loaded[slot], cl[slot].now())
                        for kb in range(2):
                            for vb in range(4):
                                col = vb * NS + b * DEC_S
                                ins = pe.matmul(
                                    ps[:, 1, col:col + DEC_S], CS[:, slot, kb, vb * P:vb * P + P],
                                    XM[:, ds(4 * h, 1), (2 * half + kb) * NS + b * DEC_S:(2 * half + kb) * NS + b * DEC_S + DEC_S]
                                    .rearrange("p o t -> p (o t)"), start=False,
                                    stop=v == UNITS - 1 and kb == 1 and vb == 3, skip_group_check=True)
                        if v == UNITS - 1:
                            done(ins)
                        if not half:
                            pe.wait_ge(kwm_ready, kws.adv())
                        for kb in range(2):
                            kc = 2 * half + kb
                            ins = pe.matmul(ps[:, bank + kb, :], KWM[:, b % 2, kc * P:kc * P + P], VTK[0:NS, 4, :],
                                            start=True, stop=True)
                    ins.then_inc(unit_done, 1)
                use(1)
                pe.wait_ge(unit_freed, units.now() + 2 * FIRST)
                pe.wait_ge(sqh_ready, n)
                for k, (bank, c0, cn) in enumerate(((4, 0, SEQ), (5, SEQ, NS))):
                    for c in range(4):
                        ins = pe.matmul(ps[:, bank, 0:cn], ONES[:, :],
                                        XM[:, ds(4 * h + c, 1), c0:c0 + cn].rearrange("p o t -> p (o t)"),
                                        start=c == 0, stop=c == 3)
                done(ins)
            use(0)
            for c in range(CR):
                ins = pe.transpose(ps[0:36, c // 4, (c % 4) * P:(c % 4) * P + P], RGSO[:, c, :], IDN[:, :])
            ins.then_inc(misc_done, 1)
            use(1)
            for c in range(CI):
                ins = pe.transpose(ps[0:27, 4 + c // 4, (c % 4) * P:(c % 4) * P + P], MLSO[:, c, :], IDN[:, :])
            ins.then_inc(misc_done, 1)
            use(0)
            pe.wait_ge(n_done, HEADS)
            pe.transpose(ps[:, 0, 0:P], NT[:, :, :, :].rearrange("p b h k -> p (b h k)"), IDN[:, :]).then_inc(misc_done, 1)
            use(1)
            pe.transpose(ps[0:16, 4, 0:P], NP[:, :, :].rearrange("p h k -> p (h k)"), IDN[:, :]).then_inc(misc_done, 1)
            y0 = y_done[0]
            for g in range(2):
                with loop(pe, 2, {slabs: 8, uses[0]: 1, uses[1]: 1}) as j:
                    for s in range(2):
                        job(s, 4, chunks(BH, BL), lambda i: pe.wait_ge(xn_ready, 16 + i + 1))
                with loop(pe, 2, {slabs: 8, uses[0]: 1, uses[1]: 1}) as j:
                    for s in range(2):
                        job(s, 4, chunks(AH, AL), lambda i: pe.wait_ge(y_lo, y0 + 4 * g + i + 1 + FIRST))
            y_done[0] += 8
            norm(1, 16)
            pe.wait_ge(xn_ready, 24)
            ffn(BH, BL, AH, AL)
            ple(1, PH1, PL1, BH, BL, 20, 24)
            pe.wait_ge(x_ready, X_READY)
            for i, (t0, n) in enumerate(TT):
                s = i % 2
                use(s)
                for c in range(CX):
                    ins = pe.transpose(ps[0:n, 4 * s + c // 4, (c % 4) * P:(c % 4) * P + P], X[:, c, t0:t0 + n], IDN[:, :])
                ins.then_inc(misc_done, 1)


ROWS_LOADED = 16 * 16
STATE_JOBS = 4
X_READY = 36

_OUTS = [("y_prompt", (1, 512, 1024)), ("y_sample", (8, 8, 1024)),
         ("rg_conv_p", (1, 1, 3, 1536)), ("rg_h_p", (1, 1, 1536)), ("ml_conv_p", (1, 1, 3, 2048)),
         ("ml_C_p", (1, 1, 4, 512, 512)), ("ml_n_p", (1, 1, 4, 512)), ("ml_m_p", (1, 1, 4)),
         ("rg_conv_s", (1, 8, 3, 1536)), ("rg_h_s", (1, 8, 1536)), ("ml_conv_s", (1, 8, 3, 2048)),
         ("ml_C_s", (1, 8, 4, 512, 512)), ("ml_n_s", (1, 8, 4, 512)), ("ml_m_s", (1, 8, 4))]


def kernel(**inputs):
    import numpy as _np
    import concourse.bacc as _bacc
    from concourse import mybir as _mybir
    from concourse.bass_utils import run_bass_kernel_spmd as _run

    nc = _bacc.Bacc("TRN2", target_bir_lowering=False, num_devices=1, dynamic_dma_scratch_size=1024)
    arrays, ins, outs = {}, {}, {}
    for name in inputs:
        a = _np.ascontiguousarray(inputs[name])
        arrays[f"in_{name}_dram"] = a
        ins[name] = nc.dram_tensor(f"in_{name}_dram", a.shape, _mybir.dt.from_np(a.dtype), kind="ExternalInput").ap()
    for name, shape in _OUTS:
        outs[name] = nc.dram_tensor(f"out_{name}_dram", shape, _mybir.dt.float32, kind="ExternalOutput").ap()
    hybrid_trunk(nc, ins, outs)
    r = _run(nc, [arrays], core_ids=[0])
    return tuple(r.results[0][f"out_{name}_dram"] for name, _ in _OUTS)
```

```python
from contextlib import ExitStack, contextmanager

import concourse.bass as bass
from concourse import mybir

F32 = mybir.dt.float32
F32R = mybir.dt.float32r
ALU = mybir.AluOpType
ACT = mybir.ActivationFunctionType
ds = bass.ds

P = 128
D_MODEL, SEQ, DEC_B, DEC_S = 1024, 512, 8, 8
NS = DEC_B * DEC_S
GT = NS // 2
T = SEQ + NS
H2 = T // 2
HP2 = SEQ - H2
D_RNN, INNER, D_FF, PLE = 1536, 2048, 2816, 256
CONV_W, TAIL = 4, 3
HEADS, HD = 4, 512
CX, CR, CI, CF = D_MODEL // P, D_RNN // P, INNER // P, D_FF // P
GROUPS = [(0, 8), (8, 8), (16, 6)]
EPS = 1e-6
SEG = TAIL + DEC_S
XB0 = TAIL + SEQ
WPAD = XB0 + DEC_B * SEG
WCONV = WPAD - TAIL
HSEG = 1 + DEC_S
WSCAN = SEQ + DEC_B * HSEG
NEG = -1.0e30
TOTAL = 484
RING = 4
FIRST = 1
UNITS = 2 + 2 * DEC_B
CSLOTS = 6
PROMPT_UNITS = (8, 9)
UNIT = [(None, v - PROMPT_UNITS[0]) if v in PROMPT_UNITS else divmod(v if v < PROMPT_UNITS[0] else v - 2, 2)
        for v in range(UNITS)]
PPO = [0, 512, 896, 1152, 1280]
TT = [(i * P, min(P, T - i * P)) for i in range(-(-T // P))]


class Tally:
    looped = None

    def __init__(self, step=1):
        self.step, self.at, self.k, self.j, self.per = step, 0, 0, None, 0

    def adv(self, n=1):
        if self.j is None:
            assert Tally.looped is None, "a tally that the loop doesn't know"
            self.at += n
        else:
            self.k += n
        return self.now()

    def now(self):
        if self.j is None or not self.per:
            return (self.at + self.k) * self.step
        return self.j * (self.per * self.step) + (self.at + self.k) * self.step


def is_zero(count):
    return isinstance(count, int) and count == 0


@contextmanager
def loop(eng, n, per):
    with eng.Fori(0, n) as j:
        Tally.looped = per
        for t, p in per.items():
            t.j, t.per, t.k = j, p, 0
        yield j
        for t, p in per.items():
            assert t.k == p, (t.k, p)
            t.j, t.k, t.at = None, 0, t.at + p * n
        Tally.looped = None




def hybrid_trunk(nc, I, O):
    ctx = ExitStack()
    with ctx:
        def sb_in(stack, name, shape, dt=F32):
            return stack.enter_context(nc.sbuf_tensor(name, shape, dt))

        def sb(name, shape, dt=F32):
            return sb_in(ctx, name, shape, dt)

        credits = {}

        def sem(name, credit=0):
            s = ctx.enter_context(nc.semaphore(name))
            credits[id(s)] = credit
            return s

        waits_passed = {}

        def give_credit(eng, *sems):
            for s in sems:
                eng.nop().then_inc(s, credits[id(s)])

        def stand_alone(eng):
            if Tally.looped is not None:
                eng.sem_inc(waits_passed[id(eng)])

        X = sb("X", [P, CX, T])
        RAW = sb("RAW", [P, 4, 2, 256])
        WH = sb("WH", [P, 4, 2, 256], F32R)
        WL = sb("WL", [P, 4, 2, 256], F32R)
        RSTD = sb("RSTD", [P, T])
        ACC = sb("ACC", [P, 2, T])
        SQ = sb("SQ", [P, 2, T])
        IDN = sb("IDN", [P, P])
        ONES = sb("ONES", [P, P])
        V1 = sb("V1", [P, P])
        V2 = sb("V2", [P, P])
        SP8 = sb("SP8", [P, 2, CR])
        EPST = sb("EPST", [P, 1])
        RGSI = sb("RGSI", [P, CR + 2, 32])
        RGSO = sb("RGSO", [P, CR, 36])
        MLSI = sb("MLSI", [P, CI, 24])
        MLSO = sb("MLSO", [P, CI, 27])
        NT = sb("NT", [P, DEC_B, HEADS, 4])
        NP = sb("NP", [P, HEADS, 4])
        WQKV = sb("WQKV", [P, 3, CI + 4, 4])
        TRI = sb("TRI", [P, P])
        M64 = sb("M64", [NS, NS])
        BM3 = sb("BM3", [3 * GT, 4])
        BDM = sb("BDM", [P, 32])
        M0T = sb("M0T", [HEADS, DEC_B])
        BG = sb("BG", [HEADS, 2])
        MO = sb("MO", [HEADS, 1 + DEC_B])
        COLS = sb("COLS", [P, len(TT), 8])
        WM3 = sb("WM3", [3 * GT, 2, HEADS, 4])

        kb36 = [P, CX, T]
        with ExitStack() as p1:
            AH, AL = sb_in(p1, "AH", kb36, F32R), sb_in(p1, "AL", kb36, F32R)
            GH, GL = sb_in(p1, "GH", kb36, F32R), sb_in(p1, "GL", kb36, F32R)
            BH, BL = sb_in(p1, "BH", kb36, F32R), sb_in(p1, "BL", kb36, F32R)
            TG = sb_in(p1, "TG", [P, 2, T])
            TU = sb_in(p1, "TU", [P, 2, T])
            PTK = sb_in(p1, "PTK", [P, len(TT), PLE])
            YTK = sb_in(p1, "YTK", [P, 2, D_MODEL])
            SRO = sb_in(p1, "SRO", [36, D_RNN])
            SMO = sb_in(p1, "SMO", [27, INNER])
            NTO = sb_in(p1, "NTO", [P, 2, P])
        with ExitStack() as p0:
            sb_in(p0, "fill0", [P, 2, CX, T])
            YH, YL = sb_in(p0, "YH", [P, CR, T], F32R), sb_in(p0, "YL", [P, CR, T], F32R)
            XBP = sb_in(p0, "XBP", [P, 2, WPAD + 1])
            XCP = sb_in(p0, "XCP", [P, 2, WPAD + 1])
            XCH, XCL = sb_in(p0, "XCH", [P, 2, T], F32R), sb_in(p0, "XCL", [P, 2, T], F32R)
            GEL = sb_in(p0, "GT", [P, 2, T])
            RT = sb_in(p0, "RT", [P, 2, T])
            IT = sb_in(p0, "IT", [P, 2, T])
            ST = sb_in(p0, "ST", [P, 2, T])
            AP_ = sb_in(p0, "APAD", [P, 2, WSCAN])
            UP = sb_in(p0, "UPAD", [P, 2, WSCAN])
            HPD = sb_in(p0, "HPAD", [P, 2, WSCAN])
            YF = sb_in(p0, "YF", [P, 2, T])
            SQA = YF
        with ExitStack() as pl:
            sb_in(pl, "fill1", [P, 2, CX, T])
            XTK = sb_in(pl, "XTK", [P, len(TT), D_MODEL])
            VR = sb_in(pl, "VR", [P, 2, P])
            NR = sb_in(pl, "NR", [P, P])
            RSR = sb_in(pl, "RSR", [32, D_RNN])
            MSR = sb_in(pl, "MSR", [24, INNER])
        with ExitStack() as pj:
            fillj = sb_in(pj, "fillj", [P, 2, CX, T])
            PJ0 = sb_in(pj, "PJ0", [P, CX, T])
            PH0, PL0 = sb_in(pj, "PH0", [P, 2, T], F32R), sb_in(pj, "PL0", [P, 2, T], F32R)
        with ExitStack() as pk:
            PJ1 = sb_in(pk, "PJ1", [P, CX, T])
            PH1, PL1 = sb_in(pk, "PH1", [P, 2, T], F32R), sb_in(pk, "PL1", [P, 2, T], F32R)
        with ExitStack() as pv:
            XMV = sb_in(pv, "XMV", [P, CI, T], F32R)
        with ExitStack() as p2:
            XMC = sb_in(p2, "XMC", [P, 2 * CI, T])
            XM = XMC[:, 0:CI, :]
            XC = XMC[:, CI:2 * CI, :]
            with ExitStack() as p2a:
                sb_in(p2a, "fill2", [P, 2, CX, T])
                XMP = sb_in(p2a, "XMP", [P, 2, WPAD + 1])
                XCV = sb_in(p2a, "XCV", [P, 2, WPAD + 1])
                WGR = sb_in(p2a, "WGR", [P, 3 * CI, 4, 8])
                ET = sb_in(p2a, "ET", [P, 2 * CI, 36])
            with ExitStack() as p2r:
                WS3 = sb_in(p2r, "WS3", [HEADS, 2, 3 * GT])
                rowt = lambda n: sb_in(p2r, n, [HEADS, T])
                LI, FF, AB, LF, BC, AS, A1, WS, T1, RM, NEGM = map(
                    rowt, ("LI", "FF", "AB", "LF", "BC", "AS", "A1", "WS", "T1", "RM", "NEGM"))
            HT = sb_in(p2, "HT", [P, 4, T])
            QT = sb_in(p2, "QT", [P, 4, T])
            VTK = sb_in(p2, "VTK", [P, len(TT), HD])
            KW = sb_in(p2, "KW", [P, 4, HD])
            KTS = sb_in(p2, "KTS", [3 * GT, 2, HD])
            PP = sb_in(p2, "PP", [P, PPO[-1]])
            PSM = sb_in(p2, "PSM", [NS, NS])
            WBD = sb_in(p2, "WBD", [P, 3, 4, P])
            CS = sb_in(p2, "CS", [P, CSLOTS, 2, HD])
            KWM = sb_in(p2, "KWM", [3 * GT, 2, HD], F32R)
            IWB = sb_in(p2, "IWB", [P, NS])
            ER = sb_in(p2, "ER", [HEADS, T])
            MR = sb_in(p2, "MR", [HEADS, T])
            IWR = sb_in(p2, "IWR", [HEADS, NS])
            SELH = sb_in(p2, "SELH", [HEADS, P])
        EM, RD, MB, FV = ACC[:, 0, :], ACC[:, 1, :], SQ[:, 0, :], SQ[:, 1, :]
        STK = [t[:, 0:4 * 3 * GT].rearrange("p (c n) -> p c n", c=4) for t in (RD, FV)]

        ps = ctx.enter_context(nc.psum_tensor("ps", [P, 8, 512], F32))
        psv = ps[:, :, :].rearrange("p (s m h) n -> p s m h n", s=2, m=2)

        raw_loaded = [sem(f"raw_loaded{i}") for i in range(4)]
        hi_ready = sem("hi_ready")
        lo_ready = sem("lo_ready", RING)
        slab_used = sem("slab_used", 2 * RING)
        psum_freed = [sem("psum0_freed"), sem("psum1_freed")]
        misc_done = sem("misc_done", FIRST)
        x_loaded = sem("x_loaded")
        rows_loaded = sem("rows_loaded")
        const_ready = sem("const_ready")
        act_step, dve_step, pool_step = sem("act_step"), sem("dve_step"), sem("pool_step")
        x_ready = sem("x_ready")
        xn_hi = sem("xn_hi")
        xn_ready = sem("xn_ready")
        sq_ready = sem("sq_ready")
        acc_ready = sem("acc_ready")
        acc_clear = sem("acc_clear")
        std_ready = sem("std_ready")
        lam_e = sem("lam_e")
        vecs_ready = sem("vecs_ready")
        pads_ready, conv_done, xc_hi, xc_ready = sem("pads_ready"), sem("conv_done", FIRST), sem("xc_hi", FIRST), sem("xc_ready")
        tails_out, h_out = sem("tails_out", FIRST), sem("h_out", FIRST)
        gelu_done, s_ready, a_ready = sem("gelu_done"), sem("s_ready"), sem("a_ready")
        v_in, v_ready, scan_done = sem("v_in"), sem("v_ready"), sem("scan_done", FIRST)
        y_ready, y_hi, y_lo = sem("y_ready"), sem("y_hi"), sem("y_lo", FIRST)
        gate_in, silu_done = sem("gate_in"), sem("silu_done")
        p_loaded, pt_hi, pt_ready, pj_ready = sem("p_loaded"), sem("pt_hi"), sem("pt_ready"), sem("pj_ready")
        sig_done = sem("sig_done")
        out_rows, stored, y_stored = sem("out_rows"), sem("stored"), [sem("y_stored0"), sem("y_stored1")]
        wqkv_loaded, wgr_loaded, et_ready = sem("wqkv_loaded"), sem("wgr_loaded"), sem("et_ready")
        xm_copied, xc_silu = sem("xm_copied"), sem("xc_silu")
        f_ready, ln_ready, t1_ready, er_ready, iws_in = sem("f_ready"), sem("ln_ready"), sem("t1_ready"), sem("er_ready"), sem("iws_in")
        rows_ready, cols_ready = sem("rows_ready"), sem("cols_ready")
        ht_ready, wbd_ready, sel_ready = sem("ht_ready"), sem("wbd_ready"), sem("sel_ready")
        nq_ready, e_ready, exp_done, masked = sem("nq_ready"), sem("e_ready"), sem("exp_done"), sem("masked")
        kt4_done, kwm_ready, rd_in, n_done = sem("kt4_done"), sem("kwm_ready"), sem("rd_in"), sem("n_done")
        unit_done, unit_freed = sem("unit_done", 2 * FIRST), sem("unit_freed", 2 * FIRST)
        c_loaded = [sem(f"c_loaded{i}") for i in range(CSLOTS)]
        c_stored = [sem(f"c_stored{i}", 16 * FIRST) for i in range(CSLOTS)]
        sqh_ready, fv_ready, sd_ready, h_done = sem("sqh_ready"), sem("fv_ready"), sem("sd_ready"), sem("h_done", FIRST)
        states_out = sem("states_out")
        stack_ready, vs_hi, kwm_hi, qz_ready, numt_ready = sem("stack_ready"), sem("vs_hi"), sem("kwm_hi"), sem("qz_ready"), sem("numt_ready")

        G_MIX, G_FFN, C_RCW, C_RCB, C_BR, C_BI, C_LAM = 0, 16, 32, 80, 92, 104, 116
        C_MCW, C_MCB, C_MN, C_PB, C_NF = 0, 64, 80, 96, 112

        def pair4(t):
            return t.rearrange("p m (h n) -> p (m h) n", h=2)

        def pair5(t):
            return t.rearrange("p m (h n) -> p m h n", h=2)

        def psum4(s):
            return ps[:, 4 * s:4 * s + 4, 0:H2]

        RB = RSTD[:, :].rearrange("p (h n) -> p h n", h=2).unsqueeze(1).broadcast_to([P, 2, 2, H2])

        def padded(t, width, seg, lead, pre):
            return (t[:, :, pre:pre + SEQ],
                    t[:, :, pre + SEQ:pre + SEQ + DEC_B * seg].rearrange("p m (b t) -> p m b t", b=DEC_B)[:, :, :, lead:lead + DEC_S])

        def tight(t):
            return t[:, :, 0:SEQ], t[:, :, SEQ:T].rearrange("p m (b t) -> p m b t", b=DEC_B)

        block = ctx.enter_context(nc.Block())

        def w_slab(w, k, col):
            return w[k * 256:k * 256 + 256, col].rearrange("(k p) n -> p k n", p=P)

        @block.sync
        def _(sp):
            lo_t = Tally()
            phase = [0]
            waits_passed[id(sp)] = sem("sp_waits_passed")
            give_credit(sp, *c_stored)

            def slab(src):
                sp.wait_ge(lo_ready, lo_t.adv() - 4 + RING)
                stand_alone(sp)
                s = phase[0] % 4
                phase[0] += 1
                sp.dma_start(RAW[:, s], src).then_inc(raw_loaded[s], 16)

            for i, (t0, n) in enumerate(TT):
                src = I["x_prompt"][0, t0:t0 + n, :] if t0 < SEQ else I["x_sample"].rearrange("b t d -> (b t) d")
                sp.dma_start(XTK[0:n, i, :], src).then_inc(x_loaded, 16)
            rg_in, rg_wr, rg_wi, rg_out = I["rg_w_in"][0], I["rg_w_r"][0], I["rg_w_i"][0], I["rg_w_out"][0]
            with loop(sp, 3, {lo_t: 20}) as j:
                for jj in range(2):
                    b = 2 * j + jj
                    for k in range(4):
                        slab(w_slab(rg_in, k, ds(b * 256 + D_RNN, 256)))
                    for k in range(4):
                        slab(w_slab(rg_in, k, ds(b * 256, 256)))
                    for w in (rg_wr, rg_wi):
                        slab(w[ds(b, 1), :, :].rearrange("o (k p) n -> p (o k) n", p=P))
            with loop(sp, 2, {lo_t: 12}) as j:
                for m in range(2):
                    for k in range(6):
                        slab(w_slab(rg_out, k, ds(j * 512 + m * 256, 256)))

            def load_p(layer, dead_sem, dead):
                sp.wait_ge(dead_sem, dead)
                sp.dma_start(PTK[:, 0:4, :], I["p_prompt"][layer, 0].rearrange("(i p) d -> p i d", p=P)).then_inc(p_loaded, 16)
                sp.dma_start(PTK[0:NS, 4, :], I["p_sample"][layer].rearrange("b t d -> (b t) d")).then_inc(p_loaded, 16)

            def ffn(layer):
                up, down = I["ffn_w_up"][layer], I["ffn_w_down"][layer]
                for g0, gn in GROUPS:
                    with loop(sp, gn // 2, {lo_t: 8}) as j:
                        for off in (0, D_FF):
                            for k in range(4):
                                slab(w_slab(up, k, ds(j * 256 + off + g0 * P, 256)))
                    ks = gn // 2
                    with loop(sp, 1 if ks % 2 else 2, {lo_t: ks * (4 if ks % 2 else 2)}) as j:
                        for m in range(4 if ks % 2 else 2):
                            for k in range(ks):
                                slab(w_slab(down, g0 // 2 + k, ds(j * 512 + m * 256, 256)))

            def ple(layer):
                for m in range(4):
                    slab(w_slab(I["ple_w_proj"][layer], 0, slice(m * 256, m * 256 + 256)))
                with loop(sp, 2, {lo_t: 8}) as j:
                    for m in range(2):
                        for k in range(4):
                            slab(w_slab(I["ple_w_gate"][layer], k, ds(j * 512 + m * 256, 256)))

            load_p(0, y_lo, 6 + FIRST)
            ffn(0)
            ple(0)

            ml_in, ml_out = I["ml_w_in"][0], I["ml_w_out"][0]
            sp.wait_ge(misc_done, 9 + FIRST)
            with nc.allow_non_contiguous_dma(reason="small weights and gate vectors, once"):
                for i, name in enumerate(("ml_w_q", "ml_w_k", "ml_w_v")):
                    sp.dma_start(WQKV[:, i, 0:CI], I[name][0].rearrange("(c b) i o -> (b i) c o", c=CI)).then_inc(wqkv_loaded, 16)
                for i in range(4):
                    for m in range(3):
                        sp.dma_start(WGR[i:P:4, m * CI:m * CI + CI],
                                     I["ml_w_gates"][0, m * INNER:m * INNER + INNER].rearrange("(c b o) g -> b c (o g)", c=CI, o=4)
                                     .rearrange("b c (o g) -> b c o g", o=4)).then_inc(wgr_loaded, 16)
                sp.dma_start(M0T[:, :], I["state_mlstm_m"][0].rearrange("b h -> h b")).then_inc(wgr_loaded, 16)
                sp.dma_start(BG[:, :], I["ml_b_gates"][0].rearrange("(g h) -> h g", g=2)).then_inc(wgr_loaded, 16)
            with loop(sp, 4, {lo_t: 8}) as j:
                for m in range(2):
                    for k in range(4):
                        slab(w_slab(ml_in, k, ds(j * 512 + m * 256, 256)))

            def o_job(m):
                for k in range(4):
                    slab(w_slab(ml_in, k, slice(INNER + m * 256, INNER + m * 256 + 256)))

            o_job(0)
            freed = Tally()
            stored_t = [Tally(16) for _ in range(CSLOTS)]
            per_slot = UNITS // CSLOTS
            sp.wait_ge(rows_ready, 1)
            with loop(sp, HEADS, {freed: UNITS, **{t: per_slot for t in stored_t}}) as h:

                def load_c(v):
                    slot, (b, half) = v % CSLOTS, UNIT[v]
                    sp.wait_ge(c_stored[slot], stored_t[slot].adv() - 16 + 16 * FIRST)
                    stand_alone(sp)
                    if b is None:
                        sp.nop().then_inc(c_loaded[slot], 16)
                    else:
                        sp.dma_start(CS[:, slot], I["state_mlstm_C"][0, b, ds(h, 1), half * 256:half * 256 + 256, :]
                                     .rearrange("o (k p) v -> p (o k) v", p=P)).then_inc(c_loaded[slot], 16)

                for v in range(CSLOTS):
                    load_c(v)
                for v in range(UNITS):
                    slot, (b, half) = v % CSLOTS, UNIT[v]
                    sp.wait_ge(unit_freed, freed.adv() + 2 * FIRST)
                    stand_alone(sp)
                    dst = (O["ml_C_p"][0, 0] if b is None else O["ml_C_s"][0, b])[ds(h, 1), half * 256:half * 256 + 256, :]
                    sp.dma_start(dst.rearrange("o (k p) v -> p (o k) v", p=P), CS[:, slot]).then_inc(c_stored[slot], 16)
                    if CSLOTS <= v - 1 + CSLOTS < UNITS:
                        load_c(v - 1 + CSLOTS)
            sp.wait_ge(wbd_ready, HEADS + 1)
            load_p(1, h_done, HEADS + FIRST)
            for m in range(1, 4):
                o_job(m)
            for g in range(2):
                if g:
                    for m in range(4, 8):
                        o_job(m)
                with loop(sp, 2, {lo_t: 8}) as j:
                    for m in range(2):
                        for k in range(4):
                            slab(w_slab(ml_out, 4 * g + k, ds(j * 512 + m * 256, 256)))
            ffn(1)
            ple(1)
            sp.wait_ge(states_out, 4)
            for dst, src in ((O["rg_conv_s"].rearrange("l b t d -> (l b t) d"), SRO[0:24, :]),
                             (O["rg_h_s"].rearrange("l b d -> (l b) d"), SRO[24:32, :]),
                             (O["rg_conv_p"].rearrange("l b t d -> (l b t) d"), SRO[32:35, :]),
                             (O["rg_h_p"].rearrange("l b d -> (l b) d"), SRO[35:36, :]),
                             (O["ml_conv_s"].rearrange("l b t d -> (l b t) d"), SMO[0:24, :]),
                             (O["ml_conv_p"].rearrange("l b t d -> (l b t) d"), SMO[24:27, :]),
                             (O["ml_n_s"].rearrange("l b h (k p) -> (l b h k) p", p=P), NTO[:, 0, :]),
                             (O["ml_n_p"].rearrange("l b h (k p) -> (l b h k) p", p=P), NTO[0:16, 1, :])):
                sp.dma_start(dst, src).then_inc(stored, 16)
            with nc.allow_non_contiguous_dma(reason="m, 36 numbers"):
                sp.dma_start(O["ml_m_p"].rearrange("l b h -> h (l b)"), MO[:, 0:1]).then_inc(stored, 16)
                sp.dma_start(O["ml_m_s"].rearrange("l b h -> h (l b)"), MO[:, 1:1 + DEC_B]).then_inc(stored, 16)
            for i, (t0, n) in enumerate(TT):
                sp.wait_ge(out_rows, i + 1)
                dst = O["y_prompt"][0, t0:t0 + n, :] if t0 < SEQ else O["y_sample"].rearrange("b t d -> (b t) d")
                sp.dma_start(dst, YTK[0:n, i % 2, :]).then_inc(y_stored[i % 2], 16)
            sp.wait_ge(stored, 16 * 10)
            sp.wait_ge(y_stored[0], 16 * 3)
            sp.wait_ge(y_stored[1], 16 * 2)
            for slot in range(CSLOTS):
                sp.wait_ge(c_stored[slot], 16 * HEADS * per_slot + 16 * FIRST)

        @block.gpsimd
        def _(pool):
            slabs, step, conv_t, sq_t, misc = Tally(), Tally(), Tally(), Tally(), Tally()
            uses = [Tally(), Tally()]
            scans, ys = Tally(), Tally()
            phase = [0]

            def split_lo():
                n = slabs.adv()
                if isinstance(n, int) and n > TOTAL:
                    return
                pool.wait_ge(hi_ready, n)
                s = phase[0] % 4
                phase[0] += 1
                pool.tensor_tensor(WL[:, s], RAW[:, s], WH[:, s].bitcast(F32), ALU.subtract).then_inc(lo_ready, 1)

            def clear_acc():
                pool.memset(ACC[:, :, :], 0.0).then_inc(acc_clear, 1)

            def add_sq():
                pool.wait_ge(sq_ready, sq_t.adv())
                pool.tensor_tensor(ACC[:, :, :], ACC[:, :, :], SQ[:, :, :], ALU.add).then_inc(acc_ready, 1)

            waits_passed[id(pool)] = sem("pool_waits_passed")
            give_credit(pool, lo_ready, tails_out, h_out, y_lo)
            pool.memset(IDN[:, :], 0.0).then_inc(pool_step, 1)
            pool.wait_ge(pool_step, step.adv())
            pool.affine_select(out=IDN[:, :], in_=IDN[:, :], compare_op=ALU.not_equal, fill=1.0, base=0,
                               pattern=[[-1, P]], channel_multiplier=1)
            pool.memset(ONES[:, :], 1.0)
            pool.memset(XBP[:, :, 0:TAIL], 0.0)
            pool.memset(RGSI[:, CR:CR + 2, :], 0.0)
            pool.memset(WQKV[:, :, CI:CI + 4, :], 0.0)
            pool.memset(AP_[:, :, SEQ:WSCAN], 0.0)
            for t in (TRI, M64, BM3, BDM):
                pool.memset(t[:, :], 1.0)
            pool.memset(EPST[:, :], EPS).then_inc(const_ready, 1)
            pool.wait_ge(const_ready, 1)

            def keep(t, pattern, base, mult):
                pool.affine_select(out=t, in_=t, compare_op=ALU.is_ge, fill=0.0, base=base, pattern=pattern,
                                   channel_multiplier=mult).then_inc(pool_step, 1)
                pool.wait_ge(pool_step, step.adv())

            keep(TRI[:, :], [[1, P]], 0, -1)
            keep(M64[:, :], [[1, NS]], 0, -1)
            keep(M64[:, :].rearrange("p (b t) -> p b t", b=DEC_B), [[-DEC_S, DEC_B], [0, DEC_S]], 0, 1)
            for r in range(0, 3 * GT, GT):
                keep(BM3[r:r + GT, :], [[-DEC_S, 4]], 0, 1)
                keep(BM3[r:r + GT, :], [[DEC_S, 4]], DEC_S - 1, -1)
            keep(BDM[:, :], [[-4, 32]], 0, 1)
            keep(BDM[:, :], [[4, 32]], 3, -1)
            clear_acc()
            for k in range(4):
                split_lo()
            pool.wait_ge(acc_clear, 1)
            for m in range(4):
                add_sq()
            pool.wait_ge(vecs_ready, 1)

            def rg_pads(c0):
                pool.tensor_copy(
                    XBP[:, :, XB0:XB0 + DEC_B * SEG].rearrange("p m (b t) -> p m b t", b=DEC_B)[:, :, :, 0:TAIL],
                    RGSI[:, ds(c0, 2), 0:24].rearrange("p m (b t) -> p m b t", b=DEC_B)).then_inc(pads_ready, 1)

            rg_pads(0)
            for k in range(2):
                split_lo()
            with loop(pool, 3, {slabs: 20, uses[0]: 4, uses[1]: 4, conv_t: 2, scans: 2, ys: 2}) as j:
                for jj in range(2):
                    c0 = 4 * j + 2 * jj
                    u0 = uses[0].adv()
                    for k in range(3):
                        split_lo()
                    pool.wait_ge(conv_done, conv_t.adv() + FIRST)
                    pool.tensor_copy(
                        RGSO[:, ds(c0, 2), 0:24].rearrange("p m (b t) -> p m b t", b=DEC_B),
                        XBP[:, :, XB0:XB0 + DEC_B * SEG].rearrange("p m (b t) -> p m b t", b=DEC_B)[:, :, :, DEC_S:SEG])
                    pool.tensor_copy(RGSO[:, ds(c0, 2), 32:35], XBP[:, :, XB0 - TAIL:XB0]).then_inc(tails_out, 1)
                    rg_pads(c0 + 2)
                    for k in range(7):
                        split_lo()
                    uses[0].adv()
                    uses[1].adv(2)
                    pool.wait_ge(scan_done, scans.adv() + FIRST)
                    pool.tensor_copy(
                        RGSO[:, ds(c0, 2), 24:32],
                        HPD[:, :, SEQ:WSCAN].rearrange("p m (b t) -> p m b t", b=DEC_B)[:, :, :, DEC_S])
                    pool.tensor_copy(RGSO[:, ds(c0, 2), 35:36], HPD[:, :, SEQ - 1:SEQ]).then_inc(h_out, 1)
                    pool.wait_ge(y_hi, ys.adv())
                    pool.tensor_tensor(YL[:, ds(c0, 2), :], YF[:, :, :], YH[:, ds(c0, 2), :].bitcast(F32),
                                       ALU.subtract).then_inc(y_lo, 1)

            def next_norm():
                pool.wait_ge(misc_done, misc.adv() + FIRST)
                clear_acc()

            misc.adv(6)
            next_norm()
            pool.wait_ge(acc_clear, 2)
            for m in range(4):
                for k in range(6 if m else 4):
                    split_lo()
                add_sq()

            def ffn1():
                ffn(AH, AL)

            def g_lo(j, dst_h, dst_l, src):
                pool.tensor_tensor(dst_l[:, ds(j * 2, 2), :], src[:, :, :], dst_h[:, ds(j * 2, 2), :].bitcast(F32),
                                   ALU.subtract).then_inc(y_lo, 1)

            def ffn(gh=GH, gl=GL):
                for g, (g0, gn) in enumerate(GROUPS):
                    with loop(pool, gn // 2, {slabs: 8, ys: 1}) as j:
                        for k in range(8):
                            split_lo()
                        pool.wait_ge(y_hi, ys.adv())
                        g_lo(j, gh, gl, TU)
                    ks = gn // 2
                    n = 4 if ks % 2 else 2
                    with loop(pool, 4 // n, {slabs: ks * n}) as j:
                        for k in range(ks * n):
                            split_lo()

            def ple(clear, last):
                for k in range(4):
                    split_lo()
                misc.adv()
                next_norm()
                pool.wait_ge(acc_clear, clear)
                for j in (range(2) if last else (None,)):
                    if last:
                        body(j)
                    else:
                        with loop(pool, 2, {slabs: 8, sq_t: 2}) as j:
                            body(j)

            def body(j):
                for m in range(2):
                    for k in range(4):
                        split_lo()
                    add_sq()

            ffn()
            ple(3, False)
            pool.memset(XMP[:, :, 0:TAIL], 0.0)

            def link(ins):
                ins.then_inc(pool_step, 1)
                pool.wait_ge(pool_step, step.adv())

            def ml_in():
                with loop(pool, 2, {slabs: 8, conv_t: 2}) as j:
                    for m in range(2):
                        c0 = 4 * j + 2 * m + ml_c[0]
                        pool.wait_ge(conv_done, conv_t.adv() - 1 + FIRST)
                        pool.tensor_copy(
                            XMP[:, :, XB0:XB0 + DEC_B * SEG].rearrange("p m (b t) -> p m b t", b=DEC_B)[:, :, :, 0:TAIL],
                            MLSI[:, ds(c0, 2), :].rearrange("p m (b t) -> p m b t", b=DEC_B)).then_inc(pads_ready, 1)
                        for k in range(4):
                            split_lo()
                        pool.wait_ge(conv_done, conv_t.now() + FIRST)
                        pool.tensor_copy(
                            MLSO[:, ds(c0, 2), 0:24].rearrange("p m (b t) -> p m b t", b=DEC_B),
                            XMP[:, :, XB0:XB0 + DEC_B * SEG].rearrange("p m (b t) -> p m b t", b=DEC_B)[:, :, :, DEC_S:SEG])
                        pool.tensor_copy(MLSO[:, ds(c0, 2), 24:27], XMP[:, :, XB0 - TAIL:XB0]).then_inc(tails_out, 1)
                ml_c[0] += 8

            ml_c = [0]
            ml_in()
            pool.wait_ge(wqkv_loaded, 48)
            pool.wait_ge(wgr_loaded, 16 * 14)
            link(pool.tensor_scalar(WQKV[:, 1, 0:CI], WQKV[:, 1, 0:CI], float(HD) ** -0.5, None, ALU.mult))
            link(pool.memset(ET[:, :, :], 0.0))
            for i in range(3):
                g = WGR[:, i * CI:i * CI + CI]
                link(pool.tensor_tensor(g, g, WQKV[:, i, 0:CI].unsqueeze(3).broadcast_to([P, CI, 4, 8]), ALU.mult))
            link(pool.tensor_tensor(WGR[:, :, 0:2, :], WGR[:, :, 0:2, :], WGR[:, :, 2:4, :], ALU.add))
            link(pool.tensor_tensor(WGR[:, :, 0, :], WGR[:, :, 0, :], WGR[:, :, 1, :], ALU.add))
            for g in range(2):
                e = ET[:, :, 32 * g:32 * g + 4]
                w = WGR[:, :, 0, 4 * g:4 * g + 4]
                pool.tensor_tensor(e[:, 0:CI], w[:, 0:CI], w[:, CI:2 * CI], ALU.add)
                pool.tensor_copy(e[:, CI:2 * CI], w[:, 2 * CI:3 * CI]).then_inc(et_ready, 1)
            ml_in()

            def blocks(h):
                for i in range(3):
                    ins = pool.tensor_tensor(
                        WBD[:, i].rearrange("p c (b o) -> p c b o", o=4),
                        WQKV[:, i, ds(4 * h, 4), :].unsqueeze(2).broadcast_to([P, 4, 32, 4]),
                        BDM[:, :].unsqueeze(1).unsqueeze(3).broadcast_to([P, 4, 32, 4]), ALU.mult)
                ins.then_inc(wbd_ready, 1)

            heads, misc_h = Tally(), Tally()
            misc_h.adv(12)
            pool.wait_ge(misc_done, misc_h.now() + FIRST)
            blocks(0)
            with loop(pool, HEADS, {heads: 1, misc_h: 15, step: 1}) as h:
                n = heads.adv()
                pool.wait_ge(exp_done, n)
                for sbk in range(4):
                    pool.tensor_tensor(PP[:, PPO[sbk]:PPO[sbk] + P], PP[:, PPO[sbk]:PPO[sbk] + P], TRI[:, :], ALU.mult)
                pool.tensor_tensor(PSM[:, :], PSM[:, :], M64[:, :], ALU.mult).then_inc(masked, 1)
                pool.wait_ge(misc_done, misc_h.adv(10) + FIRST)
                stand_alone(pool)
                link(pool.memset(QT[:, :, 0:DEC_B * NS], 0.0))
                pool.wait_ge(nq_ready, n)
                pool.tensor_copy(QT[:, :, 0:T].rearrange("p k (b x) -> p k b x", b=DEC_B)[:, :, :, 0:DEC_S],
                                 XM[:, ds(4 * h + 3, 1), 0:4 * NS].rearrange("p o (k b t) -> p (o k) b t", k=4, b=DEC_B))\
                    .then_inc(qz_ready, 1)
                blocks(h + 1)
                misc_h.adv(5)

            def small_lo(j, dst_h, dst_l):
                pool.wait_ge(y_hi, ys.adv())
                pool.tensor_tensor(dst_l[:, ds(j, 2), :], TU[:, :, :], dst_h[:, ds(j, 2), :].bitcast(F32),
                                   ALU.subtract).then_inc(y_lo, 1)

            misc.adv(2 + 15 * HEADS + STATE_JOBS)
            next_norm_at = [None]
            for g in range(2):
                with loop(pool, 2, {slabs: 8, ys: 2}) as j:
                    for m in range(2):
                        for k in range(4):
                            split_lo()
                        small_lo(4 * j + 2 * m, AH, AL)
                if g:
                    next_norm()
                    pool.wait_ge(acc_clear, 4)
                with loop(pool, 2, {slabs: 8, **({sq_t: 2} if g else {})}) as j:
                    for m in range(2):
                        for k in range(4):
                            split_lo()
                        if g:
                            add_sq()
            ffn1()
            ple(5, True)

        @block.scalar
        def _(act):
            slabs, step, sq_t, misc, jobs = Tally(), Tally(), Tally(), Tally(), Tally()
            raw_t = [Tally(16) for _ in range(4)]
            uses = [Tally(), Tally()]
            xr, blk, conv_t = Tally(), Tally(), Tally()
            phase = [0]

            def link(ins):
                ins.then_inc(act_step, 1)
                act.wait_ge(act_step, step.adv())

            def split_hi():
                n = slabs.adv()
                if isinstance(n, int) and n > TOTAL:
                    return
                s = phase[0] % 4
                phase[0] += 1
                act.wait_ge(raw_loaded[s], raw_t[s].adv())
                stand_alone(act)
                act.wait_ge(slab_used, n - 4 + 2 * RING)
                stand_alone(act)
                act.activation(WH[:, s], RAW[:, s], ACT.Copy).then_inc(hi_ready, 1)

            def split_per(n):
                return {slabs: n, **{t: n // 4 for t in raw_t}}

            def prep(c0, gain, hi, norm=True):
                act.wait_ge(x_ready, xr.adv())
                stand_alone(act)
                for m in range(2):
                    if gain is None:
                        ins = act.activation(hi[:, ds(c0 + m, 1), :], X[:, ds(c0 + m, 1), :], ACT.Copy)
                    else:
                        ins = act.activation(hi[:, ds(c0 + m, 1), :], X[:, ds(c0 + m, 1), :], ACT.Copy,
                                             scale=V1[:, ds(gain + c0 + m, 1)])
                ins.then_inc(xn_hi, 1)
                if norm:
                    before = sq_t.adv() - 1
                    if not is_zero(before):
                        act.wait_ge(acc_ready, before)
                        stand_alone(act)
                    act.activation(SQ[:, :, :], X[:, ds(c0, 2), :], ACT.Square).then_inc(sq_ready, 1)

            def std(s):
                uses[s].adv()
                act.wait_ge(misc_done, misc.adv() + FIRST)
                act.activation(RSTD[:, :].rearrange("p (h n) -> p h n", h=2), ps[:, 4 * s:4 * s + 2, 0:H2], ACT.Sqrt,
                               bias=EPST[:, :], scale=1.0 / D_MODEL).then_inc(psum_freed[s], 1)

            def rows(t, i):
                t0, n = TT[i]
                return t[0:n, i, :]

            waits_passed[id(act)] = sem("act_waits_passed")
            give_credit(act, xc_hi)
            r = lambda name, pat, **k: I[name].rearrange(pat, **k)
            vec_rows = [
                (VR[0:16, 0, :], r("norm_mix", "l (c p) -> (l c) p", p=P)),
                (VR[16:32, 0, :], r("norm_ffn", "l (c p) -> (l c) p", p=P)),
                (VR[32:80, 0, :], r("rg_conv_w", "l w (c p) -> (l w c) p", p=P)),
                (VR[80:92, 0, :], r("rg_conv_b", "l (c p) -> (l c) p", p=P)),
                (VR[92:104, 0, :], r("rg_b_r", "l (c p) -> (l c) p", p=P)),
                (VR[104:116, 0, :], r("rg_b_i", "l (c p) -> (l c) p", p=P)),
                (VR[116:128, 0, :], r("rg_lambda", "l (c p) -> (l c) p", p=P)),
                (VR[0:64, 1, :], r("ml_conv_w", "l w (c p) -> (l w c) p", p=P)),
                (VR[64:80, 1, :], r("ml_conv_b", "l (c p) -> (l c) p", p=P)),
                (VR[80:96, 1, :], r("ml_norm", "l (c p) -> (l c) p", p=P)),
                (VR[96:112, 1, :], r("ple_b_gate", "l (c p) -> (l c) p", p=P)),
                (VR[112:120, 1, :], r("norm_final", "(c p) -> c p", p=P)),
                (NR[:, :], r("state_mlstm_n", "l b h (k p) -> (l b h k) p", p=P)),
                (RSR[0:24, :], r("state_rglru_conv", "l b t d -> (l b t) d")),
                (RSR[24:32, :], r("state_rglru_h", "l b d -> (l b) d")),
                (MSR[:, :], r("state_mlstm_conv", "l b t d -> (l b t) d")),
            ]
            for dst, src in vec_rows:
                act.dma_start(dst, src).then_inc(rows_loaded, 16)
            assert 16 * len(vec_rows) == ROWS_LOADED
            for k in range(4):
                split_hi()
            act.wait_ge(vecs_ready, 1)
            link(act.activation(SP8[:, 0, :], V1[:, C_LAM:C_LAM + CR], ACT.Abs))
            act.activation(SP8[:, 1, :], SP8[:, 0, :], ACT.Exp, scale=-1.0).then_inc(lam_e, 1)
            act.wait_ge(acc_clear, 1)
            misc.adv(6)
            uses[0].adv(3)
            uses[1].adv(3)
            for m in range(4):
                prep(2 * m, G_MIX, AH)
            std(1)
            split_hi()
            split_hi()
            with loop(act, 3, {**split_per(20), jobs: 20, uses[0]: 4, uses[1]: 4, blk: 2}) as j:
                for jj in range(2):
                    c0 = 4 * j + 2 * jj
                    for k in range(3):
                        split_hi()
                    jobs.adv(8)
                    b = blk.adv()
                    act.wait_ge(conv_done, b + FIRST)
                    stand_alone(act)
                    act.wait_ge(slab_used, jobs.now() - 8 + 2 * RING)
                    stand_alone(act)
                    (src_p, src_s), (dst_p, dst_s) = padded(XCP, WPAD, SEG, 0, 0), tight(XCH)
                    src_s = XCP[:, :, XB0:XB0 + DEC_B * SEG].rearrange("p m (b t) -> p m b t", b=DEC_B)[:, :, :, 0:DEC_S]
                    act.activation(dst_p, XCP[:, :, 0:SEQ], ACT.Copy)
                    act.activation(dst_s, src_s, ACT.Copy).then_inc(xc_hi, 1)
                    for k in range(3):
                        split_hi()
                    uses[0].adv()
                    act.wait_ge(psum_freed[1], uses[1].adv())
                    stand_alone(act)
                    act.activation(GEL[:, :, :], GEL[:, :, :], ACT.Gelu_apprx_tanh).then_inc(gelu_done, 1)
                    act.wait_ge(slab_used, jobs.adv() + 2 * RING)
                    stand_alone(act)
                    for m in range(2):
                        ins = act.activation(RT[:, m].rearrange("p (h n) -> p h n", h=2), psv[:, 0, m, :, 0:H2],
                                             ACT.Sigmoid, bias=V1[:, ds(C_BR + m + c0, 1)])
                    ins.then_inc(psum_freed[0], 1)
                    split_hi()
                    act.wait_ge(slab_used, jobs.adv() + 2 * RING)
                    stand_alone(act)
                    act.wait_ge(scan_done, b - 1 + FIRST)
                    stand_alone(act)
                    for m in range(2):
                        ins = act.activation(IT[:, m].rearrange("p (h n) -> p h n", h=2), psv[:, 1, m, :, 0:H2],
                                             ACT.Sigmoid, bias=V1[:, ds(C_BI + m + c0, 1)])
                    ins.then_inc(psum_freed[1], 1)
                    act.wait_ge(psum_freed[0], uses[0].adv())
                    stand_alone(act)
                    for m in range(2):
                        ins = act.activation(ST[:, m, :], RT[:, m, :], ACT.Tanh, scale=SP8[:, 0, ds(c0 + m, 1)])
                    ins.then_inc(s_ready, 1)
                    for m in range(2):
                        act.activation(AP_[:, m, 0:SEQ], RT[:, m, 0:SEQ], ACT.Exp, scale=SP8[:, 1, ds(c0 + m, 1)])
                        ins = act.activation(
                            AP_[:, m, SEQ:WSCAN].rearrange("p (b t) -> p b t", b=DEC_B)[:, :, 1:HSEG],
                            RT[:, m, SEQ:T].rearrange("p (b t) -> p b t", b=DEC_B), ACT.Exp,
                            scale=SP8[:, 1, ds(c0 + m, 1)])
                    ins.then_inc(a_ready, 1)
                    split_hi()
                    act.wait_ge(v_in, b)
                    stand_alone(act)
                    act.activation(ST[:, :, :], ST[:, :, :], ACT.Sqrt).then_inc(v_ready, 1)
                    uses[1].adv()
                    split_hi()
                    split_hi()
                    act.wait_ge(y_ready, b)
                    stand_alone(act)
                    act.activation(YH[:, ds(c0, 2), :], YF[:, :, :], ACT.Copy).then_inc(y_hi, 1)
            act.wait_ge(acc_clear, 2)
            for m in range(4):
                for k in range(6 if m else 4):
                    split_hi()
                jobs.adv(6)
                uses[m % 2].adv()
                prep(2 * m, G_FFN, AH)
            std(1)

            def ffn(last_out, gh):
                for g, (g0, gn) in enumerate(GROUPS):
                    with loop(act, gn // 2, {**split_per(8), jobs: 8, uses[0]: 1, uses[1]: 1, blk: 1}) as j:
                        for k in range(4):
                            split_hi()
                        b = blk.adv()
                        act.wait_ge(psum_freed[0], uses[0].adv())
                        stand_alone(act)
                        act.activation(TG[:, :, :], TG[:, :, :], ACT.Silu).then_inc(silu_done, 1)
                        for k in range(4):
                            split_hi()
                        jobs.adv(8)
                        uses[1].adv()
                        act.wait_ge(y_ready, b)
                        stand_alone(act)
                        act.activation(gh[:, ds(2 * j, 2), :], TU[:, :, :], ACT.Copy).then_inc(y_hi, 1)
                    ks = gn // 2
                    n = 4 if ks % 2 else 2
                    lastg = g == len(GROUPS) - 1
                    with loop(act, 4 // n, {**split_per(ks * n), jobs: ks * n, uses[0]: n // 2, uses[1]: n // 2,
                                            xr: n if lastg else 0}) as j:
                        for m in range(n):
                            for k in range(ks):
                                split_hi()
                            jobs.adv(ks)
                            uses[m % 2].adv()
                            if lastg:
                                prep(4 * j + 2 * m, None, last_out, norm=False)

            def ple(layer, PH, PJ, gain, dst, acc0):
                act.wait_ge(misc_done, misc.adv() + FIRST)
                act.activation(PH[:, :, 0:SEQ], ps[:, 0:4:2, 0:SEQ], ACT.Copy)
                act.activation(PH[:, :, SEQ:T], ps[:, 1:4:2, 0:NS], ACT.Copy).then_inc(pt_hi, 1)
                uses[0].adv()
                for m in range(4):
                    split_hi()
                    s = (m + 1) % 2
                    uses[s].adv()
                    act.wait_ge(slab_used, jobs.adv() + 2 * RING)
                    act.activation(pair4(PJ[:, 2 * m:2 * m + 2, :]), psum4(s), ACT.Copy).then_inc(psum_freed[s], 1)
                act.wait_ge(acc_clear, acc0)

                def body(j):
                    for m in range(2):
                        for k in range(4):
                            split_hi()
                        act.wait_ge(slab_used, jobs.adv(4) + 2 * RING)
                        stand_alone(act)
                        s = (m + 1) % 2
                        uses[s].adv()
                        act.wait_ge(x_ready, xr.now())
                        stand_alone(act)
                        for c in range(2):
                            ins = act.activation(TG[:, c].rearrange("p (h n) -> p h n", h=2), psv[:, s, c, :, 0:H2],
                                                 ACT.Sigmoid, bias=V2[:, ds(C_PB + 8 * layer + 2 * m + c + 4 * j, 1)])
                        ins.then_inc(psum_freed[s], 1)
                        if dst is None:
                            act.wait_ge(x_ready, xr.adv())
                            act.wait_ge(acc_ready, sq_t.adv() - 1)
                            act.activation(SQ[:, :, :], X[:, ds(4 * j + 2 * m, 2), :], ACT.Square).then_inc(sq_ready, 1)
                        else:
                            prep(4 * j + 2 * m, gain, dst)

                if layer:
                    for j in range(2):
                        body(j)
                else:
                    with loop(act, 2, {**split_per(8), jobs: 8, uses[0]: 1, uses[1]: 1, xr: 2, sq_t: 2}) as j:
                        body(j)
                std(1)

            ffn(AH, GH)
            ple(0, PH0, PJ0, G_MIX + 8, BH, 3)

            with loop(act, 4, {**split_per(8), jobs: 8, uses[0]: 1, uses[1]: 1, conv_t: 2}) as j:
                for m in range(2):
                    c0 = 4 * j + 2 * m
                    for k in range(4):
                        split_hi()
                    jobs.adv(4)
                    act.wait_ge(psum_freed[m], uses[m].adv())
                    stand_alone(act)
                    mp, ms = tight(XM[:, ds(c0, 2), :])
                    act.activation(mp, XMP[:, :, TAIL:XB0], ACT.Copy)
                    act.activation(ms, XMP[:, :, XB0:XB0 + DEC_B * SEG].rearrange("p m (b t) -> p m b t", b=DEC_B)[:, :, :, TAIL:SEG],
                                   ACT.Copy).then_inc(xm_copied, 1)
                    act.wait_ge(conv_done, 6 + conv_t.adv() + FIRST)
                    stand_alone(act)
                    cp, cs = tight(XC[:, ds(c0, 2), :])
                    act.activation(cp, XCV[:, :, 0:SEQ], ACT.Silu)
                    act.activation(cs, XCV[:, :, XB0:XB0 + DEC_B * SEG].rearrange("p m (b t) -> p m b t", b=DEC_B)[:, :, :, 0:DEC_S],
                                   ACT.Silu).then_inc(xc_silu, 1)
            misc.adv()
            uses[0].adv()
            act.wait_ge(f_ready, 1)
            link(act.activation(AB[:, :], FF[:, :], ACT.Abs))
            link(act.activation(AB[:, :], AB[:, :], ACT.Exp, scale=-1.0))
            act.activation(AB[:, :], AB[:, :], ACT.Ln, bias=1.0).then_inc(ln_ready, 1)
            act.wait_ge(t1_ready, 1)
            act.activation(ER[:, :], T1[:, :], ACT.Exp, scale=-1.0)
            act.activation(IWR[:, :], IWR[:, :], ACT.Exp)
            link(act.activation(WS[:, :], WS[:, :], ACT.Exp))
            for g in range(2):
                ins = act.activation(WS3[:, g, :].rearrange("p (r t) -> p r t", r=3), WS[:, SEQ + g * GT:SEQ + g * GT + GT]
                                     .unsqueeze(1).broadcast_to([HEADS, 3, GT]), ACT.Copy)
            ins.then_inc(rows_ready, 1)

            def stack(src):
                for g in range(2):
                    ins = act.activation(STK[g].rearrange("p c (r t) -> p c r t", r=3), src[:, :, SEQ + g * GT:SEQ + g * GT + GT]
                                         .unsqueeze(2).broadcast_to([P, 4, 3, GT]), ACT.Copy)
                ins.then_inc(stack_ready, 1)
            misc.adv()
            uses[1].adv()
            heads, units = Tally(), Tally()
            act.wait_ge(misc_done, misc.now() + FIRST)
            act.activation(HT[:, :, :], XMC[:, 0:4, :], ACT.Copy).then_inc(ht_ready, 1)
            with loop(act, HEADS, {misc: 15, uses[0]: 7, uses[1]: 6, heads: 1, units: UNITS}) as h:
                n = heads.adv()
                act.wait_ge(misc_done, misc.adv() + FIRST)
                stand_alone(act)
                act.activation(VTK[:, 0:4, :], ps[:, 0:4, :], ACT.Copy).then_inc(psum_freed[0], 1)
                uses[0].adv()
                act.wait_ge(misc_done, misc.adv() + FIRST)
                stand_alone(act)
                act.activation(VTK[0:NS, 4, :], ps[0:NS, 4, :], ACT.Copy)
                act.activation(MB[:, 0:SEQ], ps[:, 5, :], ACT.Copy)
                act.activation(EM[:, 0:SEQ], ps[:, 6, :], ACT.Copy)
                act.activation(MB[:, SEQ:T], ps[:, 7, 0:NS], ACT.Copy)
                act.activation(EM[:, SEQ:T], ps[:, 7, NS:2 * NS], ACT.Copy)
                act.activation(IWB[:, :], ps[:, 7, 2 * NS:3 * NS], ACT.Copy).then_inc(psum_freed[1], 1)
                uses[1].adv()
                for s in range(2):
                    act.wait_ge(misc_done, misc.adv() + FIRST)
                    stand_alone(act)
                    act.activation(pair4(QT[:, 2 * s:2 * s + 2, :]), psum4(s), ACT.Copy).then_inc(psum_freed[s], 1)
                    uses[s].adv()
                act.wait_ge(h_done, n - 1 + FIRST)
                stand_alone(act)
                stack(HT)
                act.wait_ge(misc_done, misc.adv() + FIRST)
                act.wait_ge(ht_ready, n)
                stand_alone(act)
                act.activation(XMV[0:3 * GT, ds(4 * h, 2), 0:HD], ps[0:3 * GT, 0:2, :], ACT.Copy).then_inc(vs_hi, 1)
                uses[0].adv()
                for s in (1, 0):
                    act.wait_ge(misc_done, misc.adv() + FIRST)
                    stand_alone(act)
                    act.activation(pair4(HT[:, 2 * s:2 * s + 2, :]), psum4(s), ACT.Copy).then_inc(psum_freed[s], 1)
                    uses[s].adv()
                act.wait_ge(psum_freed[1], uses[1].now())
                stand_alone(act)
                act.wait_ge(psum_freed[0], uses[0].now())
                stand_alone(act)
                stack(HT)
                act.wait_ge(e_ready, n)
                stand_alone(act)
                act.activation(PP[:, :], PP[:, :], ACT.Exp, scale=-1.0)
                act.activation(PSM[:, :], PSM[:, :], ACT.Exp, scale=-1.0).then_inc(exp_done, 1)
                act.wait_ge(misc_done, misc.adv() + FIRST)
                stand_alone(act)
                for i in range(4):
                    ins = act.activation(KW[:, i, :], ps[:, i, :], ACT.Copy, scale=COLS[:, i, ds(h + 4, 1)])
                ins.then_inc(psum_freed[0], 1)
                uses[0].adv()
                act.wait_ge(misc_done, misc.adv() + FIRST)
                stand_alone(act)
                act.activation(KTS[:, :, :], ps[0:3 * GT, 4:7:2, :], ACT.Copy).then_inc(kt4_done, 1)
                uses[1].adv()
                act.wait_ge(kt4_done, n)
                stand_alone(act)

                def kwm(b):
                    if b >= 2:
                        act.wait_ge(unit_done, units.now() + UNIT.index((b - 2, 1)) + 1 + 2 * FIRST)
                        stand_alone(act)
                    act.activation(KWM[:, b % 2, :], KTS[:, b // 4, :], ACT.Copy,
                                   scale=WM3[:, b // 4, ds(h, 1), b % 4]).then_inc(kwm_hi, 1)

                kwm(0)
                kwm(1)
                misc.adv()
                uses[0].adv()
                act.wait_ge(misc_done, misc.adv() + FIRST)
                stand_alone(act)
                act.activation(XC[:, ds(4 * h, 4), 0:SEQ], ps[:, 4:8, :], ACT.Copy).then_inc(psum_freed[1], 1)
                uses[1].adv()
                act.activation(HT[:, :, :], XMC[:, ds(4 * h + 4, 4), :], ACT.Copy).then_inc(ht_ready, 1)
                act.wait_ge(misc_done, misc.adv() + FIRST)
                stand_alone(act)
                act.activation(RD[:, 0:SEQ], ps[:, 0, :], ACT.Abs)
                act.activation(RD[:, SEQ:T], ps[:, 2, 0:NS], ACT.Abs).then_inc(rd_in, 1)
                for b in range(2, DEC_B):
                    kwm(b)
                    if b == 5:
                        act.wait_ge(unit_done, units.now() + PROMPT_UNITS[1] + 1 + 2 * FIRST)
                        stand_alone(act)
                        act.wait_ge(psum_freed[1], uses[1].now())
                        stand_alone(act)
                        act.activation(KW[:, :, :], XC[:, ds(4 * h, 4), 0:SEQ], ACT.Square)
                units.adv(UNITS)
                act.wait_ge(misc_done, misc.adv() + FIRST)
                stand_alone(act)
                act.activation(VTK[0:NS, 4, :], ps[0:NS, 1, :], ACT.Copy).then_inc(numt_ready, 1)
                act.wait_ge(misc_done, misc.adv() + FIRST)
                act.wait_ge(n_done, n)
                stand_alone(act)
                act.activation(XC[:, ds(4 * h, 4), SEQ:T], ps[:, 0, 0:4 * NS].rearrange("p (v t) -> p v t", v=4),
                               ACT.Copy).then_inc(psum_freed[0], 1)
                act.wait_ge(psum_freed[0], uses[0].adv())
                stand_alone(act)
                act.activation(XM[:, ds(4 * h, 4), SEQ:T], XC[:, ds(4 * h, 4), SEQ:T], ACT.Square).then_inc(sqh_ready, 1)
                misc.adv()
                uses[1].adv()
                act.wait_ge(fv_ready, n)
                stand_alone(act)
                act.activation(FV[:, :], FV[:, :], ACT.Sqrt, bias=EPST[:, :], scale=1.0 / HD).then_inc(sd_ready, 1)
            act.wait_ge(misc_done, misc.now() + FIRST)
            act.wait_ge(h_done, HEADS + FIRST)
            for m in range(4):
                for c in range(2 * m, 2 * m + 2):
                    ins = act.activation(BH[:, c, :], X[:, c, :], ACT.Copy, scale=V1[:, G_MIX + 8 + c:G_MIX + 9 + c])
                ins.then_inc(xn_hi, 1)
            for g in range(2):
                if g:
                    misc.adv(STATE_JOBS)
                    uses[0].adv(2)
                    uses[1].adv(2)
                with loop(act, 2, {**split_per(8), jobs: 8, uses[0]: 1, uses[1]: 1, blk: 2}) as j:
                    for m in range(2):
                        for k in range(4):
                            split_hi()
                        jobs.adv(4)
                        b = blk.adv()
                        act.wait_ge(psum_freed[m], uses[m].adv())
                        stand_alone(act)
                        act.activation(TG[:, :, :], TG[:, :, :], ACT.Sigmoid).then_inc(silu_done, 1)
                        act.wait_ge(y_ready, b)
                        stand_alone(act)
                        act.activation(AH[:, ds(4 * j + 2 * m, 2), :], TU[:, :, :], ACT.Copy).then_inc(y_hi, 1)
                if g:
                    act.wait_ge(acc_clear, 4)
                with loop(act, 2, {**split_per(8), jobs: 8, uses[0]: 1, uses[1]: 1,
                                   **({xr: 2, sq_t: 2} if g else {})}) as j:
                    for m in range(2):
                        for k in range(4):
                            split_hi()
                        jobs.adv(4)
                        uses[m].adv()
                        if g:
                            prep(4 * j + 2 * m, G_FFN + 8, BH)
            std(1)
            ffn(BH, AH)
            ple(1, PH1, PJ1, None, None, 5)

        @block.vector
        def _(dve):
            step, misc, jobs, hi_t, blk = Tally(), Tally(), Tally(), Tally(), Tally()
            uses = [Tally(), Tally()]
            ys = Tally()

            def link(ins):
                ins.then_inc(dve_step, 1)
                dve.wait_ge(dve_step, step.adv())

            def xn_lo(c0, gain, hi, lo):
                dve.wait_ge(xn_hi, hi_t.adv())
                if gain is None:
                    dve.tensor_tensor(lo[:, ds(c0, 2), :], X[:, ds(c0, 2), :], hi[:, ds(c0, 2), :].bitcast(F32),
                                      ALU.subtract).then_inc(xn_ready, 1)
                    return
                for m in range(2):
                    ins = dve.scalar_tensor_tensor(
                        lo[:, ds(c0 + m, 1), :], X[:, ds(c0 + m, 1), :], V1[:, ds(gain + c0 + m, 1)],
                        hi[:, ds(c0 + m, 1), :].bitcast(F32), ALU.mult, ALU.subtract)
                ins.then_inc(xn_ready, 1)

            def evac_padded(dst, s):
                R = RSTD[:, :]
                dve.tensor_tensor(dst[:, :, TAIL:TAIL + H2], psv[:, s, :, 0, 0:H2],
                                  R[:, 0:H2].unsqueeze(1).broadcast_to([P, 2, H2]), ALU.mult)
                dve.tensor_tensor(dst[:, :, TAIL + H2:XB0], psv[:, s, :, 1, 0:HP2],
                                  R[:, H2:SEQ].unsqueeze(1).broadcast_to([P, 2, HP2]), ALU.mult)
                dve.tensor_tensor(
                    dst[:, :, XB0:XB0 + DEC_B * SEG].rearrange("p m (b t) -> p m b t", b=DEC_B)[:, :, :, TAIL:SEG],
                    psv[:, s, :, 1, HP2:H2].rearrange("p m (b t) -> p m b t", b=DEC_B),
                    R[:, SEQ:T].rearrange("p (b t) -> p b t", b=DEC_B).unsqueeze(1).broadcast_to([P, 2, DEC_B, DEC_S]),
                    ALU.mult).then_inc(psum_freed[s], 1)

            def conv(src, dst, c0, V, cw, cb, per):
                for k in range(CONV_W):
                    for m in range(2):
                        o = dst[:, m, 0:WCONV]
                        wk = V[:, ds(cw + k * per + c0 + m, 1)]
                        if k == 0:
                            ins = dve.tensor_scalar(o, src[:, m, 0:WCONV], wk, V[:, ds(cb + c0 + m, 1)], ALU.mult, ALU.add)
                        else:
                            ins = dve.scalar_tensor_tensor(o, src[:, m, k:k + WCONV], wk, o, ALU.mult, ALU.add)
                    if k < CONV_W - 1:
                        link(ins)
                ins.then_inc(conv_done, 1)

            so = [0]
            cl = [Tally(16), Tally(16)]

            def rstd(s):
                dve.wait_ge(psum_freed[s], uses[s].adv())
                misc.adv()
                dve.reciprocal(RSTD[:, :], RSTD[:, :]).then_inc(std_ready, 1)

            stds = Tally()
            give_credit(dve, conv_done, scan_done, unit_freed, h_done)
            dve.wait_ge(misc_done, misc.adv() + FIRST)
            for dst, src in ((V1[:, :], ps[:, 4, 0:P]), (V2[:, 0:120], ps[:, 4, P:P + 120]),
                             (NT[:, :, :, :].rearrange("p b h k -> p (b h k)"), ps[:, 4, 256:384]),
                             (RGSI[:, 0:CR, :].rearrange("p c r -> p (c r)"), ps[:, 5, 0:CR * 32]),
                             (MLSI[:, :, :].rearrange("p c r -> p (c r)"), ps[:, 6, 0:CI * 24])):
                ins = dve.tensor_copy(dst, src)
                ins.then_inc(dve_step, 1)
                step.adv()
            uses[1].adv()
            dve.wait_ge(dve_step, step.now())
            dve.nop().then_inc(vecs_ready, 1)
            dve.nop().then_inc(psum_freed[1], 1)
            for i, (t0, n) in enumerate(TT):
                s = i % 2
                dve.wait_ge(misc_done, misc.adv() + FIRST)
                uses[s].adv()
                dve.tensor_copy(X[:, :, t0:t0 + n],
                                ps[:, 4 * s:4 * s + 2, :].rearrange("p b (c t) -> p (b c) t", t=P)[:, :, 0:n])\
                    .then_inc(psum_freed[s], 1)
            dve.wait_ge(psum_freed[0], 3)
            dve.wait_ge(psum_freed[1], 3)
            for m in range(4):
                dve.nop().then_inc(x_ready, 1)
            for m in range(4):
                xn_lo(2 * m, G_MIX, AH, AL)
            dve.wait_ge(lam_e, 1)
            e_, z, z2, p = SP8[:, 1, :], SQA[:, 0, 0:CR], SQA[:, 0, 16:16 + CR], SQA[:, 0, 32:32 + CR]
            link(dve.tensor_scalar(z2, e_, 2.0, None, ALU.add))
            link(dve.reciprocal(z2, z2))
            link(dve.tensor_tensor(z, e_, z2, ALU.mult))
            link(dve.tensor_tensor(z2, z, z, ALU.mult))
            link(dve.tensor_scalar(p, z2, 1.0 / 17, None, ALU.mult))
            for k in (15, 13, 11, 9, 7, 5, 3):
                link(dve.scalar_tensor_tensor(p, p, 1.0 / k, z2, ALU.add, ALU.mult))
            link(dve.scalar_tensor_tensor(p, p, 1.0, z, ALU.add, ALU.mult))
            link(dve.tensor_scalar(z, V1[:, C_LAM:C_LAM + CR], -1.0, 0.0, ALU.mult, ALU.max))
            link(dve.scalar_tensor_tensor(p, p, 2.0, z, ALU.mult, ALU.add))
            link(dve.tensor_scalar(SP8[:, 0, :], p, 8.0, None, ALU.mult))
            link(dve.tensor_scalar(SP8[:, 1, :], p, -8.0, None, ALU.mult))
            rstd(1)
            dve.wait_ge(std_ready, stds.adv())
            with loop(dve, 3, {jobs: 20, uses[0]: 4, uses[1]: 4, blk: 2, step: 2 * 10}) as j:
                for jj in range(2):
                    c0 = 4 * j + 2 * jj
                    b = blk.adv()
                    dve.wait_ge(slab_used, jobs.adv(4) + 2 * RING)
                    dve.wait_ge(tails_out, b - 1 + FIRST)
                    evac_padded(XBP, 0)
                    dve.wait_ge(psum_freed[0], uses[0].adv())
                    dve.wait_ge(pads_ready, b)
                    dve.wait_ge(xc_hi, b - 1 + FIRST)
                    conv(XBP, XCP, c0, V1, C_RCW, C_RCB, CR)
                    dve.wait_ge(xc_hi, b + FIRST)
                    src_s = XCP[:, :, XB0:XB0 + DEC_B * SEG].rearrange("p m (b t) -> p m b t", b=DEC_B)[:, :, :, 0:DEC_S]
                    hp, hs = tight(XCH)
                    lp, ls = tight(XCL)
                    dve.tensor_tensor(lp, XCP[:, :, 0:SEQ], hp.bitcast(F32), ALU.subtract)
                    dve.tensor_tensor(ls, src_s, hs.bitcast(F32), ALU.subtract).then_inc(xc_ready, 1)
                    dve.wait_ge(slab_used, jobs.adv(4) + 2 * RING)
                    dve.tensor_tensor(pair5(GEL[:, :, :]), psv[:, 1, :, :, 0:H2], RB, ALU.mult).then_inc(psum_freed[1], 1)
                    uses[1].adv()
                    jobs.adv(2)
                    uses[0].adv()
                    uses[1].adv()
                    dve.wait_ge(s_ready, b)
                    ip, is_ = tight(IT)
                    dve.tensor_tensor(ip, ip, XCP[:, :, 0:SEQ], ALU.mult)
                    link(dve.tensor_tensor(is_, is_, src_s, ALU.mult))
                    dve.wait_ge(a_ready, b)
                    dve.wait_ge(y_lo, b - 1 + FIRST)
                    sp_, ss_ = tight(SQA)
                    as_ = AP_[:, :, SEQ:WSCAN].rearrange("p m (b t) -> p m b t", b=DEC_B)[:, :, :, 1:HSEG]
                    dve.tensor_tensor(sp_, AP_[:, :, 0:SEQ], AP_[:, :, 0:SEQ], ALU.mult)
                    link(dve.tensor_tensor(ss_, as_, as_, ALU.mult))
                    flat = lambda t: t[:, :, :].rearrange("p m t -> p (m t)")
                    dve.scalar_tensor_tensor(flat(ST), flat(SQA), 1.0, flat(ST), ALU.add, ALU.mult).then_inc(v_in, 1)
                    up_p = UP[:, :, 0:SEQ]
                    up_s = UP[:, :, SEQ:WSCAN].rearrange("p m (b t) -> p m b t", b=DEC_B)
                    dve.tensor_copy(up_s[:, :, :, 0], RGSI[:, ds(c0, 2), 24:32])
                    dve.wait_ge(v_ready, b)
                    vp, vs = tight(ST)
                    dve.tensor_tensor(up_p, vp, ip, ALU.mult)
                    link(dve.tensor_tensor(up_s[:, :, :, 1:HSEG], vs, is_, ALU.mult))
                    dve.wait_ge(h_out, b - 1 + FIRST)
                    for m in range(2):
                        ins = dve.tensor_tensor_scan(HPD[:, m, :], AP_[:, m, :], UP[:, m, :], 0.0, ALU.mult, ALU.add)
                        if m == 0:
                            link(ins)
                    ins.then_inc(scan_done, 1)
                    dve.wait_ge(scan_done, b + FIRST)
                    dve.wait_ge(gelu_done, b)
                    dve.wait_ge(y_lo, b - 1 + FIRST)
                    gp, gs = tight(GEL)
                    yp, ys_ = tight(YF)
                    dve.tensor_tensor(yp, HPD[:, :, 0:SEQ], gp, ALU.mult)
                    dve.tensor_tensor(ys_, HPD[:, :, SEQ:WSCAN].rearrange("p m (b t) -> p m b t", b=DEC_B)[:, :, :, 1:HSEG],
                                      gs, ALU.mult).then_inc(y_ready, 1)
                    link(dve.nop())
                    link(dve.nop())
                    link(dve.nop())

            def add_to_x(n_slabs, s, c0, ready):
                dve.wait_ge(slab_used, jobs.adv(n_slabs) + 2 * RING)
                xx = pair4(X[:, ds(c0, 2), :])
                dve.tensor_tensor(xx, xx, psum4(s), ALU.add).then_inc(psum_freed[s], 1)
                u = uses[s].adv()
                if ready:
                    dve.wait_ge(psum_freed[s], u)
                    dve.nop().then_inc(x_ready, 1)

            with loop(dve, 2, {jobs: 12, uses[0]: 1, uses[1]: 1, hi_t: 2}) as j:
                for m in range(2):
                    add_to_x(6, m, 4 * j + 2 * m, True)
                    xn_lo(4 * j + 2 * m, G_FFN, AH, AL)
            rstd(1)
            dve.wait_ge(std_ready, stds.adv())

            def ffn(hi, lo):
                for g, (g0, gn) in enumerate(GROUPS):
                    with loop(dve, gn // 2, {jobs: 8, uses[0]: 1, uses[1]: 1, blk: 1, ys: 1, step: 1}) as j:
                        b = blk.adv()
                        y = ys.adv()
                        dve.wait_ge(slab_used, jobs.adv(4) + 2 * RING)
                        dve.tensor_tensor(pair5(TG[:, :, :]), psv[:, 0, :, :, 0:H2], RB, ALU.mult).then_inc(psum_freed[0], 1)
                        uses[0].adv()
                        dve.wait_ge(slab_used, jobs.adv(4) + 2 * RING)
                        dve.wait_ge(silu_done, y)
                        dve.wait_ge(y_lo, b - 1 + FIRST)
                        link(dve.tensor_tensor(pair5(TU[:, :, :]), psv[:, 1, :, :, 0:H2], pair5(TG[:, :, :]), ALU.mult))
                        dve.nop().then_inc(psum_freed[1], 1)
                        uses[1].adv()
                        dve.tensor_tensor(pair5(TU[:, :, :]), pair5(TU[:, :, :]), RB, ALU.mult).then_inc(y_ready, 1)
                    ks = gn // 2
                    n = 4 if ks % 2 else 2
                    last = g == len(GROUPS) - 1
                    with loop(dve, 4 // n, {jobs: ks * n, uses[0]: n // 2, uses[1]: n // 2, hi_t: n if last else 0}) as j:
                        for m in range(n):
                            add_to_x(ks, m % 2, 4 * j + 2 * m, last)
                            if last:
                                xn_lo(4 * j + 2 * m, None, hi, lo)

            def ple(layer, PH, PL, PJ, gain, hi, lo):
                dve.wait_ge(misc_done, misc.adv() + FIRST)
                dve.wait_ge(pt_hi, layer + 1)
                dve.tensor_tensor(PL[:, :, 0:SEQ], ps[:, 0:4:2, 0:SEQ], PH[:, :, 0:SEQ].bitcast(F32), ALU.subtract)
                link(dve.tensor_tensor(PL[:, :, SEQ:T], ps[:, 1:4:2, 0:NS], PH[:, :, SEQ:T].bitcast(F32), ALU.subtract))
                dve.nop().then_inc(pt_ready, 1)
                dve.nop().then_inc(psum_freed[0], 1)
                uses[0].adv()
                jobs.adv(4)
                uses[0].adv(2)
                uses[1].adv(2)
                with loop(dve, 2, {jobs: 8, uses[0]: 1, uses[1]: 1, hi_t: 0 if hi is None else 2, step: 2}) as j:
                    for m in range(2):
                        s = (m + 1) % 2
                        jobs.adv(4)
                        dve.wait_ge(psum_freed[s], uses[s].adv())
                        c0 = 4 * j + 2 * m
                        link(dve.tensor_tensor(TG[:, :, :], TG[:, :, :], PJ[:, ds(c0, 2), :], ALU.mult))
                        dve.tensor_tensor(X[:, ds(c0, 2), :], X[:, ds(c0, 2), :], TG[:, :, :], ALU.add).then_inc(x_ready, 1)
                        if hi is not None:
                            xn_lo(c0, gain, hi, lo)
                rstd(1)
                dve.wait_ge(std_ready, stds.adv())

            ffn(AH, AL)
            ple(0, PH0, PL0, PJ0, G_MIX + 8, BH, BL)
            ml = Tally()
            with loop(dve, 4, {jobs: 8, uses[0]: 1, uses[1]: 1, ml: 2, step: 6}) as j:
                for m in range(2):
                    c0 = 4 * j + 2 * m
                    n = ml.adv()
                    dve.wait_ge(slab_used, jobs.adv(4) + 2 * RING)
                    dve.wait_ge(tails_out, 6 + n - 1 + FIRST)
                    dve.wait_ge(xm_copied, n - 1)
                    evac_padded(XMP, m)
                    dve.wait_ge(psum_freed[m], uses[m].adv())
                    dve.wait_ge(pads_ready, 7 + n)
                    dve.wait_ge(xc_silu, n - 1)
                    conv(XMP, XCV, c0, V2, C_MCW, C_MCB, CI)
            dve.wait_ge(misc_done, misc.adv() + FIRST)
            pg = ps[:, 0:2, 0:H2]
            link(dve.memset(RM[:, :], 1.0))
            dve.memset(RM[:, 0:1], 0.0)
            dve.memset(RM[:, SEQ:T:DEC_S], 0.0)
            dve.wait_ge(wgr_loaded, 16 * 14)
            dve.tensor_scalar(LI[:, :].rearrange("p (h n) -> p h n", h=2), pg[0:4], BG[:, 0:1], None, ALU.add)
            dve.tensor_copy(FF[:, :].rearrange("p (h n) -> p h n", h=2), pg[32:36]).then_inc(psum_freed[0], 1)
            dve.wait_ge(psum_freed[0], uses[0].adv())
            dve.tensor_scalar(FF[:, :], FF[:, :], BG[:, 1:2], None, ALU.add).then_inc(f_ready, 1)
            dve.tensor_scalar(NEGM[:, :], RM[:, :], 1.0, -NEG, ALU.subtract, ALU.mult)
            dve.wait_ge(ln_ready, 1)
            link(dve.scalar_tensor_tensor(LF[:, :], FF[:, :], 0.0, AB[:, :], ALU.min, ALU.subtract))
            link(dve.tensor_tensor_scan(BC[:, :], RM[:, :], LF[:, :], 0.0, ALU.mult, ALU.add))
            link(dve.tensor_tensor(AS[:, :], LI[:, :], BC[:, :], ALU.subtract))
            link(dve.tensor_copy(A1[:, :], AS[:, :]))
            dve.tensor_scalar(A1[:, 0:1], AS[:, 0:1], 0.0, None, ALU.max)
            link(dve.tensor_tensor(A1[:, SEQ:T:DEC_S], AS[:, SEQ:T:DEC_S], M0T[:, :], ALU.max))
            link(dve.tensor_tensor_scan(MR[:, :], NEGM[:, :], A1[:, :], 0.0, ALU.add, ALU.max))
            link(dve.tensor_tensor(T1[:, :], BC[:, :], MR[:, :], ALU.add))
            dve.tensor_copy(MO[:, 0:1], T1[:, SEQ - 1:SEQ])
            dve.tensor_copy(MO[:, 1:1 + DEC_B], T1[:, SEQ + DEC_S - 1:T:DEC_S])
            b8 = lambda t: t.rearrange("p (b t) -> p b t", b=DEC_B)
            bc8 = lambda t: t.unsqueeze(2).broadcast_to([HEADS, DEC_B, DEC_S])
            dve.tensor_tensor(b8(IWR[:, :]), bc8(M0T[:, :]), b8(MR[:, SEQ:T]), ALU.subtract)
            dve.tensor_scalar(WS[:, 0:SEQ], AS[:, 0:SEQ], MR[:, SEQ - 1:SEQ], None, ALU.subtract)
            dve.tensor_tensor(b8(WS[:, SEQ:T]), b8(AS[:, SEQ:T]), bc8(MR[:, SEQ + DEC_S - 1:T:DEC_S]),
                              ALU.subtract).then_inc(t1_ready, 1)
            dve.wait_ge(misc_done, misc.adv() + FIRST)
            dve.tensor_copy(COLS[:, 0:4, :], ps[:, 4, 0:32].rearrange("p (i g) -> p i g", g=8))
            for g in range(2):
                dve.tensor_copy(WM3[:, g], ps[0:3 * GT, 4, 40 + 4 * g:44 + 4 * g].unsqueeze(2).broadcast_to([3 * GT, HEADS, 4]))
            dve.tensor_copy(COLS[0:NS, 4, :], ps[0:NS, 4, 32:40]).then_inc(psum_freed[1], 1)
            dve.wait_ge(psum_freed[1], uses[1].adv())
            for g in range(2):
                ins = dve.tensor_tensor(WM3[:, g], WM3[:, g], BM3[:, :].unsqueeze(1).broadcast_to([3 * GT, HEADS, 4]), ALU.mult)
            ins.then_inc(cols_ready, 1)
            dve.wait_ge(rows_ready, 1)
            dve.tensor_scalar(SELH[:, :], ONES[0:HEADS, :], IDN[0:HEADS, 0:1], None, ALU.mult).then_inc(sel_ready, 1)
            heads, units, kwms = Tally(), Tally(), Tally()
            with loop(dve, HEADS, {kwms: DEC_B, misc: 15, uses[0]: 7, uses[1]: 6, heads: 1, units: UNITS, step: 8, cl[0]: 3, cl[1]: 3}) as h:
                n = heads.adv()
                misc.adv(2)
                uses[0].adv(3)
                dve.wait_ge(psum_freed[1], uses[1].adv())
                for i in range(4):
                    dve.tensor_scalar(PP[:, PPO[i]:PPO[i + 1]], MB[:, i * P:SEQ], COLS[:, i, ds(h, 1)], 0.0,
                                      ALU.subtract, ALU.max)
                dve.tensor_scalar(PSM[:, :], MB[0:NS, SEQ:T], COLS[0:NS, 4, ds(h, 1)], 0.0,
                                  ALU.subtract, ALU.max).then_inc(e_ready, 1)
                dve.tensor_scalar(SELH[:, :], ONES[0:HEADS, :], IDN[0:HEADS, ds(h + 1, 1)], None, ALU.mult).then_inc(sel_ready, 1)
                dve.wait_ge(psum_freed[1], uses[1].adv())
                dve.wait_ge(psum_freed[0], uses[0].now() - 1)
                qi = XM[:, ds(4 * h + 3, 1), 0:4 * NS].rearrange("p o (k t) -> p (o k) t", k=4)
                nq = XM[:, ds(4 * h + 2, 1), 0:4 * NS].rearrange("p o (k b t) -> p (o k) b t", k=4, b=DEC_B)
                link(dve.tensor_tensor(qi, QT[:, :, SEQ:T], IWB[:, :].unsqueeze(1).broadcast_to([P, 4, NS]), ALU.mult))
                dve.tensor_tensor(nq, qi.rearrange("p k (b t) -> p k b t", b=DEC_B),
                                  NT[:, :, ds(h, 1), :].rearrange("p b o k -> p (o k) b").unsqueeze(3)
                                  .broadcast_to([P, 4, DEC_B, DEC_S]), ALU.mult).then_inc(nq_ready, 1)
                dve.wait_ge(vs_hi, n)
                vs = XMV[2 * GT:3 * GT, ds(4 * h, 2), 0:HD]
                dve.tensor_tensor(vs, ps[2 * GT:3 * GT, 0:2, :], vs.bitcast(F32), ALU.subtract).then_inc(psum_freed[0], 1)
                misc.adv(6)
                uses[0].adv(2)
                uses[1].adv()
                dve.wait_ge(misc_done, misc.adv() + FIRST)
                dve.wait_ge(masked, n)
                dve.wait_ge(kt4_done, n)
                dve.tensor_tensor(PSM[:, :], PSM[:, :], ps[0:NS, 5, 0:NS], ALU.mult).then_inc(psum_freed[1], 1)
                uses[1].adv()
                dve.wait_ge(misc_done, misc.adv() + FIRST)
                for i in range(4):
                    ins = dve.tensor_tensor(PP[:, PPO[i]:PPO[i + 1]], PP[:, PPO[i]:PPO[i + 1]],
                                            ps[:, i, i * P:SEQ], ALU.mult)
                ins.then_inc(psum_freed[0], 1)
                uses[0].adv()
                misc.adv()
                uses[1].adv()
                dve.wait_ge(misc_done, misc.adv() + FIRST)
                nt = NT[:, :, ds(h, 1), :].rearrange("p b o k -> p (o k) b")
                dve.tensor_copy(NP[:, ds(h, 1), :], ps[:, 3, 0:4].unsqueeze(1))
                link(dve.tensor_tensor(nt, nt, IWB[:, DEC_S - 1:NS:DEC_S].unsqueeze(1).broadcast_to([P, 4, DEC_B]), ALU.mult))
                dve.tensor_tensor(nt, nt, ps[:, 3, 8:40].rearrange("p (k b) -> p k b", k=4), ALU.add).then_inc(n_done, 1)
                def kwm_lo(b):
                    dve.wait_ge(kwm_hi, kwms.adv())
                    dve.scalar_tensor_tensor(KWM[GT:2 * GT, b % 2, :], KTS[GT:2 * GT, b // 4, :], WM3[GT:2 * GT, b // 4, ds(h, 1), b % 4],
                                             KWM[GT:2 * GT, b % 2, :].bitcast(F32), ALU.mult, ALU.subtract).then_inc(kwm_ready, 1)

                kwm_lo(0)
                kwm_lo(1)
                for v in range(UNITS):
                    dve.wait_ge(unit_done, units.adv() + 2 * FIRST)
                    bank = 4 + 2 * (v % 2)
                    c = CS[:, v % CSLOTS]
                    b, half = UNIT[v]
                    if b is None:
                        dve.wait_ge(c_loaded[v % CSLOTS], cl[half].adv(2))
                        cl[half].adv()
                        ins = dve.tensor_copy(c, ps[:, bank:bank + 2, :])
                    else:
                        cc = c.rearrange("p k v -> p (k v)")
                        ins = dve.scalar_tensor_tensor(cc, cc, IWB[:, DEC_S * b + DEC_S - 1:DEC_S * b + DEC_S],
                                                       ps[:, bank:bank + 2, :].rearrange("p k v -> p (k v)"), ALU.mult, ALU.add)
                    ins.then_inc(unit_freed, 1)
                    if b and not half and b + 1 < DEC_B:
                        kwm_lo(b + 1)
                    if v == PROMPT_UNITS[0] - 1:
                        dve.wait_ge(rd_in, n)
                        link(dve.tensor_tensor(RD, RD, EM, ALU.max))
                        link(dve.reciprocal(RD, RD))
                        dve.tensor_tensor(FV, RD, RD, ALU.mult)
                misc.adv(2)
                uses[0].adv()
                dve.wait_ge(misc_done, misc.adv() + FIRST)
                link(dve.tensor_tensor(FV[:, 0:SEQ], FV[:, 0:SEQ], ps[:, 4, :], ALU.mult))
                dve.tensor_tensor(FV[:, SEQ:T], FV[:, SEQ:T], ps[:, 5, 0:NS], ALU.mult).then_inc(psum_freed[1], 1)
                dve.wait_ge(psum_freed[1], uses[1].adv())
                link(dve.nop())
                dve.nop().then_inc(fv_ready, 1)
                dve.wait_ge(sd_ready, n)
                link(dve.reciprocal(FV, FV))
                link(dve.tensor_tensor(FV, FV, RD, ALU.mult))
                for c in range(4):
                    hh = XC[:, ds(4 * h + c, 1), :].rearrange("p o t -> p (o t)")
                    ins = dve.scalar_tensor_tensor(hh, hh, V2[:, ds(C_MN + c + 4 * h, 1)], FV, ALU.mult, ALU.mult)
                ins.then_inc(h_done, 1)
            for m in range(4):
                xn_lo(2 * m, G_MIX + 8, BH, BL)

            def states():
                for s, srcs in ((0, ((SRO[:, :].rearrange("p (b n) -> p b n", b=3), ps[0:36, 0:3, :]),)),
                                (1, ((SMO[:, :].rearrange("p (b n) -> p b n", b=4), ps[0:27, 4:8, :]),)),
                                (0, ((NTO[:, 0, :], ps[:, 0, 0:P]),)),
                                (1, ((NTO[0:16, 1, :], ps[0:16, 4, 0:P]),))):
                    dve.wait_ge(misc_done, misc.adv() + FIRST)
                    uses[s].adv()
                    for dst, src in srcs:
                        if s == 0:
                            for slot in range(CSLOTS):
                                dve.wait_ge(c_stored[slot], 16 * HEADS * UNITS // CSLOTS + 16 * FIRST)
                        dve.tensor_copy(dst, src).then_inc(states_out, 1)
                    dve.wait_ge(states_out, 1 + so[0])
                    so[0] += 1
                    dve.nop().then_inc(psum_freed[s], 1)

            for g in range(2):
                if g:
                    states()
                with loop(dve, 2, {jobs: 8, uses[0]: 1, uses[1]: 1, blk: 2, ys: 2}) as j:
                    for m in range(2):
                        b = blk.adv()
                        y = ys.adv()
                        dve.wait_ge(slab_used, jobs.adv(4) + 2 * RING)
                        dve.wait_ge(y_ready, b - 1)
                        dve.tensor_tensor(pair5(TG[:, :, :]), psv[:, m, :, :, 0:H2], RB, ALU.mult).then_inc(psum_freed[m], 1)
                        uses[m].adv()
                        dve.wait_ge(silu_done, y)
                        dve.wait_ge(y_lo, b - 1 + FIRST)
                        dve.tensor_tensor(TU[:, :, :], TG[:, :, :], XC[:, ds(8 * g + 4 * j + 2 * m, 2), :], ALU.mult)\
                            .then_inc(y_ready, 1)
                with loop(dve, 2, {jobs: 8, uses[0]: 1, uses[1]: 1, **({hi_t: 2} if g else {})}) as j:
                    for m in range(2):
                        add_to_x(4, m, 4 * j + 2 * m, bool(g))
                        if g:
                            xn_lo(4 * j + 2 * m, G_FFN + 8, BH, BL)
            rstd(1)
            dve.wait_ge(std_ready, stds.adv())
            ffn(BH, BL)
            ple(1, PH1, PL1, PJ1, None, None, None)
            for c in range(CX):
                dve.scalar_tensor_tensor(X[:, c, :], X[:, c, :], V2[:, C_NF + c:C_NF + c + 1], RSTD[:, :],
                                         ALU.mult, ALU.mult).then_inc(x_ready, 1)
            for i, (t0, n) in enumerate(TT):
                s = i % 2
                dve.wait_ge(misc_done, misc.adv() + FIRST)
                if i >= 2:
                    dve.wait_ge(y_stored[s], 16 * (i // 2))
                dve.tensor_copy(YTK[0:n, s, :].rearrange("p (b c) -> p b c", b=2), ps[0:n, 4 * s:4 * s + 2, :]).then_inc(out_rows, 1)
                dve.wait_ge(out_rows, i + 1)
                dve.nop().then_inc(psum_freed[s], 1)

        @block.tensor
        def _(pe):
            slabs, blk, xn, ys = Tally(), Tally(), Tally(), Tally()
            uses = [Tally(), Tally()]
            phase = [0]

            def use(s):
                before = uses[s].adv() - 1
                if not is_zero(before):
                    pe.wait_ge(psum_freed[s], before)

            def job(s, pairs, operand, before=None):
                use(s)
                for i in range(pairs):
                    if before:
                        before(i)
                    pe.wait_ge(lo_ready, slabs.adv() + RING)
                    w = phase[0] % 4
                    phase[0] += 1
                    for k in range(2):
                        hi, lo = operand(2 * i + k)
                        for m in range(2):
                            wc = slice(m * P, m * P + P)
                            for q, (a, x) in enumerate(((WH, hi), (WH, lo), (WL, hi))):
                                for h in range(2):
                                    ins = pe.matmul(ps[:, 4 * s + 2 * m + h, 0:H2], a[:, w, k, wc], x[:, h * H2:h * H2 + H2],
                                                    start=i == 0 and k == 0 and q == 0,
                                                    stop=i == pairs - 1 and k == 1 and q == 2)
                    ins.then_inc(slab_used, 1)

            def norm(s, acc):
                use(s)
                pe.wait_ge(acc_ready, acc)
                for h in range(2):
                    for k in range(2):
                        ins = pe.matmul(ps[:, 4 * s + h, 0:H2], ONES[:, :], ACC[:, k, h * H2:h * H2 + H2], start=k == 0, stop=k == 1)
                ins.then_inc(misc_done, 1)

            def chunks(hi, lo):
                return lambda k: (hi[:, k, :], lo[:, k, :])

            def starts(acc, xn0):
                def before(i):
                    if i == CX // 2 - 1:
                        norm(1, acc)
                    pe.wait_ge(xn_ready, xn0 + i + 1)
                return before


            give_credit(pe, slab_used, misc_done, unit_done)
            pe.wait_ge(const_ready, 1)
            pe.wait_ge(rows_loaded, ROWS_LOADED)
            use(1)
            pe.transpose(ps[:, 4, 0:P], VR[:, 0, :], IDN[:, :])
            pe.transpose(ps[:, 4, P:P + 120], VR[0:120, 1, :], IDN[0:120, 0:120])
            pe.transpose(ps[:, 4, 256:384], NR[:, :], IDN[:, :])
            for c in range(CR):
                pe.transpose(ps[:, 5, c * 32:c * 32 + 32], RSR[:, c * P:c * P + P], IDN[0:32, 0:32])
            for c in range(CI):
                ins = pe.transpose(ps[:, 6, c * 24:c * 24 + 24], MSR[:, c * P:c * P + P], IDN[0:24, 0:24])
            ins.then_inc(misc_done, 1)
            pe.wait_ge(x_loaded, 16 * len(TT))
            for i, (t0, n) in enumerate(TT):
                s = i % 2
                use(s)
                for c in range(CX):
                    ins = pe.transpose(ps[:, 4 * s + c // 4, (c % 4) * P:(c % 4) * P + n], XTK[0:n, i, c * P:c * P + P],
                                       IDN[0:n, 0:n])
                ins.then_inc(misc_done, 1)

            def rg_block(before=None):
                job(0, 4, chunks(AH, AL), before)
                job(1, 4, chunks(AH, AL))
                pe.wait_ge(xc_ready, blk.adv())
                job(0, 1, chunks(XCH, XCL))
                job(1, 1, chunks(XCH, XCL))

            rg_block(starts(4, 0))
            rg_block()
            with loop(pe, 2, {slabs: 20, uses[0]: 4, uses[1]: 4, blk: 2}) as j:
                for jj in range(2):
                    rg_block()
            with loop(pe, 2, {slabs: 12, uses[0]: 1, uses[1]: 1}) as j:
                for m in range(2):
                    job(m, 6, chunks(YH, YL), lambda i: pe.wait_ge(y_lo, i + 1 + FIRST))
            y_done = [6]

            def ffn(hi, lo, gh, gl, acc, xn0):
                for g, (g0, gn) in enumerate(GROUPS):
                    if g == 0:
                        job(0, 4, chunks(hi, lo), starts(acc, xn0))
                        job(1, 4, chunks(hi, lo))
                    with loop(pe, gn // 2 - (g == 0), {slabs: 8, uses[0]: 1, uses[1]: 1}) as j:
                        for s in range(2):
                            job(s, 4, chunks(hi, lo))
                    ks = gn // 2
                    n = 4 if ks % 2 else 2
                    with loop(pe, 4 // n, {slabs: ks * n, uses[0]: n // 2, uses[1]: n // 2}) as j:
                        for m in range(n):
                            job(m % 2, ks, chunks(gh, gl), lambda i: pe.wait_ge(y_lo, y_done[0] + i + 1 + FIRST))
                    y_done[0] += ks

            def ple(layer, PH, PL, hi, lo, acc, xn0):
                pe.wait_ge(p_loaded, 32 * (layer + 1))
                use(0)
                for c in range(2):
                    for i, (t0, n) in enumerate(TT):
                        dst = ps[:, 2 * c, t0:t0 + n] if t0 < SEQ else ps[:, 2 * c + 1, 0:n]
                        ins = pe.transpose(dst, PTK[0:n, i, c * P:c * P + P], IDN[0:n, 0:n])
                ins.then_inc(misc_done, 1)
                pe.wait_ge(pt_ready, layer + 1)
                for m in range(4):
                    job((m + 1) % 2, 1, chunks(PH, PL))
                with loop(pe, 2, {slabs: 8, uses[0]: 1, uses[1]: 1}) as j:
                    for m in range(2):
                        job((m + 1) % 2, 4, chunks(hi, lo), lambda i: pe.wait_ge(xn_ready, xn0 + i + 1))
                if layer:
                    norm(1, acc)

            ffn(AH, AL, GH, GL, 8, 4)
            ple(0, PH0, PL0, AH, AL, None, 8)
            job(0, 4, chunks(BH, BL), starts(12, 12))
            job(1, 4, chunks(BH, BL))
            with loop(pe, 3, {slabs: 8, uses[0]: 1, uses[1]: 1}) as j:
                for s in range(2):
                    job(s, 4, chunks(BH, BL))
            use(0)
            pe.wait_ge(et_ready, 2)
            pe.wait_ge(xm_copied, 8)
            order = [CI + c for c in range(CI)] + list(range(CI))
            for i, c in enumerate(order):
                if c < CI and c % 2 == 0:
                    pe.wait_ge(xc_silu, c // 2 + 1)
                for hf in range(2):
                    src = (XC if c < CI else XM)[:, c % CI, hf * H2:hf * H2 + H2]
                    ins = pe.matmul(ps[0:36, hf, 0:H2], ET[:, c, :], src, start=i == 0, stop=i == 2 * CI - 1)
            ins.then_inc(misc_done, 1)
            use(1)
            pe.wait_ge(rows_ready, 1)
            for i, (t0, n) in enumerate(TT):
                for k, t in enumerate((AS, WS)):
                    pe.transpose(ps[0:n, 4, i * 8 + 4 * k:i * 8 + 4 * k + 4], t[:, t0:t0 + n], IDN[0:4, 0:4])
            for g in range(2):
                ins = pe.transpose(ps[0:3 * GT, 4, 40 + 4 * g:44 + 4 * g], WS3[:, g, :], IDN[0:4, 0:4])
            ins.then_inc(misc_done, 1)
            pe.wait_ge(cols_ready, 1)
            heads, units, kws = Tally(), Tally(), Tally()
            cl = [Tally(16) for _ in range(CSLOTS)]
            with loop(pe, HEADS, {uses[0]: 7, uses[1]: 6, heads: 1, units: UNITS, kws: DEC_B,
                                  **{t: UNITS // CSLOTS for t in cl}}) as h:
                n = heads.adv()
                done = lambda ins: ins.then_inc(misc_done, 1)
                use(0)
                pe.wait_ge(ht_ready, n)
                pe.wait_ge(wbd_ready, n)

                def v_rows(i, bank):
                    t0, nt = TT[i]
                    for c in range(4):
                        ins = pe.matmul(ps[0:nt, bank, c * P:c * P + P], HT[:, c, t0:t0 + nt], WBD[:, 2, c, :],
                                        start=True, stop=True)
                    return ins

                for i in range(4):
                    ins = v_rows(i, i)
                done(ins)
                use(1)
                v_rows(4, 4)
                pe.wait_ge(sel_ready, n)
                pe.matmul(ps[:, 5, :], SELH[:, :], MR[:, 0:SEQ], start=True, stop=True)
                pe.matmul(ps[:, 6, :], SELH[:, :], ER[:, 0:SEQ], start=True, stop=True)
                for k, t in enumerate((MR[:, SEQ:T], ER[:, SEQ:T], IWR[:, :])):
                    ins = pe.matmul(ps[:, 7, k * NS:k * NS + NS], SELH[:, :], t, start=True, stop=True)
                done(ins)
                def project(i, order):
                    for s in order:
                        use(s)
                        for m in range(2):
                            c = 2 * s + m
                            for hf in range(2):
                                ins = pe.matmul(ps[:, 4 * s + 2 * m + hf, 0:H2], WBD[:, i, c, :],
                                                XC[:, ds(4 * h + c, 1), hf * H2:hf * H2 + H2].rearrange("p o t -> p (o t)"),
                                                start=True, stop=True)
                        done(ins)

                project(0, (0, 1))
                use(0)
                pe.wait_ge(stack_ready, 2 * n - 1)
                for g in range(2):
                    for c in range(4):
                        ins = pe.matmul(ps[0:3 * GT, g, c * P:c * P + P], STK[g][:, c, :], WBD[:, 2, c, :],
                                        start=True, stop=True)
                done(ins)
                project(1, (1, 0))
                pe.wait_ge(psum_freed[1], uses[1].now())
                use(0)

                def k_rows(i, bank):
                    t0, nt = TT[i]
                    for c in range(4):
                        ins = pe.transpose(ps[0:nt, bank, c * P:c * P + P], HT[:, c, t0:t0 + nt], IDN[:, :])
                    return ins

                for i in range(4):
                    ins = k_rows(i, i)
                done(ins)
                use(1)
                pe.wait_ge(stack_ready, 2 * n)
                for c in range(4):
                    pe.matmul(ps[0:NS, 5, 0:NS], HT[:, c, SEQ:T], QT[:, c, SEQ:T], start=c == 0, stop=c == 3)
                for g in range(2):
                    for c in range(4):
                        ins = pe.transpose(ps[0:3 * GT, 4 + 2 * g, c * P:c * P + P], STK[g][:, c, :], IDN[:, :])
                done(ins)
                use(0)
                for i in range(4):
                    for c in range(4):
                        ins = pe.matmul(ps[:, i, i * P:SEQ], HT[:, c, i * P:i * P + P], QT[:, c, i * P:SEQ],
                                        start=c == 0, stop=c == 3)
                done(ins)
                use(1)
                pe.wait_ge(psum_freed[0], uses[0].now())
                for vb in range(4):
                    for i in range(4):
                        ins = pe.matmul(ps[:, 4 + vb, i * P:SEQ], VTK[:, i, vb * P:vb * P + P], PP[:, PPO[i]:PPO[i + 1]],
                                        start=i == 0, stop=i == 3)
                done(ins)
                use(0)
                for i in range(4):
                    pe.matmul(ps[:, 0, i * P:SEQ], ONES[:, :], PP[:, PPO[i]:PPO[i + 1]], start=i == 0, stop=i == 3)
                pe.wait_ge(nq_ready, n)
                pe.matmul(ps[:, 2, 0:NS], ONES[0:NS, :], PSM[:, :], start=True, stop=False)
                for c in range(4):
                    pe.matmul(ps[:, 2, 0:NS], ONES[:, :],
                              XM[:, ds(4 * h + 2, 1), c * NS:c * NS + NS].rearrange("p o t -> p (o t)"), start=False, stop=c == 3)
                for kb in range(4):
                    for i in range(4):
                        pe.matmul(ps[:, 3, kb:kb + 1], KW[:, i, kb * P:kb * P + P], ONES[:, 0:1], start=i == 0, stop=i == 3)
                pe.wait_ge(kt4_done, n)
                for kb in range(4):
                    for g in range(2):
                        pe.matmul(ps[:, 3, 8 + 8 * kb + 4 * g:12 + 8 * kb + 4 * g], KTS[0:GT, g, kb * P:kb * P + P],
                                  WM3[0:GT, g, ds(h, 1), :].rearrange("p o b -> p (o b)"), start=True, stop=True)
                done(pe.matmul(ps[0:NS, 1, :], PSM[:, :], VTK[0:NS, 4, :], start=True, stop=False))
                pe.wait_ge(psum_freed[1], uses[1].now())
                for v in range(UNITS):
                    u = units.adv()
                    bank, slot = 4 + 2 * (v % 2), v % CSLOTS
                    pe.wait_ge(unit_freed, u - 2 + 2 * FIRST)
                    cl[slot].adv()
                    b, half = UNIT[v]
                    if b is None:
                        for kb in range(2):
                            for i in range(4):
                                kc = 2 * half + kb
                                ins = pe.matmul(ps[:, bank + kb, :], KW[:, i, kc * P:kc * P + P], VTK[:, i, :],
                                                start=i == 0, stop=i == 3)
                    else:
                        pe.wait_ge(c_loaded[slot], cl[slot].now())
                        if v == 0:
                            pe.wait_ge(qz_ready, n)
                        for kb in range(2):
                            ins = pe.matmul(ps[0:NS, 1, :], QT[:, 2 * half + kb, b * NS:b * NS + NS], CS[:, slot, kb, :],
                                            start=False, stop=v == UNITS - 1 and kb == 1)
                        if v == UNITS - 1:
                            done(ins)
                        if not half:
                            pe.wait_ge(kwm_ready, kws.adv())
                        for kb in range(2):
                            kc = 2 * half + kb
                            ins = pe.matmul(ps[:, bank + kb, :], KWM[:, b % 2, kc * P:kc * P + P],
                                            XMV[0:3 * GT, ds(4 * h + b // 4, 1), 0:HD].rearrange("p o v -> p (o v)"),
                                            start=True, stop=True)
                    ins.then_inc(unit_done, 1)
                pe.wait_ge(numt_ready, n)
                for c in range(4):
                    ins = pe.matmul(ps[:, 0, c * NS:c * NS + NS], VTK[0:NS, 4, c * P:c * P + P], IDN[0:NS, 0:NS], start=True, stop=True)
                done(ins)
                use(1)
                pe.wait_ge(unit_freed, units.now() + 2 * FIRST)
                for c in range(4):
                    pe.matmul(ps[:, 4, :], ONES[:, :], KW[:, c, :], start=c == 0, stop=c == 3)
                pe.wait_ge(sqh_ready, n)
                for c in range(4):
                    ins = pe.matmul(ps[:, 5, 0:NS], ONES[:, :], XM[:, ds(4 * h + c, 1), SEQ:T].rearrange("p o t -> p (o t)"),
                                    start=c == 0, stop=c == 3)
                done(ins)
            def states():
                use(0)
                for c in range(CR):
                    ins = pe.transpose(ps[0:36, c // 4, (c % 4) * P:(c % 4) * P + P], RGSO[:, c, :], IDN[:, :])
                ins.then_inc(misc_done, 1)
                use(1)
                for c in range(CI):
                    ins = pe.transpose(ps[0:27, 4 + c // 4, (c % 4) * P:(c % 4) * P + P], MLSO[:, c, :], IDN[:, :])
                ins.then_inc(misc_done, 1)
                use(0)
                pe.wait_ge(n_done, HEADS)
                pe.transpose(ps[:, 0, 0:P], NT[:, :, :, :].rearrange("p b h k -> p (b h k)"), IDN[:, :]).then_inc(misc_done, 1)
                use(1)
                pe.transpose(ps[0:16, 4, 0:P], NP[:, :, :].rearrange("p h k -> p (h k)"), IDN[:, :]).then_inc(misc_done, 1)

            y0 = y_done[0]
            for g in range(2):
                if g:
                    states()
                with loop(pe, 2, {slabs: 8, uses[0]: 1, uses[1]: 1}) as j:
                    for s in range(2):
                        job(s, 4, chunks(BH, BL), lambda i: pe.wait_ge(xn_ready, 16 + i + 1))
                with loop(pe, 2, {slabs: 8, uses[0]: 1, uses[1]: 1}) as j:
                    for s in range(2):
                        job(s, 4, chunks(AH, AL), lambda i: pe.wait_ge(y_lo, y0 + 4 * g + i + 1 + FIRST))
            y_done[0] += 8
            ffn(BH, BL, AH, AL, 16, 20)
            ple(1, PH1, PL1, BH, BL, 20, 24)
            pe.wait_ge(x_ready, X_READY)
            for i, (t0, n) in enumerate(TT):
                s = i % 2
                use(s)
                for c in range(CX):
                    ins = pe.transpose(ps[0:n, 4 * s + c // 4, (c % 4) * P:(c % 4) * P + P], X[:, c, t0:t0 + n], IDN[:, :])
                ins.then_inc(misc_done, 1)


ROWS_LOADED = 16 * 16
STATE_JOBS = 4
X_READY = 36

_OUTS = [("y_prompt", (1, 512, 1024)), ("y_sample", (8, 8, 1024)),
         ("rg_conv_p", (1, 1, 3, 1536)), ("rg_h_p", (1, 1, 1536)), ("ml_conv_p", (1, 1, 3, 2048)),
         ("ml_C_p", (1, 1, 4, 512, 512)), ("ml_n_p", (1, 1, 4, 512)), ("ml_m_p", (1, 1, 4)),
         ("rg_conv_s", (1, 8, 3, 1536)), ("rg_h_s", (1, 8, 1536)), ("ml_conv_s", (1, 8, 3, 2048)),
         ("ml_C_s", (1, 8, 4, 512, 512)), ("ml_n_s", (1, 8, 4, 512)), ("ml_m_s", (1, 8, 4))]


def kernel(**inputs):
    import numpy as _np
    import concourse.bacc as _bacc
    from concourse import mybir as _mybir
    from concourse.bass_utils import run_bass_kernel_spmd as _run

    nc = _bacc.Bacc("TRN2", target_bir_lowering=False, num_devices=1, dynamic_dma_scratch_size=1024)
    arrays, ins, outs = {}, {}, {}
    for name in inputs:
        a = _np.ascontiguousarray(inputs[name])
        arrays[f"in_{name}_dram"] = a
        ins[name] = nc.dram_tensor(f"in_{name}_dram", a.shape, _mybir.dt.from_np(a.dtype), kind="ExternalInput").ap()
    for name, shape in _OUTS:
        outs[name] = nc.dram_tensor(f"out_{name}_dram", shape, _mybir.dt.float32, kind="ExternalOutput").ap()
    hybrid_trunk(nc, ins, outs)
    r = _run(nc, [arrays], core_ids=[0])
    return tuple(r.results[0][f"out_{name}_dram"] for name, _ in _OUTS)
```

```python
from contextlib import ExitStack, contextmanager

import concourse.bass as bass
from concourse import mybir

F32 = mybir.dt.float32
F32R = mybir.dt.float32r
ALU = mybir.AluOpType
ACT = mybir.ActivationFunctionType
ds = bass.ds

P = 128
D_MODEL, SEQ, DEC_B, DEC_S = 1024, 512, 8, 8
N_STOK = DEC_B * DEC_S
GROUP_T = N_STOK // 2
T = SEQ + N_STOK
HALF_T = T // 2
HALF_TP = SEQ - HALF_T
D_RNN, INNER, D_FF, PLE = 1536, 2048, 2816, 256
CONV_W, TAIL = 4, 3
HEADS, HD = 4, 512
CX, CR, CI, CF = D_MODEL // P, D_RNN // P, INNER // P, D_FF // P
GROUPS = [(0, 8), (8, 8), (16, 6)]
EPS = 1e-6
SEG = TAIL + DEC_S
XB0 = TAIL + SEQ
WPAD = XB0 + DEC_B * SEG
WCONV = WPAD - TAIL
HSEG = 1 + DEC_S
WSCAN = SEQ + DEC_B * HSEG
NEG = -1.0e30
TOTAL = 484
RING = 4
FIRST = 1
UNITS = 2 + 2 * DEC_B
CSLOTS = 6
PROMPT_UNITS = (8, 9)
UNIT = [(None, v - PROMPT_UNITS[0]) if v in PROMPT_UNITS else divmod(v if v < PROMPT_UNITS[0] else v - 2, 2)
        for v in range(UNITS)]
ROWS_LOADED = 16 * 16
STATE_JOBS = 4
X_PAIRS_DONE = 6 * CX // 2
PROBS_AT = [0, 512, 896, 1152, 1280]
TOKEN_TILES = [(i * P, min(P, T - i * P)) for i in range(-(-T // P))]


class Tally:
    looped = None

    def __init__(self, step=1):
        self.step, self.at, self.k, self.j, self.per = step, 0, 0, None, 0

    def adv(self, n=1):
        if self.j is None:
            assert Tally.looped is None, "a tally that the loop doesn't know"
            self.at += n
        else:
            self.k += n
        return self.now()

    def now(self):
        if self.j is None or not self.per:
            return (self.at + self.k) * self.step
        return self.j * (self.per * self.step) + (self.at + self.k) * self.step


def is_zero(count):
    return isinstance(count, int) and count == 0


@contextmanager
def loop(eng, n, per):
    with eng.Fori(0, n) as j:
        Tally.looped = per
        for t, p in per.items():
            t.j, t.per, t.k = j, p, 0
        yield j
        for t, p in per.items():
            assert t.k == p, (t.k, p)
            t.j, t.k, t.at = None, 0, t.at + p * n
        Tally.looped = None


def hybrid_trunk(nc, I, O):
    ctx = ExitStack()
    with ctx:
        def sb_in(stack, name, shape, dt=F32):
            return stack.enter_context(nc.sbuf_tensor(name, shape, dt))

        def sb(name, shape, dt=F32):
            return sb_in(ctx, name, shape, dt)

        credits = {}

        def sem(name, credit=0):
            s = ctx.enter_context(nc.semaphore(name))
            credits[id(s)] = credit
            return s

        waits_passed = {}

        def give_credit(eng, *sems):
            for s in sems:
                eng.nop().then_inc(s, credits[id(s)])

        def stand_alone(eng):
            if Tally.looped is not None:
                eng.sem_inc(waits_passed[id(eng)])

        X = sb("X", [P, CX, T])
        W_RAW = sb("W_RAW", [P, 4, 2, 256])
        W_HI = sb("W_HI", [P, 4, 2, 256], F32R)
        W_LO = sb("W_LO", [P, 4, 2, 256], F32R)
        RSTD = sb("RSTD", [P, T])
        SQUARE_SUM = sb("SQUARE_SUM", [P, 2, T])
        SQUARES = sb("SQUARES", [P, 2, T])
        IDENT = sb("IDENT", [P, P])
        ONES = sb("ONES", [P, P])
        VECS1 = sb("VECS1", [P, P])
        VECS2 = sb("VECS2", [P, P])
        LAM8 = sb("LAM8", [P, 2, CR])
        EPS_COL = sb("EPS_COL", [P, 1])
        RSTD_COLS = sb("RSTD_COLS", [P, 8])
        RG_STATE_IN = sb("RG_STATE_IN", [P, CR + 2, 32])
        RG_STATE_OUT = sb("RG_STATE_OUT", [P, CR, 36])
        ML_CONV_IN = sb("ML_CONV_IN", [P, CI, 24])
        ML_CONV_OUT = sb("ML_CONV_OUT", [P, CI, 27])
        N_SAMPLES = sb("N_SAMPLES", [P, DEC_B, HEADS, 4])
        N_PROMPT = sb("N_PROMPT", [P, HEADS, 4])
        QKV_BLOCKS = sb("QKV_BLOCKS", [P, 3, CI + 4, 4])
        CAUSAL = sb("CAUSAL", [P, P])
        CAUSAL_S = sb("CAUSAL_S", [N_STOK, N_STOK])
        SAMPLE_MASK = sb("SAMPLE_MASK", [3 * GROUP_T, 4])
        BLOCK_MASK = sb("BLOCK_MASK", [P, 32])
        M_OLD = sb("M_OLD", [HEADS, DEC_B])
        GATE_BIAS = sb("GATE_BIAS", [HEADS, 2])
        M_OUT = sb("M_OUT", [HEADS, 1 + DEC_B])
        KEY_COLS = sb("KEY_COLS", [P, len(TOKEN_TILES), 8])
        KEY_WEIGHTS = sb("KEY_WEIGHTS", [3 * GROUP_T, 2, HEADS, 4])

        kb36 = [P, CX, T]
        with ExitStack() as p1:
            A_HI, A_LO = sb_in(p1, "A_HI", kb36, F32R), sb_in(p1, "A_LO", kb36, F32R)
            G_HI, G_LO = sb_in(p1, "G_HI", kb36, F32R), sb_in(p1, "G_LO", kb36, F32R)
            B_HI, B_LO = sb_in(p1, "B_HI", kb36, F32R), sb_in(p1, "B_LO", kb36, F32R)
            GATE = sb_in(p1, "GATE", [P, 2, T])
            GATED = sb_in(p1, "GATED", [P, 2, T])
            P_ROWS = sb_in(p1, "P_ROWS", [P, len(TOKEN_TILES), PLE])
            Y_ROWS = sb_in(p1, "Y_ROWS", [P, 2, D_MODEL])
            RG_ROWS = sb_in(p1, "RG_ROWS", [36, D_RNN])
            ML_ROWS = sb_in(p1, "ML_ROWS", [27, INNER])
            N_ROWS = sb_in(p1, "N_ROWS", [P, 2, P])
        with ExitStack() as p0:
            sb_in(p0, "fill0", [P, 2, CX, T])
            Y_HI, Y_LO = sb_in(p0, "Y_HI", [P, CR, T], F32R), sb_in(p0, "Y_LO", [P, CR, T], F32R)
            XB_PAD = sb_in(p0, "XB_PAD", [P, 2, WPAD + 1])
            XC_PAD = sb_in(p0, "XC_PAD", [P, 2, WPAD + 1])
            XC_HI, XC_LO = sb_in(p0, "XC_HI", [P, 2, T], F32R), sb_in(p0, "XC_LO", [P, 2, T], F32R)
            GELU_T = sb_in(p0, "GELU_T", [P, 2, T])
            R_GATE = sb_in(p0, "R_GATE", [P, 2, T])
            I_GATE = sb_in(p0, "I_GATE", [P, 2, T])
            TANH_T = sb_in(p0, "TANH_T", [P, 2, T])
            A_PAD = sb_in(p0, "A_PAD", [P, 2, WSCAN])
            U_PAD = sb_in(p0, "U_PAD", [P, 2, WSCAN])
            H_PAD = sb_in(p0, "H_PAD", [P, 2, WSCAN])
            Y_F32 = sb_in(p0, "Y_F32", [P, 2, T])
            A_SQUARE = Y_F32
        with ExitStack() as pl:
            sb_in(pl, "fill1", [P, 2, CX, T])
            X_ROWS = sb_in(pl, "X_ROWS", [P, len(TOKEN_TILES), D_MODEL])
            VEC_ROWS = sb_in(pl, "VEC_ROWS", [P, 2, P])
            N_IN_ROWS = sb_in(pl, "N_IN_ROWS", [P, P])
            RG_IN_ROWS = sb_in(pl, "RG_IN_ROWS", [32, D_RNN])
            ML_IN_ROWS = sb_in(pl, "ML_IN_ROWS", [24, INNER])
        with ExitStack() as pj:
            sb_in(pj, "fillj", [P, 2, CX, T])
            P_PROJ0 = sb_in(pj, "P_PROJ0", [P, CX, T])
            P_HI0, P_LO0 = sb_in(pj, "P_HI0", [P, 2, T], F32R), sb_in(pj, "P_LO0", [P, 2, T], F32R)
        with ExitStack() as pf:
            sb_in(pf, "fillf", [P, 2, CX, T])
            X_GAIN = sb_in(pf, "X_GAIN", [P, CX, T])
        with ExitStack() as pk:
            P_PROJ1 = sb_in(pk, "P_PROJ1", [P, CX, T])
            P_HI1, P_LO1 = sb_in(pk, "P_HI1", [P, 2, T], F32R), sb_in(pk, "P_LO1", [P, 2, T], F32R)
        with ExitStack() as pv:
            V_STACK = sb_in(pv, "V_STACK", [P, CI, T], F32R)
        with ExitStack() as p2:
            XM_XC = sb_in(p2, "XM_XC", [P, 2 * CI, T])
            XM = XM_XC[:, 0:CI, :]
            XC = XM_XC[:, CI:2 * CI, :]
            with ExitStack() as p2a:
                sb_in(p2a, "fill2", [P, 2, CX, T])
                XM_PAD = sb_in(p2a, "XM_PAD", [P, 2, WPAD + 1])
                CONV_OUT = sb_in(p2a, "CONV_OUT", [P, 2, WPAD + 1])
                GATE_W = sb_in(p2a, "GATE_W", [P, 3 * CI, 4, 8])
                GATE_FOLD = sb_in(p2a, "GATE_FOLD", [P, 2 * CI, 36])
            with ExitStack() as p2r:
                KEY_W_STACK = sb_in(p2r, "KEY_W_STACK", [HEADS, 2, 3 * GROUP_T])
                rowt = lambda n: sb_in(p2r, n, [HEADS, T])
                I_ROW, F_ROW, ABS_F, LOG_F, B_SUM, A_ROW, A_START, KEY_W_ROW, M_ROW, RUN_MASK, RUN_NEG = map(
                    rowt, ("I_ROW", "F_ROW", "ABS_F", "LOG_F", "B_SUM", "A_ROW", "A_START", "KEY_W_ROW", "M_ROW", "RUN_MASK", "RUN_NEG"))
            HEAD_T = sb_in(p2, "HEAD_T", [P, 4, T])
            Q_T = sb_in(p2, "Q_T", [P, 4, T])
            V_ROWS = sb_in(p2, "V_ROWS", [P, len(TOKEN_TILES), HD])
            K_WEIGHTED = sb_in(p2, "K_WEIGHTED", [P, 4, HD])
            K_STACK = sb_in(p2, "K_STACK", [3 * GROUP_T, 2, HD])
            PROBS = sb_in(p2, "PROBS", [P, PROBS_AT[-1]])
            PROBS_S = sb_in(p2, "PROBS_S", [N_STOK, N_STOK])
            QKV_DIAG = sb_in(p2, "QKV_DIAG", [P, 3, 4, P])
            C_HALVES = sb_in(p2, "C_HALVES", [P, CSLOTS, 2, HD])
            KW_STACK = sb_in(p2, "KW_STACK", [3 * GROUP_T, 2, HD], F32R)
            OLD_W = sb_in(p2, "OLD_W", [P, N_STOK])
            EXP_ROW = sb_in(p2, "EXP_ROW", [HEADS, T])
            MAX_ROW = sb_in(p2, "MAX_ROW", [HEADS, T])
            OLD_W_ROW = sb_in(p2, "OLD_W_ROW", [HEADS, N_STOK])
            HEAD_SEL = sb_in(p2, "HEAD_SEL", [HEADS, P])
        EXP_NEG_M, DEN, MAX_B, SCALE_F = SQUARE_SUM[:, 0, :], SQUARE_SUM[:, 1, :], SQUARES[:, 0, :], SQUARES[:, 1, :]
        X_STACK = [t[:, 0:4 * 3 * GROUP_T].rearrange("p (c n) -> p c n", c=4) for t in (DEN, SCALE_F)]

        ps = ctx.enter_context(nc.psum_tensor("ps", [P, 8, 512], F32))
        psv = ps[:, :, :].rearrange("p (s m h) n -> p s m h n", s=2, m=2)

        raw_loaded = [sem(f"raw_loaded{i}") for i in range(4)]
        hi_ready = sem("hi_ready")
        lo_ready = sem("lo_ready", RING)
        slab_used = sem("slab_used", 2 * RING)
        psum_freed = [sem("psum0_freed"), sem("psum1_freed")]
        misc_done = sem("misc_done", FIRST)
        x_loaded = [sem(f"x_loaded{i}") for i in range(len(TOKEN_TILES))]
        rows_loaded = sem("rows_loaded")
        const_ready = sem("const_ready")
        act_step, dve_step, pool_step = sem("act_step"), sem("dve_step"), sem("pool_step")
        x_ready = sem("x_ready")
        xn_hi = sem("xn_hi")
        xn_ready = sem("xn_ready")
        sq_ready = sem("sq_ready")
        acc_ready = sem("acc_ready")
        acc_clear = sem("acc_clear")
        std_ready = sem("std_ready")
        lam_e = sem("lam_e")
        vecs_ready = sem("vecs_ready")
        pads_ready, conv_done, xc_hi, xc_ready = sem("pads_ready"), sem("conv_done", FIRST), sem("xc_hi", FIRST), sem("xc_ready")
        tails_out, h_out = sem("tails_out", FIRST), sem("h_out", FIRST)
        gelu_done, s_ready, a_ready = sem("gelu_done"), sem("s_ready"), sem("a_ready")
        v_in, v_ready, scan_done = sem("v_in"), sem("v_ready"), sem("scan_done", FIRST)
        y_ready, y_hi, y_lo = sem("y_ready"), sem("y_hi"), sem("y_lo", FIRST)
        silu_done = sem("silu_done")
        p_loaded, pt_hi, pt_ready = sem("p_loaded"), sem("pt_hi"), sem("pt_ready")
        out_rows, stored, y_stored = sem("out_rows"), sem("stored"), [sem("y_stored0"), sem("y_stored1")]
        wqkv_loaded, wgr_loaded, et_ready = sem("wqkv_loaded"), sem("wgr_loaded"), sem("et_ready")
        xm_copied, xc_silu = sem("xm_copied"), sem("xc_silu")
        f_ready, ln_ready, t1_ready, er_ready, iws_in = sem("f_ready"), sem("ln_ready"), sem("t1_ready"), sem("er_ready"), sem("iws_in")
        rows_ready, cols_ready = sem("rows_ready"), sem("cols_ready")
        ht_ready, wbd_ready, sel_ready = sem("ht_ready"), sem("wbd_ready"), sem("sel_ready")
        nq_ready, e_ready, exp_done, masked = sem("nq_ready"), sem("e_ready"), sem("exp_done"), sem("masked")
        kt4_done, kwm_ready, rd_in, n_done = sem("kt4_done"), sem("kwm_ready"), sem("rd_in"), sem("n_done")
        unit_done, unit_freed = sem("unit_done", 2 * FIRST), sem("unit_freed", 2 * FIRST)
        c_loaded = [sem(f"c_loaded{i}") for i in range(CSLOTS)]
        c_stored = [sem(f"c_stored{i}", 16 * FIRST) for i in range(CSLOTS)]
        sqh_ready, fv_ready, sd_ready, h_done = sem("sqh_ready"), sem("fv_ready"), sem("sd_ready"), sem("h_done", FIRST)
        states_out, xf_ready = sem("states_out"), sem("xf_ready")
        stack_ready, vs_hi, kwm_hi, qz_ready, numt_ready = sem("stack_ready"), sem("vs_hi"), sem("kwm_hi"), sem("qz_ready"), sem("numt_ready")

        G_MIX, G_FFN, C_RCW, C_RCB, C_BR, C_BI, C_LAM = 0, 16, 32, 80, 92, 104, 116
        C_MCW, C_MCB, C_MN, C_PB, C_NF = 0, 64, 80, 96, 112

        def pair4(t):
            return t.rearrange("p m (h n) -> p (m h) n", h=2)

        def pair5(t):
            return t.rearrange("p m (h n) -> p m h n", h=2)

        def psum4(s):
            return ps[:, 4 * s:4 * s + 4, 0:HALF_T]

        RB = RSTD[:, :].rearrange("p (h n) -> p h n", h=2).unsqueeze(1).broadcast_to([P, 2, 2, HALF_T])

        def padded(t, width, seg, lead, pre):
            return (t[:, :, pre:pre + SEQ],
                    t[:, :, pre + SEQ:pre + SEQ + DEC_B * seg].rearrange("p m (b t) -> p m b t", b=DEC_B)[:, :, :, lead:lead + DEC_S])

        def tight(t):
            return t[:, :, 0:SEQ], t[:, :, SEQ:T].rearrange("p m (b t) -> p m b t", b=DEC_B)

        block = ctx.enter_context(nc.Block())

        def w_slab(w, k, col):
            return w[k * 256:k * 256 + 256, col].rearrange("(k p) n -> p k n", p=P)

        @block.sync
        def _(sp):
            lo_t = Tally()
            phase = [0]
            waits_passed[id(sp)] = sem("sp_waits_passed")
            give_credit(sp, *c_stored)

            def slab(src):
                sp.wait_ge(lo_ready, lo_t.adv() - 4 + RING)
                stand_alone(sp)
                s = phase[0] % 4
                phase[0] += 1
                sp.dma_start(W_RAW[:, s], src).then_inc(raw_loaded[s], 16)

            for i, (t0, n) in enumerate(TOKEN_TILES):
                src = I["x_prompt"][0, t0:t0 + n, :] if t0 < SEQ else I["x_sample"].rearrange("b t d -> (b t) d")
                sp.dma_start(X_ROWS[0:n, i, :], src).then_inc(x_loaded[i], 16)
            rg_in, rg_wr, rg_wi, rg_out = I["rg_w_in"][0], I["rg_w_r"][0], I["rg_w_i"][0], I["rg_w_out"][0]
            with loop(sp, 3, {lo_t: 20}) as j:
                for jj in range(2):
                    b = 2 * j + jj
                    for k in range(4):
                        slab(w_slab(rg_in, k, ds(b * 256 + D_RNN, 256)))
                    for k in range(4):
                        slab(w_slab(rg_in, k, ds(b * 256, 256)))
                    for w in (rg_wr, rg_wi):
                        slab(w[ds(b, 1), :, :].rearrange("o (k p) n -> p (o k) n", p=P))
            with loop(sp, 2, {lo_t: 12}) as j:
                for m in range(2):
                    for k in range(6):
                        slab(w_slab(rg_out, k, ds(j * 512 + m * 256, 256)))

            def load_p(layer, dead_sem, dead):
                sp.wait_ge(dead_sem, dead)
                sp.dma_start(P_ROWS[:, 0:4, :], I["p_prompt"][layer, 0].rearrange("(i p) d -> p i d", p=P)).then_inc(p_loaded, 16)
                sp.dma_start(P_ROWS[0:N_STOK, 4, :], I["p_sample"][layer].rearrange("b t d -> (b t) d")).then_inc(p_loaded, 16)

            def ffn(layer):
                up, down = I["ffn_w_up"][layer], I["ffn_w_down"][layer]
                for g0, gn in GROUPS:
                    with loop(sp, gn // 2, {lo_t: 8}) as j:
                        for off in (0, D_FF):
                            for k in range(4):
                                slab(w_slab(up, k, ds(j * 256 + off + g0 * P, 256)))
                    ks = gn // 2
                    with loop(sp, 1 if ks % 2 else 2, {lo_t: ks * (4 if ks % 2 else 2)}) as j:
                        for m in range(4 if ks % 2 else 2):
                            for k in range(ks):
                                slab(w_slab(down, g0 // 2 + k, ds(j * 512 + m * 256, 256)))

            def ple(layer):
                for m in range(4):
                    slab(w_slab(I["ple_w_proj"][layer], 0, slice(m * 256, m * 256 + 256)))
                with loop(sp, 2, {lo_t: 8}) as j:
                    for m in range(2):
                        for k in range(4):
                            slab(w_slab(I["ple_w_gate"][layer], k, ds(j * 512 + m * 256, 256)))

            load_p(0, y_lo, 6 + FIRST)
            ffn(0)
            ple(0)

            ml_in, ml_out = I["ml_w_in"][0], I["ml_w_out"][0]
            sp.wait_ge(misc_done, 9 + FIRST)
            with nc.allow_non_contiguous_dma(reason="small weights and gate vectors, once"):
                for i, name in enumerate(("ml_w_q", "ml_w_k", "ml_w_v")):
                    sp.dma_start(QKV_BLOCKS[:, i, 0:CI], I[name][0].rearrange("(c b) i o -> (b i) c o", c=CI)).then_inc(wqkv_loaded, 16)
                for i in range(4):
                    for m in range(3):
                        sp.dma_start(GATE_W[i:P:4, m * CI:m * CI + CI],
                                     I["ml_w_gates"][0, m * INNER:m * INNER + INNER].rearrange("(c b o) g -> b c (o g)", c=CI, o=4)
                                     .rearrange("b c (o g) -> b c o g", o=4)).then_inc(wgr_loaded, 16)
                sp.dma_start(M_OLD[:, :], I["state_mlstm_m"][0].rearrange("b h -> h b")).then_inc(wgr_loaded, 16)
                sp.dma_start(GATE_BIAS[:, :], I["ml_b_gates"][0].rearrange("(g h) -> h g", g=2)).then_inc(wgr_loaded, 16)
            with loop(sp, 4, {lo_t: 8}) as j:
                for m in range(2):
                    for k in range(4):
                        slab(w_slab(ml_in, k, ds(j * 512 + m * 256, 256)))

            def o_job(m):
                for k in range(4):
                    slab(w_slab(ml_in, k, slice(INNER + m * 256, INNER + m * 256 + 256)))

            o_job(0)
            freed = Tally()
            stored_t = [Tally(16) for _ in range(CSLOTS)]
            per_slot = UNITS // CSLOTS
            sp.wait_ge(rows_ready, 1)
            with loop(sp, HEADS, {freed: UNITS, **{t: per_slot for t in stored_t}}) as h:

                def load_c(v):
                    slot, (b, half) = v % CSLOTS, UNIT[v]
                    sp.wait_ge(c_stored[slot], stored_t[slot].adv() - 16 + 16 * FIRST)
                    stand_alone(sp)
                    if b is None:
                        sp.nop().then_inc(c_loaded[slot], 16)
                    else:
                        sp.dma_start(C_HALVES[:, slot], I["state_mlstm_C"][0, b, ds(h, 1), half * 256:half * 256 + 256, :]
                                     .rearrange("o (k p) v -> p (o k) v", p=P)).then_inc(c_loaded[slot], 16)

                for v in range(CSLOTS):
                    load_c(v)
                for v in range(UNITS):
                    slot, (b, half) = v % CSLOTS, UNIT[v]
                    sp.wait_ge(unit_freed, freed.adv() + 2 * FIRST)
                    stand_alone(sp)
                    dst = (O["ml_C_p"][0, 0] if b is None else O["ml_C_s"][0, b])[ds(h, 1), half * 256:half * 256 + 256, :]
                    sp.dma_start(dst.rearrange("o (k p) v -> p (o k) v", p=P), C_HALVES[:, slot]).then_inc(c_stored[slot], 16)
                    if CSLOTS <= v - 1 + CSLOTS < UNITS:
                        load_c(v - 1 + CSLOTS)
            sp.wait_ge(wbd_ready, HEADS + 1)
            load_p(1, h_done, HEADS + FIRST)
            for m in range(1, 4):
                o_job(m)
            for g in range(2):
                if g:
                    for m in range(4, 8):
                        o_job(m)
                with loop(sp, 2, {lo_t: 8}) as j:
                    for m in range(2):
                        for k in range(4):
                            slab(w_slab(ml_out, 4 * g + k, ds(j * 512 + m * 256, 256)))
            ffn(1)
            ple(1)
            sp.wait_ge(states_out, 4)
            for dst, src in ((O["rg_conv_s"].rearrange("l b t d -> (l b t) d"), RG_ROWS[0:24, :]),
                             (O["rg_h_s"].rearrange("l b d -> (l b) d"), RG_ROWS[24:32, :]),
                             (O["rg_conv_p"].rearrange("l b t d -> (l b t) d"), RG_ROWS[32:35, :]),
                             (O["rg_h_p"].rearrange("l b d -> (l b) d"), RG_ROWS[35:36, :]),
                             (O["ml_conv_s"].rearrange("l b t d -> (l b t) d"), ML_ROWS[0:24, :]),
                             (O["ml_conv_p"].rearrange("l b t d -> (l b t) d"), ML_ROWS[24:27, :]),
                             (O["ml_n_s"].rearrange("l b h (k p) -> (l b h k) p", p=P), N_ROWS[:, 0, :]),
                             (O["ml_n_p"].rearrange("l b h (k p) -> (l b h k) p", p=P), N_ROWS[0:16, 1, :])):
                sp.dma_start(dst, src).then_inc(stored, 16)
            with nc.allow_non_contiguous_dma(reason="m, 36 numbers"):
                sp.dma_start(O["ml_m_p"].rearrange("l b h -> h (l b)"), M_OUT[:, 0:1]).then_inc(stored, 16)
                sp.dma_start(O["ml_m_s"].rearrange("l b h -> h (l b)"), M_OUT[:, 1:1 + DEC_B]).then_inc(stored, 16)
            for i, (t0, n) in enumerate(TOKEN_TILES):
                sp.wait_ge(out_rows, i + 1)
                dst = O["y_prompt"][0, t0:t0 + n, :] if t0 < SEQ else O["y_sample"].rearrange("b t d -> (b t) d")
                sp.dma_start(dst, Y_ROWS[0:n, i % 2, :]).then_inc(y_stored[i % 2], 16)
            sp.wait_ge(stored, 16 * 10)
            sp.wait_ge(y_stored[0], 16 * 3)
            sp.wait_ge(y_stored[1], 16 * 2)
            for slot in range(CSLOTS):
                sp.wait_ge(c_stored[slot], 16 * HEADS * per_slot + 16 * FIRST)

        @block.gpsimd
        def _(pool):
            slabs, step, conv_t, sq_t, misc = Tally(), Tally(), Tally(), Tally(), Tally()
            uses = [Tally(), Tally()]
            scans, ys = Tally(), Tally()
            phase = [0]

            def split_lo():
                n = slabs.adv()
                if isinstance(n, int) and n > TOTAL:
                    return
                pool.wait_ge(hi_ready, n)
                s = phase[0] % 4
                phase[0] += 1
                pool.tensor_tensor(W_LO[:, s], W_RAW[:, s], W_HI[:, s].bitcast(F32), ALU.subtract).then_inc(lo_ready, 1)

            def clear_acc():
                pool.memset(SQUARE_SUM[:, :, :], 0.0).then_inc(acc_clear, 1)

            def add_sq():
                pool.wait_ge(sq_ready, sq_t.adv())
                pool.tensor_tensor(SQUARE_SUM[:, :, :], SQUARE_SUM[:, :, :], SQUARES[:, :, :], ALU.add).then_inc(acc_ready, 1)

            waits_passed[id(pool)] = sem("pool_waits_passed")
            give_credit(pool, lo_ready, tails_out, h_out, y_lo)
            pool.memset(IDENT[:, :], 0.0).then_inc(pool_step, 1)
            pool.wait_ge(pool_step, step.adv())
            pool.affine_select(out=IDENT[:, :], in_=IDENT[:, :], compare_op=ALU.not_equal, fill=1.0, base=0,
                               pattern=[[-1, P]], channel_multiplier=1)
            pool.memset(ONES[:, :], 1.0)
            pool.memset(XB_PAD[:, :, 0:TAIL], 0.0)
            pool.memset(RG_STATE_IN[:, CR:CR + 2, :], 0.0)
            pool.memset(QKV_BLOCKS[:, :, CI:CI + 4, :], 0.0)
            pool.memset(A_PAD[:, :, SEQ:WSCAN], 0.0)
            for t in (CAUSAL, CAUSAL_S, SAMPLE_MASK, BLOCK_MASK):
                pool.memset(t[:, :], 1.0)
            pool.memset(EPS_COL[:, :], EPS).then_inc(const_ready, 1)
            pool.wait_ge(const_ready, 1)

            def keep(t, pattern, base, mult):
                pool.affine_select(out=t, in_=t, compare_op=ALU.is_ge, fill=0.0, base=base, pattern=pattern,
                                   channel_multiplier=mult).then_inc(pool_step, 1)
                pool.wait_ge(pool_step, step.adv())

            keep(CAUSAL[:, :], [[1, P]], 0, -1)
            keep(CAUSAL_S[:, :], [[1, N_STOK]], 0, -1)
            keep(CAUSAL_S[:, :].rearrange("p (b t) -> p b t", b=DEC_B), [[-DEC_S, DEC_B], [0, DEC_S]], 0, 1)
            for r in range(0, 3 * GROUP_T, GROUP_T):
                keep(SAMPLE_MASK[r:r + GROUP_T, :], [[-DEC_S, 4]], 0, 1)
                keep(SAMPLE_MASK[r:r + GROUP_T, :], [[DEC_S, 4]], DEC_S - 1, -1)
            keep(BLOCK_MASK[:, :], [[-4, 32]], 0, 1)
            keep(BLOCK_MASK[:, :], [[4, 32]], 3, -1)
            clear_acc()
            for k in range(4):
                split_lo()
            pool.wait_ge(acc_clear, 1)
            for m in range(4):
                add_sq()
            pool.wait_ge(vecs_ready, 1)

            def rg_pads(c0):
                pool.tensor_copy(
                    XB_PAD[:, :, XB0:XB0 + DEC_B * SEG].rearrange("p m (b t) -> p m b t", b=DEC_B)[:, :, :, 0:TAIL],
                    RG_STATE_IN[:, ds(c0, 2), 0:24].rearrange("p m (b t) -> p m b t", b=DEC_B)).then_inc(pads_ready, 1)

            rg_pads(0)
            for k in range(2):
                split_lo()
            with loop(pool, 3, {slabs: 20, uses[0]: 4, uses[1]: 4, conv_t: 2, scans: 2, ys: 2}) as j:
                for jj in range(2):
                    c0 = 4 * j + 2 * jj
                    u0 = uses[0].adv()
                    for k in range(3):
                        split_lo()
                    pool.wait_ge(conv_done, conv_t.adv() + FIRST)
                    pool.tensor_copy(
                        RG_STATE_OUT[:, ds(c0, 2), 0:24].rearrange("p m (b t) -> p m b t", b=DEC_B),
                        XB_PAD[:, :, XB0:XB0 + DEC_B * SEG].rearrange("p m (b t) -> p m b t", b=DEC_B)[:, :, :, DEC_S:SEG])
                    pool.tensor_copy(RG_STATE_OUT[:, ds(c0, 2), 32:35], XB_PAD[:, :, XB0 - TAIL:XB0]).then_inc(tails_out, 1)
                    rg_pads(c0 + 2)
                    for k in range(7):
                        split_lo()
                    uses[0].adv()
                    uses[1].adv(2)
                    pool.wait_ge(scan_done, scans.adv() + FIRST)
                    pool.tensor_copy(
                        RG_STATE_OUT[:, ds(c0, 2), 24:32],
                        H_PAD[:, :, SEQ:WSCAN].rearrange("p m (b t) -> p m b t", b=DEC_B)[:, :, :, DEC_S])
                    pool.tensor_copy(RG_STATE_OUT[:, ds(c0, 2), 35:36], H_PAD[:, :, SEQ - 1:SEQ]).then_inc(h_out, 1)
                    pool.wait_ge(y_hi, ys.adv())
                    pool.tensor_tensor(Y_LO[:, ds(c0, 2), :], Y_F32[:, :, :], Y_HI[:, ds(c0, 2), :].bitcast(F32),
                                       ALU.subtract).then_inc(y_lo, 1)

            def next_norm():
                pool.wait_ge(misc_done, misc.adv() + FIRST)
                clear_acc()

            misc.adv(6)
            next_norm()
            pool.wait_ge(acc_clear, 2)
            for m in range(4):
                for k in range(6 if m else 4):
                    split_lo()
                add_sq()

            def ffn1():
                ffn(A_HI, A_LO)

            def g_lo(j, dst_h, dst_l, src):
                pool.tensor_tensor(dst_l[:, ds(j * 2, 2), :], src[:, :, :], dst_h[:, ds(j * 2, 2), :].bitcast(F32),
                                   ALU.subtract).then_inc(y_lo, 1)

            def ffn(gh=G_HI, gl=G_LO):
                for g, (g0, gn) in enumerate(GROUPS):
                    with loop(pool, gn // 2, {slabs: 8, ys: 1}) as j:
                        for k in range(8):
                            split_lo()
                        pool.wait_ge(y_hi, ys.adv())
                        g_lo(j, gh, gl, GATED)
                    ks = gn // 2
                    n = 4 if ks % 2 else 2
                    with loop(pool, 4 // n, {slabs: ks * n}) as j:
                        for k in range(ks * n):
                            split_lo()

            def ple(clear, last):
                for k in range(4):
                    split_lo()
                misc.adv()
                next_norm()
                pool.wait_ge(acc_clear, clear)
                for j in (range(2) if last else (None,)):
                    if last:
                        body(j)
                    else:
                        with loop(pool, 2, {slabs: 8, sq_t: 2}) as j:
                            body(j)

            def body(j):
                for m in range(2):
                    for k in range(4):
                        split_lo()
                    add_sq()

            ffn()
            ple(3, False)
            pool.memset(XM_PAD[:, :, 0:TAIL], 0.0)

            def link(ins):
                ins.then_inc(pool_step, 1)
                pool.wait_ge(pool_step, step.adv())

            def ml_in():
                with loop(pool, 4, {slabs: 8, conv_t: 2}) as j:
                    for m in range(2):
                        c0 = 4 * j + 2 * m
                        pool.wait_ge(conv_done, conv_t.adv() - 1 + FIRST)
                        pool.tensor_copy(
                            XM_PAD[:, :, XB0:XB0 + DEC_B * SEG].rearrange("p m (b t) -> p m b t", b=DEC_B)[:, :, :, 0:TAIL],
                            ML_CONV_IN[:, ds(c0, 2), :].rearrange("p m (b t) -> p m b t", b=DEC_B)).then_inc(pads_ready, 1)
                        for k in range(4):
                            split_lo()
                        pool.wait_ge(conv_done, conv_t.now() + FIRST)
                        pool.tensor_copy(
                            ML_CONV_OUT[:, ds(c0, 2), 0:24].rearrange("p m (b t) -> p m b t", b=DEC_B),
                            XM_PAD[:, :, XB0:XB0 + DEC_B * SEG].rearrange("p m (b t) -> p m b t", b=DEC_B)[:, :, :, DEC_S:SEG])
                        pool.tensor_copy(ML_CONV_OUT[:, ds(c0, 2), 24:27], XM_PAD[:, :, XB0 - TAIL:XB0]).then_inc(tails_out, 1)

            pool.wait_ge(wqkv_loaded, 48)
            pool.wait_ge(wgr_loaded, 16 * 14)
            link(pool.tensor_scalar(QKV_BLOCKS[:, 1, 0:CI], QKV_BLOCKS[:, 1, 0:CI], float(HD) ** -0.5, None, ALU.mult))
            link(pool.memset(GATE_FOLD[:, :, :], 0.0))
            for i in range(3):
                g = GATE_W[:, i * CI:i * CI + CI]
                link(pool.tensor_tensor(g, g, QKV_BLOCKS[:, i, 0:CI].unsqueeze(3).broadcast_to([P, CI, 4, 8]), ALU.mult))
            link(pool.tensor_tensor(GATE_W[:, :, 0:2, :], GATE_W[:, :, 0:2, :], GATE_W[:, :, 2:4, :], ALU.add))
            link(pool.tensor_tensor(GATE_W[:, :, 0, :], GATE_W[:, :, 0, :], GATE_W[:, :, 1, :], ALU.add))
            for g in range(2):
                e = GATE_FOLD[:, :, 32 * g:32 * g + 4]
                w = GATE_W[:, :, 0, 4 * g:4 * g + 4]
                pool.tensor_tensor(e[:, 0:CI], w[:, 0:CI], w[:, CI:2 * CI], ALU.add)
                pool.tensor_copy(e[:, CI:2 * CI], w[:, 2 * CI:3 * CI]).then_inc(et_ready, 1)
            ml_in()

            def blocks(h):
                for i in range(3):
                    ins = pool.tensor_tensor(
                        QKV_DIAG[:, i].rearrange("p c (b o) -> p c b o", o=4),
                        QKV_BLOCKS[:, i, ds(4 * h, 4), :].unsqueeze(2).broadcast_to([P, 4, 32, 4]),
                        BLOCK_MASK[:, :].unsqueeze(1).unsqueeze(3).broadcast_to([P, 4, 32, 4]), ALU.mult)
                ins.then_inc(wbd_ready, 1)

            heads, misc_h = Tally(), Tally()
            misc_h.adv(12)
            pool.wait_ge(misc_done, misc_h.now() + FIRST)
            blocks(0)
            with loop(pool, HEADS, {heads: 1, misc_h: 15, step: 1}) as h:
                n = heads.adv()
                pool.wait_ge(exp_done, n)
                for sbk in range(4):
                    pool.tensor_tensor(PROBS[:, PROBS_AT[sbk]:PROBS_AT[sbk] + P], PROBS[:, PROBS_AT[sbk]:PROBS_AT[sbk] + P], CAUSAL[:, :], ALU.mult)
                pool.tensor_tensor(PROBS_S[:, :], PROBS_S[:, :], CAUSAL_S[:, :], ALU.mult).then_inc(masked, 1)
                pool.wait_ge(misc_done, misc_h.adv(10) + FIRST)
                stand_alone(pool)
                link(pool.memset(Q_T[:, :, 0:DEC_B * N_STOK], 0.0))
                pool.wait_ge(nq_ready, n)
                pool.tensor_copy(Q_T[:, :, 0:T].rearrange("p k (b x) -> p k b x", b=DEC_B)[:, :, :, 0:DEC_S],
                                 XM[:, ds(4 * h + 3, 1), 0:4 * N_STOK].rearrange("p o (k b t) -> p (o k) b t", k=4, b=DEC_B))\
                    .then_inc(qz_ready, 1)
                blocks(h + 1)
                misc_h.adv(5)

            def small_lo(j, dst_h, dst_l):
                pool.wait_ge(y_hi, ys.adv())
                pool.tensor_tensor(dst_l[:, ds(j, 2), :], GATED[:, :, :], dst_h[:, ds(j, 2), :].bitcast(F32),
                                   ALU.subtract).then_inc(y_lo, 1)

            misc.adv(2 + 15 * HEADS + STATE_JOBS)
            for g in range(2):
                with loop(pool, 2, {slabs: 8, ys: 2}) as j:
                    for m in range(2):
                        for k in range(4):
                            split_lo()
                        small_lo(4 * j + 2 * m, A_HI, A_LO)
                if g:
                    next_norm()
                    pool.wait_ge(acc_clear, 4)
                with loop(pool, 2, {slabs: 8, **({sq_t: 2} if g else {})}) as j:
                    for m in range(2):
                        for k in range(4):
                            split_lo()
                        if g:
                            add_sq()
            ffn1()
            ple(5, True)

        @block.scalar
        def _(act):
            slabs, step, sq_t, misc, jobs = Tally(), Tally(), Tally(), Tally(), Tally()
            raw_t = [Tally(16) for _ in range(4)]
            uses = [Tally(), Tally()]
            xr, blk, conv_t = Tally(), Tally(), Tally()
            phase = [0]

            def link(ins):
                ins.then_inc(act_step, 1)
                act.wait_ge(act_step, step.adv())

            def split_hi():
                n = slabs.adv()
                if isinstance(n, int) and n > TOTAL:
                    return
                s = phase[0] % 4
                phase[0] += 1
                act.wait_ge(raw_loaded[s], raw_t[s].adv())
                stand_alone(act)
                act.wait_ge(slab_used, n - 4 + 2 * RING)
                stand_alone(act)
                act.activation(W_HI[:, s], W_RAW[:, s], ACT.Copy).then_inc(hi_ready, 1)

            def split_per(n):
                return {slabs: n, **{t: n // 4 for t in raw_t}}

            def prep(c0, gain, hi, norm=True):
                act.wait_ge(x_ready, xr.adv())
                stand_alone(act)
                for m in range(2):
                    if gain is None:
                        ins = act.activation(hi[:, ds(c0 + m, 1), :], X[:, ds(c0 + m, 1), :], ACT.Copy)
                    else:
                        ins = act.activation(hi[:, ds(c0 + m, 1), :], X[:, ds(c0 + m, 1), :], ACT.Copy,
                                             scale=VECS1[:, ds(gain + c0 + m, 1)])
                ins.then_inc(xn_hi, 1)
                if norm:
                    before = sq_t.adv() - 1
                    if not is_zero(before):
                        act.wait_ge(acc_ready, before)
                        stand_alone(act)
                    act.activation(SQUARES[:, :, :], X[:, ds(c0, 2), :], ACT.Square).then_inc(sq_ready, 1)

            def std(s):
                uses[s].adv()
                act.wait_ge(misc_done, misc.adv() + FIRST)
                act.activation(RSTD[:, :].rearrange("p (h n) -> p h n", h=2), ps[:, 4 * s:4 * s + 2, 0:HALF_T], ACT.Sqrt,
                               bias=EPS_COL[:, :], scale=1.0 / D_MODEL).then_inc(psum_freed[s], 1)

            waits_passed[id(act)] = sem("act_waits_passed")
            give_credit(act, xc_hi)
            r = lambda name, pat, **k: I[name].rearrange(pat, **k)
            vec_rows = [
                (VEC_ROWS[0:16, 0, :], r("norm_mix", "l (c p) -> (l c) p", p=P)),
                (VEC_ROWS[16:32, 0, :], r("norm_ffn", "l (c p) -> (l c) p", p=P)),
                (VEC_ROWS[32:80, 0, :], r("rg_conv_w", "l w (c p) -> (l w c) p", p=P)),
                (VEC_ROWS[80:92, 0, :], r("rg_conv_b", "l (c p) -> (l c) p", p=P)),
                (VEC_ROWS[92:104, 0, :], r("rg_b_r", "l (c p) -> (l c) p", p=P)),
                (VEC_ROWS[104:116, 0, :], r("rg_b_i", "l (c p) -> (l c) p", p=P)),
                (VEC_ROWS[116:128, 0, :], r("rg_lambda", "l (c p) -> (l c) p", p=P)),
                (VEC_ROWS[0:64, 1, :], r("ml_conv_w", "l w (c p) -> (l w c) p", p=P)),
                (VEC_ROWS[64:80, 1, :], r("ml_conv_b", "l (c p) -> (l c) p", p=P)),
                (VEC_ROWS[80:96, 1, :], r("ml_norm", "l (c p) -> (l c) p", p=P)),
                (VEC_ROWS[96:112, 1, :], r("ple_b_gate", "l (c p) -> (l c) p", p=P)),
                (VEC_ROWS[112:120, 1, :], r("norm_final", "(c p) -> c p", p=P)),
                (N_IN_ROWS[:, :], r("state_mlstm_n", "l b h (k p) -> (l b h k) p", p=P)),
                (RG_IN_ROWS[0:24, :], r("state_rglru_conv", "l b t d -> (l b t) d")),
                (RG_IN_ROWS[24:32, :], r("state_rglru_h", "l b d -> (l b) d")),
                (ML_IN_ROWS[:, :], r("state_mlstm_conv", "l b t d -> (l b t) d")),
            ]
            for dst, src in vec_rows:
                act.dma_start(dst, src).then_inc(rows_loaded, 16)
            assert 16 * len(vec_rows) == ROWS_LOADED
            for k in range(4):
                split_hi()
            act.wait_ge(vecs_ready, 1)
            link(act.activation(LAM8[:, 0, :], VECS1[:, C_LAM:C_LAM + CR], ACT.Abs))
            act.activation(LAM8[:, 1, :], LAM8[:, 0, :], ACT.Exp, scale=-1.0).then_inc(lam_e, 1)
            act.wait_ge(acc_clear, 1)
            misc.adv(6)
            uses[0].adv(3)
            uses[1].adv(3)
            for m in range(4):
                prep(2 * m, G_MIX, A_HI)
            std(1)
            split_hi()
            split_hi()
            with loop(act, 3, {**split_per(20), jobs: 20, uses[0]: 4, uses[1]: 4, blk: 2}) as j:
                for jj in range(2):
                    c0 = 4 * j + 2 * jj
                    for k in range(3):
                        split_hi()
                    jobs.adv(8)
                    b = blk.adv()
                    act.wait_ge(conv_done, b + FIRST)
                    stand_alone(act)
                    act.wait_ge(slab_used, jobs.now() - 8 + 2 * RING)
                    stand_alone(act)
                    (src_p, src_s), (dst_p, dst_s) = padded(XC_PAD, WPAD, SEG, 0, 0), tight(XC_HI)
                    src_s = XC_PAD[:, :, XB0:XB0 + DEC_B * SEG].rearrange("p m (b t) -> p m b t", b=DEC_B)[:, :, :, 0:DEC_S]
                    act.activation(dst_p, XC_PAD[:, :, 0:SEQ], ACT.Copy)
                    act.activation(dst_s, src_s, ACT.Copy).then_inc(xc_hi, 1)
                    for k in range(3):
                        split_hi()
                    uses[0].adv()
                    act.wait_ge(psum_freed[1], uses[1].adv())
                    stand_alone(act)
                    act.activation(GELU_T[:, :, :], GELU_T[:, :, :], ACT.Gelu_apprx_tanh).then_inc(gelu_done, 1)
                    act.wait_ge(slab_used, jobs.adv() + 2 * RING)
                    stand_alone(act)
                    for m in range(2):
                        ins = act.activation(R_GATE[:, m].rearrange("p (h n) -> p h n", h=2), psv[:, 0, m, :, 0:HALF_T],
                                             ACT.Sigmoid, bias=VECS1[:, ds(C_BR + m + c0, 1)])
                    ins.then_inc(psum_freed[0], 1)
                    split_hi()
                    act.wait_ge(slab_used, jobs.adv() + 2 * RING)
                    stand_alone(act)
                    act.wait_ge(scan_done, b - 1 + FIRST)
                    stand_alone(act)
                    for m in range(2):
                        ins = act.activation(I_GATE[:, m].rearrange("p (h n) -> p h n", h=2), psv[:, 1, m, :, 0:HALF_T],
                                             ACT.Sigmoid, bias=VECS1[:, ds(C_BI + m + c0, 1)])
                    ins.then_inc(psum_freed[1], 1)
                    act.wait_ge(psum_freed[0], uses[0].adv())
                    stand_alone(act)
                    for m in range(2):
                        ins = act.activation(TANH_T[:, m, :], R_GATE[:, m, :], ACT.Tanh, scale=LAM8[:, 0, ds(c0 + m, 1)])
                    ins.then_inc(s_ready, 1)
                    for m in range(2):
                        act.activation(A_PAD[:, m, 0:SEQ], R_GATE[:, m, 0:SEQ], ACT.Exp, scale=LAM8[:, 1, ds(c0 + m, 1)])
                        ins = act.activation(
                            A_PAD[:, m, SEQ:WSCAN].rearrange("p (b t) -> p b t", b=DEC_B)[:, :, 1:HSEG],
                            R_GATE[:, m, SEQ:T].rearrange("p (b t) -> p b t", b=DEC_B), ACT.Exp,
                            scale=LAM8[:, 1, ds(c0 + m, 1)])
                    ins.then_inc(a_ready, 1)
                    split_hi()
                    act.wait_ge(v_in, b)
                    stand_alone(act)
                    act.activation(TANH_T[:, :, :], TANH_T[:, :, :], ACT.Sqrt).then_inc(v_ready, 1)
                    uses[1].adv()
                    split_hi()
                    split_hi()
                    act.wait_ge(y_ready, b)
                    stand_alone(act)
                    act.activation(Y_HI[:, ds(c0, 2), :], Y_F32[:, :, :], ACT.Copy).then_inc(y_hi, 1)
            act.wait_ge(acc_clear, 2)
            for m in range(4):
                for k in range(6 if m else 4):
                    split_hi()
                jobs.adv(6)
                uses[m % 2].adv()
                prep(2 * m, G_FFN, A_HI)
            std(1)

            def ffn(last_out, gh):
                for g, (g0, gn) in enumerate(GROUPS):
                    with loop(act, gn // 2, {**split_per(8), jobs: 8, uses[0]: 1, uses[1]: 1, blk: 1}) as j:
                        for k in range(4):
                            split_hi()
                        b = blk.adv()
                        act.wait_ge(psum_freed[0], uses[0].adv())
                        stand_alone(act)
                        act.activation(GATE[:, :, :], GATE[:, :, :], ACT.Silu).then_inc(silu_done, 1)
                        for k in range(4):
                            split_hi()
                        jobs.adv(8)
                        uses[1].adv()
                        act.wait_ge(y_ready, b)
                        stand_alone(act)
                        act.activation(gh[:, ds(2 * j, 2), :], GATED[:, :, :], ACT.Copy).then_inc(y_hi, 1)
                    ks = gn // 2
                    n = 4 if ks % 2 else 2
                    lastg = g == len(GROUPS) - 1
                    with loop(act, 4 // n, {**split_per(ks * n), jobs: ks * n, uses[0]: n // 2, uses[1]: n // 2,
                                            xr: n if lastg else 0}) as j:
                        for m in range(n):
                            for k in range(ks):
                                split_hi()
                            jobs.adv(ks)
                            uses[m % 2].adv()
                            if lastg:
                                prep(4 * j + 2 * m, None, last_out, norm=False)

            def ple(layer, P_HI, P_PROJ, gain, dst, acc0):
                act.wait_ge(misc_done, misc.adv() + FIRST)
                act.activation(P_HI[:, :, 0:SEQ], ps[:, 0:4:2, 0:SEQ], ACT.Copy)
                act.activation(P_HI[:, :, SEQ:T], ps[:, 1:4:2, 0:N_STOK], ACT.Copy).then_inc(pt_hi, 1)
                uses[0].adv()
                for m in range(4):
                    split_hi()
                    s = (m + 1) % 2
                    uses[s].adv()
                    act.wait_ge(slab_used, jobs.adv() + 2 * RING)
                    act.activation(pair4(P_PROJ[:, 2 * m:2 * m + 2, :]), psum4(s), ACT.Copy).then_inc(psum_freed[s], 1)
                act.wait_ge(acc_clear, acc0)

                def body(j):
                    for m in range(2):
                        for k in range(4):
                            split_hi()
                        act.wait_ge(slab_used, jobs.adv(4) + 2 * RING)
                        stand_alone(act)
                        s = (m + 1) % 2
                        uses[s].adv()
                        act.wait_ge(x_ready, xr.now())
                        stand_alone(act)
                        for c in range(2):
                            ins = act.activation(GATE[:, c].rearrange("p (h n) -> p h n", h=2), psv[:, s, c, :, 0:HALF_T],
                                                 ACT.Sigmoid, bias=VECS2[:, ds(C_PB + 8 * layer + 2 * m + c + 4 * j, 1)])
                        ins.then_inc(psum_freed[s], 1)
                        if dst is None:
                            act.wait_ge(x_ready, xr.adv())
                            act.wait_ge(acc_ready, sq_t.adv() - 1)
                            act.activation(SQUARES[:, :, :], X[:, ds(4 * j + 2 * m, 2), :], ACT.Square).then_inc(sq_ready, 1)
                        else:
                            prep(4 * j + 2 * m, gain, dst)

                if layer:
                    for j in range(2):
                        body(j)
                else:
                    with loop(act, 2, {**split_per(8), jobs: 8, uses[0]: 1, uses[1]: 1, xr: 2, sq_t: 2}) as j:
                        body(j)
                if dst is not None:
                    std(1)

            ffn(A_HI, G_HI)
            ple(0, P_HI0, P_PROJ0, G_MIX + 8, B_HI, 3)

            with loop(act, 4, {**split_per(8), jobs: 8, uses[0]: 1, uses[1]: 1, conv_t: 2}) as j:
                for m in range(2):
                    c0 = 4 * j + 2 * m
                    for k in range(4):
                        split_hi()
                    jobs.adv(4)
                    act.wait_ge(psum_freed[m], uses[m].adv())
                    stand_alone(act)
                    mp, ms = tight(XM[:, ds(c0, 2), :])
                    act.activation(mp, XM_PAD[:, :, TAIL:XB0], ACT.Copy)
                    act.activation(ms, XM_PAD[:, :, XB0:XB0 + DEC_B * SEG].rearrange("p m (b t) -> p m b t", b=DEC_B)[:, :, :, TAIL:SEG],
                                   ACT.Copy).then_inc(xm_copied, 1)
                    act.wait_ge(conv_done, 6 + conv_t.adv() + FIRST)
                    stand_alone(act)
                    cp, cs = tight(XC[:, ds(c0, 2), :])
                    act.activation(cp, CONV_OUT[:, :, 0:SEQ], ACT.Silu)
                    act.activation(cs, CONV_OUT[:, :, XB0:XB0 + DEC_B * SEG].rearrange("p m (b t) -> p m b t", b=DEC_B)[:, :, :, 0:DEC_S],
                                   ACT.Silu).then_inc(xc_silu, 1)
            misc.adv()
            uses[0].adv()
            act.wait_ge(f_ready, 1)
            link(act.activation(ABS_F[:, :], F_ROW[:, :], ACT.Abs))
            link(act.activation(ABS_F[:, :], ABS_F[:, :], ACT.Exp, scale=-1.0))
            act.activation(ABS_F[:, :], ABS_F[:, :], ACT.Ln, bias=1.0).then_inc(ln_ready, 1)
            act.wait_ge(t1_ready, 1)
            act.activation(EXP_ROW[:, :], M_ROW[:, :], ACT.Exp, scale=-1.0)
            act.activation(OLD_W_ROW[:, :], OLD_W_ROW[:, :], ACT.Exp)
            link(act.activation(KEY_W_ROW[:, :], KEY_W_ROW[:, :], ACT.Exp))
            for g in range(2):
                ins = act.activation(KEY_W_STACK[:, g, :].rearrange("p (r t) -> p r t", r=3), KEY_W_ROW[:, SEQ + g * GROUP_T:SEQ + g * GROUP_T + GROUP_T]
                                     .unsqueeze(1).broadcast_to([HEADS, 3, GROUP_T]), ACT.Copy)
            ins.then_inc(rows_ready, 1)

            def stack(src):
                for g in range(2):
                    ins = act.activation(X_STACK[g].rearrange("p c (r t) -> p c r t", r=3), src[:, :, SEQ + g * GROUP_T:SEQ + g * GROUP_T + GROUP_T]
                                         .unsqueeze(2).broadcast_to([P, 4, 3, GROUP_T]), ACT.Copy)
                ins.then_inc(stack_ready, 1)
            misc.adv()
            uses[1].adv()
            heads, units = Tally(), Tally()
            act.wait_ge(misc_done, misc.now() + FIRST)
            act.activation(HEAD_T[:, :, :], XM_XC[:, 0:4, :], ACT.Copy).then_inc(ht_ready, 1)
            with loop(act, HEADS, {misc: 15, uses[0]: 7, uses[1]: 6, heads: 1, units: UNITS}) as h:
                n = heads.adv()
                act.wait_ge(misc_done, misc.adv() + FIRST)
                stand_alone(act)
                act.activation(V_ROWS[:, 0:4, :], ps[:, 0:4, :], ACT.Copy).then_inc(psum_freed[0], 1)
                uses[0].adv()
                act.wait_ge(misc_done, misc.adv() + FIRST)
                stand_alone(act)
                act.activation(V_ROWS[0:N_STOK, 4, :], ps[0:N_STOK, 4, :], ACT.Copy)
                act.activation(MAX_B[:, 0:SEQ], ps[:, 5, :], ACT.Copy)
                act.activation(EXP_NEG_M[:, 0:SEQ], ps[:, 6, :], ACT.Copy)
                act.activation(MAX_B[:, SEQ:T], ps[:, 7, 0:N_STOK], ACT.Copy)
                act.activation(EXP_NEG_M[:, SEQ:T], ps[:, 7, N_STOK:2 * N_STOK], ACT.Copy)
                act.activation(OLD_W[:, :], ps[:, 7, 2 * N_STOK:3 * N_STOK], ACT.Copy).then_inc(psum_freed[1], 1)
                uses[1].adv()
                for s in range(2):
                    act.wait_ge(misc_done, misc.adv() + FIRST)
                    stand_alone(act)
                    act.activation(pair4(Q_T[:, 2 * s:2 * s + 2, :]), psum4(s), ACT.Copy).then_inc(psum_freed[s], 1)
                    uses[s].adv()
                act.wait_ge(h_done, n - 1 + FIRST)
                stand_alone(act)
                stack(HEAD_T)
                act.wait_ge(misc_done, misc.adv() + FIRST)
                act.wait_ge(ht_ready, n)
                stand_alone(act)
                act.activation(V_STACK[0:3 * GROUP_T, ds(4 * h, 2), 0:HD], ps[0:3 * GROUP_T, 0:2, :], ACT.Copy).then_inc(vs_hi, 1)
                uses[0].adv()
                for s in (1, 0):
                    act.wait_ge(misc_done, misc.adv() + FIRST)
                    stand_alone(act)
                    act.activation(pair4(HEAD_T[:, 2 * s:2 * s + 2, :]), psum4(s), ACT.Copy).then_inc(psum_freed[s], 1)
                    uses[s].adv()
                act.wait_ge(psum_freed[1], uses[1].now())
                stand_alone(act)
                act.wait_ge(psum_freed[0], uses[0].now())
                stand_alone(act)
                stack(HEAD_T)
                act.wait_ge(e_ready, n)
                stand_alone(act)
                act.activation(PROBS[:, :], PROBS[:, :], ACT.Exp, scale=-1.0)
                act.activation(PROBS_S[:, :], PROBS_S[:, :], ACT.Exp, scale=-1.0).then_inc(exp_done, 1)
                act.wait_ge(misc_done, misc.adv() + FIRST)
                stand_alone(act)
                for i in range(4):
                    ins = act.activation(K_WEIGHTED[:, i, :], ps[:, i, :], ACT.Copy, scale=KEY_COLS[:, i, ds(h + 4, 1)])
                ins.then_inc(psum_freed[0], 1)
                uses[0].adv()
                act.wait_ge(misc_done, misc.adv() + FIRST)
                stand_alone(act)
                act.activation(K_STACK[:, :, :], ps[0:3 * GROUP_T, 4:7:2, :], ACT.Copy).then_inc(kt4_done, 1)
                uses[1].adv()
                act.wait_ge(kt4_done, n)
                stand_alone(act)

                def kwm(b):
                    if b >= 2:
                        act.wait_ge(unit_done, units.now() + UNIT.index((b - 2, 1)) + 1 + 2 * FIRST)
                        stand_alone(act)
                    act.activation(KW_STACK[:, b % 2, :], K_STACK[:, b // 4, :], ACT.Copy,
                                   scale=KEY_WEIGHTS[:, b // 4, ds(h, 1), b % 4]).then_inc(kwm_hi, 1)

                kwm(0)
                kwm(1)
                misc.adv()
                uses[0].adv()
                act.wait_ge(misc_done, misc.adv() + FIRST)
                stand_alone(act)
                act.activation(XC[:, ds(4 * h, 4), 0:SEQ], ps[:, 4:8, :], ACT.Copy).then_inc(psum_freed[1], 1)
                uses[1].adv()
                act.activation(HEAD_T[:, :, :], XM_XC[:, ds(4 * h + 4, 4), :], ACT.Copy).then_inc(ht_ready, 1)
                act.wait_ge(misc_done, misc.adv() + FIRST)
                stand_alone(act)
                act.activation(DEN[:, 0:SEQ], ps[:, 0, :], ACT.Abs)
                act.activation(DEN[:, SEQ:T], ps[:, 2, 0:N_STOK], ACT.Abs).then_inc(rd_in, 1)
                for b in range(2, DEC_B):
                    kwm(b)
                    if b == 5:
                        act.wait_ge(unit_done, units.now() + PROMPT_UNITS[1] + 1 + 2 * FIRST)
                        stand_alone(act)
                        act.wait_ge(psum_freed[1], uses[1].now())
                        stand_alone(act)
                        act.activation(K_WEIGHTED[:, :, :], XC[:, ds(4 * h, 4), 0:SEQ], ACT.Square)
                units.adv(UNITS)
                act.wait_ge(misc_done, misc.adv() + FIRST)
                stand_alone(act)
                act.activation(V_ROWS[0:N_STOK, 4, :], ps[0:N_STOK, 1, :], ACT.Copy).then_inc(numt_ready, 1)
                act.wait_ge(misc_done, misc.adv() + FIRST)
                act.wait_ge(n_done, n)
                stand_alone(act)
                act.activation(XC[:, ds(4 * h, 4), SEQ:T], ps[:, 0, 0:4 * N_STOK].rearrange("p (v t) -> p v t", v=4),
                               ACT.Copy).then_inc(psum_freed[0], 1)
                act.wait_ge(psum_freed[0], uses[0].adv())
                stand_alone(act)
                act.activation(XM[:, ds(4 * h, 4), SEQ:T], XC[:, ds(4 * h, 4), SEQ:T], ACT.Square).then_inc(sqh_ready, 1)
                misc.adv()
                uses[1].adv()
                act.wait_ge(fv_ready, n)
                stand_alone(act)
                act.activation(SCALE_F[:, :], SCALE_F[:, :], ACT.Sqrt, bias=EPS_COL[:, :], scale=1.0 / HD).then_inc(sd_ready, 1)
            act.wait_ge(misc_done, misc.now() + FIRST)
            act.wait_ge(h_done, HEADS + FIRST)
            for m in range(4):
                for c in range(2 * m, 2 * m + 2):
                    ins = act.activation(B_HI[:, c, :], X[:, c, :], ACT.Copy, scale=VECS1[:, G_MIX + 8 + c:G_MIX + 9 + c])
                ins.then_inc(xn_hi, 1)
            for g in range(2):
                if g:
                    misc.adv(STATE_JOBS)
                    uses[0].adv(2)
                    uses[1].adv(2)
                with loop(act, 2, {**split_per(8), jobs: 8, uses[0]: 1, uses[1]: 1, blk: 2}) as j:
                    for m in range(2):
                        for k in range(4):
                            split_hi()
                        jobs.adv(4)
                        b = blk.adv()
                        act.wait_ge(psum_freed[m], uses[m].adv())
                        stand_alone(act)
                        act.activation(GATE[:, :, :], GATE[:, :, :], ACT.Sigmoid).then_inc(silu_done, 1)
                        act.wait_ge(y_ready, b)
                        stand_alone(act)
                        act.activation(A_HI[:, ds(4 * j + 2 * m, 2), :], GATED[:, :, :], ACT.Copy).then_inc(y_hi, 1)
                if g:
                    act.wait_ge(acc_clear, 4)
                with loop(act, 2, {**split_per(8), jobs: 8, uses[0]: 1, uses[1]: 1,
                                   **({xr: 2, sq_t: 2} if g else {})}) as j:
                    for m in range(2):
                        for k in range(4):
                            split_hi()
                        jobs.adv(4)
                        uses[m].adv()
                        if g:
                            prep(4 * j + 2 * m, G_FFN + 8, B_HI)
            std(1)
            ffn(B_HI, A_HI)
            ple(1, P_HI1, P_PROJ1, None, None, 5)
            act.wait_ge(misc_done, misc.adv(2) + FIRST)
            act.activation(RSTD_COLS[:, 0:4], ps[:, 4, 0:4], ACT.Sqrt, bias=EPS_COL[:, :], scale=1.0 / D_MODEL)
            act.activation(RSTD_COLS[0:N_STOK, 4:5], ps[0:N_STOK, 4, 4:5], ACT.Sqrt, bias=EPS_COL[0:N_STOK, :], scale=1.0 / D_MODEL)\
                .then_inc(psum_freed[1], 1)

        @block.vector
        def _(dve):
            step, misc, jobs, hi_t, blk = Tally(), Tally(), Tally(), Tally(), Tally()
            uses = [Tally(), Tally()]
            ys = Tally()

            def link(ins):
                ins.then_inc(dve_step, 1)
                dve.wait_ge(dve_step, step.adv())

            def xn_lo(c0, gain, hi, lo):
                dve.wait_ge(xn_hi, hi_t.adv())
                if gain is None:
                    dve.tensor_tensor(lo[:, ds(c0, 2), :], X[:, ds(c0, 2), :], hi[:, ds(c0, 2), :].bitcast(F32),
                                      ALU.subtract).then_inc(xn_ready, 1)
                    return
                for m in range(2):
                    ins = dve.scalar_tensor_tensor(
                        lo[:, ds(c0 + m, 1), :], X[:, ds(c0 + m, 1), :], VECS1[:, ds(gain + c0 + m, 1)],
                        hi[:, ds(c0 + m, 1), :].bitcast(F32), ALU.mult, ALU.subtract)
                ins.then_inc(xn_ready, 1)

            def evac_padded(dst, s):
                R = RSTD[:, :]
                dve.tensor_tensor(dst[:, :, TAIL:TAIL + HALF_T], psv[:, s, :, 0, 0:HALF_T],
                                  R[:, 0:HALF_T].unsqueeze(1).broadcast_to([P, 2, HALF_T]), ALU.mult)
                dve.tensor_tensor(dst[:, :, TAIL + HALF_T:XB0], psv[:, s, :, 1, 0:HALF_TP],
                                  R[:, HALF_T:SEQ].unsqueeze(1).broadcast_to([P, 2, HALF_TP]), ALU.mult)
                dve.tensor_tensor(
                    dst[:, :, XB0:XB0 + DEC_B * SEG].rearrange("p m (b t) -> p m b t", b=DEC_B)[:, :, :, TAIL:SEG],
                    psv[:, s, :, 1, HALF_TP:HALF_T].rearrange("p m (b t) -> p m b t", b=DEC_B),
                    R[:, SEQ:T].rearrange("p (b t) -> p b t", b=DEC_B).unsqueeze(1).broadcast_to([P, 2, DEC_B, DEC_S]),
                    ALU.mult).then_inc(psum_freed[s], 1)

            def conv(src, dst, c0, V, cw, cb, per):
                for k in range(CONV_W):
                    for m in range(2):
                        o = dst[:, m, 0:WCONV]
                        wk = V[:, ds(cw + k * per + c0 + m, 1)]
                        if k == 0:
                            ins = dve.tensor_scalar(o, src[:, m, 0:WCONV], wk, V[:, ds(cb + c0 + m, 1)], ALU.mult, ALU.add)
                        else:
                            ins = dve.scalar_tensor_tensor(o, src[:, m, k:k + WCONV], wk, o, ALU.mult, ALU.add)
                    if k < CONV_W - 1:
                        link(ins)
                ins.then_inc(conv_done, 1)

            so = [0]
            cl = [Tally(16), Tally(16)]

            def rstd(s):
                dve.wait_ge(psum_freed[s], uses[s].adv())
                misc.adv()
                dve.reciprocal(RSTD[:, :], RSTD[:, :]).then_inc(std_ready, 1)

            stds, xf = Tally(), Tally()
            xf.adv(X_PAIRS_DONE)
            give_credit(dve, conv_done, scan_done, unit_freed, h_done)
            for i, (t0, n) in enumerate(TOKEN_TILES):
                s = i % 2
                dve.wait_ge(misc_done, misc.adv() + FIRST)
                uses[s].adv()
                dve.tensor_copy(X[:, :, t0:t0 + n],
                                ps[:, 4 * s:4 * s + 2, :].rearrange("p b (c t) -> p (b c) t", t=P)[:, :, 0:n])\
                    .then_inc(psum_freed[s], 1)
            dve.wait_ge(misc_done, misc.adv() + FIRST)
            for dst, src in ((VECS1[:, :], ps[:, 4, 0:P]), (VECS2[:, 0:120], ps[:, 4, P:P + 120]),
                             (N_SAMPLES[:, :, :, :].rearrange("p b h k -> p (b h k)"), ps[:, 4, 256:384]),
                             (RG_STATE_IN[:, 0:CR, :].rearrange("p c r -> p (c r)"), ps[:, 5, 0:CR * 32]),
                             (ML_CONV_IN[:, :, :].rearrange("p c r -> p (c r)"), ps[:, 6, 0:CI * 24])):
                ins = dve.tensor_copy(dst, src)
                ins.then_inc(dve_step, 1)
                step.adv()
            uses[1].adv()
            dve.wait_ge(dve_step, step.now())
            dve.nop().then_inc(vecs_ready, 1)
            dve.nop().then_inc(psum_freed[1], 1)
            dve.wait_ge(psum_freed[0], 3)
            dve.wait_ge(psum_freed[1], 3)
            for m in range(4):
                dve.nop().then_inc(x_ready, 1)
            for m in range(4):
                xn_lo(2 * m, G_MIX, A_HI, A_LO)
            dve.wait_ge(lam_e, 1)
            e_, z, z2, p = LAM8[:, 1, :], A_SQUARE[:, 0, 0:CR], A_SQUARE[:, 0, 16:16 + CR], A_SQUARE[:, 0, 32:32 + CR]
            link(dve.tensor_scalar(z2, e_, 2.0, None, ALU.add))
            link(dve.reciprocal(z2, z2))
            link(dve.tensor_tensor(z, e_, z2, ALU.mult))
            link(dve.tensor_tensor(z2, z, z, ALU.mult))
            link(dve.tensor_scalar(p, z2, 1.0 / 17, None, ALU.mult))
            for k in (15, 13, 11, 9, 7, 5, 3):
                link(dve.scalar_tensor_tensor(p, p, 1.0 / k, z2, ALU.add, ALU.mult))
            link(dve.scalar_tensor_tensor(p, p, 1.0, z, ALU.add, ALU.mult))
            link(dve.tensor_scalar(z, VECS1[:, C_LAM:C_LAM + CR], -1.0, 0.0, ALU.mult, ALU.max))
            link(dve.scalar_tensor_tensor(p, p, 2.0, z, ALU.mult, ALU.add))
            link(dve.tensor_scalar(LAM8[:, 0, :], p, 8.0, None, ALU.mult))
            link(dve.tensor_scalar(LAM8[:, 1, :], p, -8.0, None, ALU.mult))
            rstd(1)
            dve.wait_ge(std_ready, stds.adv())
            with loop(dve, 3, {jobs: 20, uses[0]: 4, uses[1]: 4, blk: 2, step: 2 * 7}) as j:
                for jj in range(2):
                    c0 = 4 * j + 2 * jj
                    b = blk.adv()
                    dve.wait_ge(slab_used, jobs.adv(4) + 2 * RING)
                    dve.wait_ge(tails_out, b - 1 + FIRST)
                    evac_padded(XB_PAD, 0)
                    dve.wait_ge(psum_freed[0], uses[0].adv())
                    dve.wait_ge(pads_ready, b)
                    dve.wait_ge(xc_hi, b - 1 + FIRST)
                    conv(XB_PAD, XC_PAD, c0, VECS1, C_RCW, C_RCB, CR)
                    dve.wait_ge(xc_hi, b + FIRST)
                    src_s = XC_PAD[:, :, XB0:XB0 + DEC_B * SEG].rearrange("p m (b t) -> p m b t", b=DEC_B)[:, :, :, 0:DEC_S]
                    hp, hs = tight(XC_HI)
                    lp, ls = tight(XC_LO)
                    dve.tensor_tensor(lp, XC_PAD[:, :, 0:SEQ], hp.bitcast(F32), ALU.subtract)
                    dve.tensor_tensor(ls, src_s, hs.bitcast(F32), ALU.subtract).then_inc(xc_ready, 1)
                    dve.wait_ge(slab_used, jobs.adv(4) + 2 * RING)
                    dve.tensor_tensor(pair5(GELU_T[:, :, :]), psv[:, 1, :, :, 0:HALF_T], RB, ALU.mult).then_inc(psum_freed[1], 1)
                    uses[1].adv()
                    jobs.adv(2)
                    uses[0].adv()
                    uses[1].adv()
                    dve.wait_ge(s_ready, b)
                    ip, is_ = tight(I_GATE)
                    dve.tensor_tensor(ip, ip, XC_PAD[:, :, 0:SEQ], ALU.mult)
                    link(dve.tensor_tensor(is_, is_, src_s, ALU.mult))
                    dve.wait_ge(a_ready, b)
                    dve.wait_ge(y_lo, b - 1 + FIRST)
                    sp_, ss_ = tight(A_SQUARE)
                    as_ = A_PAD[:, :, SEQ:WSCAN].rearrange("p m (b t) -> p m b t", b=DEC_B)[:, :, :, 1:HSEG]
                    dve.tensor_tensor(sp_, A_PAD[:, :, 0:SEQ], A_PAD[:, :, 0:SEQ], ALU.mult)
                    link(dve.tensor_tensor(ss_, as_, as_, ALU.mult))
                    flat = lambda t: t[:, :, :].rearrange("p m t -> p (m t)")
                    dve.scalar_tensor_tensor(flat(TANH_T), flat(A_SQUARE), 1.0, flat(TANH_T), ALU.add, ALU.mult).then_inc(v_in, 1)
                    up_p = U_PAD[:, :, 0:SEQ]
                    up_s = U_PAD[:, :, SEQ:WSCAN].rearrange("p m (b t) -> p m b t", b=DEC_B)
                    dve.tensor_copy(up_s[:, :, :, 0], RG_STATE_IN[:, ds(c0, 2), 24:32])
                    dve.wait_ge(v_ready, b)
                    vp, vs = tight(TANH_T)
                    dve.tensor_tensor(up_p, vp, ip, ALU.mult)
                    link(dve.tensor_tensor(up_s[:, :, :, 1:HSEG], vs, is_, ALU.mult))
                    dve.wait_ge(h_out, b - 1 + FIRST)
                    for m in range(2):
                        ins = dve.tensor_tensor_scan(H_PAD[:, m, :], A_PAD[:, m, :], U_PAD[:, m, :], 0.0, ALU.mult, ALU.add)
                        if m == 0:
                            link(ins)
                    ins.then_inc(scan_done, 1)
                    dve.wait_ge(scan_done, b + FIRST)
                    dve.wait_ge(gelu_done, b)
                    dve.wait_ge(y_lo, b - 1 + FIRST)
                    gp, gs = tight(GELU_T)
                    yp, ys_ = tight(Y_F32)
                    dve.tensor_tensor(yp, H_PAD[:, :, 0:SEQ], gp, ALU.mult)
                    dve.tensor_tensor(ys_, H_PAD[:, :, SEQ:WSCAN].rearrange("p m (b t) -> p m b t", b=DEC_B)[:, :, :, 1:HSEG],
                                      gs, ALU.mult).then_inc(y_ready, 1)

            def add_to_x(n_slabs, s, c0, ready):
                dve.wait_ge(slab_used, jobs.adv(n_slabs) + 2 * RING)
                xx = pair4(X[:, ds(c0, 2), :])
                dve.tensor_tensor(xx, xx, psum4(s), ALU.add).then_inc(psum_freed[s], 1)
                u = uses[s].adv()
                if ready:
                    dve.wait_ge(psum_freed[s], u)
                    dve.nop().then_inc(x_ready, 1)

            with loop(dve, 2, {jobs: 12, uses[0]: 1, uses[1]: 1, hi_t: 2}) as j:
                for m in range(2):
                    add_to_x(6, m, 4 * j + 2 * m, True)
                    xn_lo(4 * j + 2 * m, G_FFN, A_HI, A_LO)
            rstd(1)
            dve.wait_ge(std_ready, stds.adv())

            def ffn(hi, lo):
                for g, (g0, gn) in enumerate(GROUPS):
                    with loop(dve, gn // 2, {jobs: 8, uses[0]: 1, uses[1]: 1, blk: 1, ys: 1, step: 1}) as j:
                        b = blk.adv()
                        y = ys.adv()
                        dve.wait_ge(slab_used, jobs.adv(4) + 2 * RING)
                        dve.tensor_tensor(pair5(GATE[:, :, :]), psv[:, 0, :, :, 0:HALF_T], RB, ALU.mult).then_inc(psum_freed[0], 1)
                        uses[0].adv()
                        dve.wait_ge(slab_used, jobs.adv(4) + 2 * RING)
                        dve.wait_ge(silu_done, y)
                        dve.wait_ge(y_lo, b - 1 + FIRST)
                        link(dve.tensor_tensor(pair5(GATED[:, :, :]), psv[:, 1, :, :, 0:HALF_T], pair5(GATE[:, :, :]), ALU.mult))
                        dve.nop().then_inc(psum_freed[1], 1)
                        uses[1].adv()
                        dve.tensor_tensor(pair5(GATED[:, :, :]), pair5(GATED[:, :, :]), RB, ALU.mult).then_inc(y_ready, 1)
                    ks = gn // 2
                    n = 4 if ks % 2 else 2
                    last = g == len(GROUPS) - 1
                    with loop(dve, 4 // n, {jobs: ks * n, uses[0]: n // 2, uses[1]: n // 2, hi_t: n if last else 0}) as j:
                        for m in range(n):
                            add_to_x(ks, m % 2, 4 * j + 2 * m, last)
                            if last:
                                xn_lo(4 * j + 2 * m, None, hi, lo)

            def ple(layer, P_HI, P_LO, P_PROJ, gain, hi, lo):
                dve.wait_ge(misc_done, misc.adv() + FIRST)
                dve.wait_ge(pt_hi, layer + 1)
                dve.tensor_tensor(P_LO[:, :, 0:SEQ], ps[:, 0:4:2, 0:SEQ], P_HI[:, :, 0:SEQ].bitcast(F32), ALU.subtract)
                link(dve.tensor_tensor(P_LO[:, :, SEQ:T], ps[:, 1:4:2, 0:N_STOK], P_HI[:, :, SEQ:T].bitcast(F32), ALU.subtract))
                dve.nop().then_inc(pt_ready, 1)
                dve.nop().then_inc(psum_freed[0], 1)
                uses[0].adv()
                jobs.adv(4)
                uses[0].adv(2)
                uses[1].adv(2)
                with loop(dve, 2, {jobs: 8, uses[0]: 1, uses[1]: 1, hi_t: 0 if hi is None else 2, step: 2,
                                   xf: 2 if hi is None else 0}) as j:
                    for m in range(2):
                        s = (m + 1) % 2
                        jobs.adv(4)
                        dve.wait_ge(psum_freed[s], uses[s].adv())
                        c0 = 4 * j + 2 * m
                        link(dve.tensor_tensor(GATE[:, :, :], GATE[:, :, :], P_PROJ[:, ds(c0, 2), :], ALU.mult))
                        dve.tensor_tensor(X[:, ds(c0, 2), :], X[:, ds(c0, 2), :], GATE[:, :, :], ALU.add).then_inc(x_ready, 1)
                        if hi is not None:
                            xn_lo(c0, gain, hi, lo)
                        else:
                            dve.wait_ge(x_ready, xf.adv())
                            for c in range(2):
                                ins = dve.tensor_scalar(X_GAIN[:, ds(c0 + c, 1), :], X[:, ds(c0 + c, 1), :],
                                                        VECS2[:, ds(C_NF + c + c0, 1)], None, ALU.mult)
                            ins.then_inc(xf_ready, 1)
                if hi is not None:
                    rstd(1)
                    dve.wait_ge(std_ready, stds.adv())

            ffn(A_HI, A_LO)
            ple(0, P_HI0, P_LO0, P_PROJ0, G_MIX + 8, B_HI, B_LO)
            ml = Tally()
            with loop(dve, 4, {jobs: 8, uses[0]: 1, uses[1]: 1, ml: 2, step: 6}) as j:
                for m in range(2):
                    c0 = 4 * j + 2 * m
                    n = ml.adv()
                    dve.wait_ge(slab_used, jobs.adv(4) + 2 * RING)
                    dve.wait_ge(tails_out, 6 + n - 1 + FIRST)
                    dve.wait_ge(xm_copied, n - 1)
                    evac_padded(XM_PAD, m)
                    dve.wait_ge(psum_freed[m], uses[m].adv())
                    dve.wait_ge(pads_ready, 7 + n)
                    dve.wait_ge(xc_silu, n - 1)
                    conv(XM_PAD, CONV_OUT, c0, VECS2, C_MCW, C_MCB, CI)
            dve.wait_ge(misc_done, misc.adv() + FIRST)
            pg = ps[:, 0:2, 0:HALF_T]
            link(dve.memset(RUN_MASK[:, :], 1.0))
            dve.memset(RUN_MASK[:, 0:1], 0.0)
            dve.memset(RUN_MASK[:, SEQ:T:DEC_S], 0.0)
            dve.wait_ge(wgr_loaded, 16 * 14)
            dve.tensor_scalar(I_ROW[:, :].rearrange("p (h n) -> p h n", h=2), pg[0:4], GATE_BIAS[:, 0:1], None, ALU.add)
            dve.tensor_copy(F_ROW[:, :].rearrange("p (h n) -> p h n", h=2), pg[32:36]).then_inc(psum_freed[0], 1)
            dve.wait_ge(psum_freed[0], uses[0].adv())
            dve.tensor_scalar(F_ROW[:, :], F_ROW[:, :], GATE_BIAS[:, 1:2], None, ALU.add).then_inc(f_ready, 1)
            dve.tensor_scalar(RUN_NEG[:, :], RUN_MASK[:, :], 1.0, -NEG, ALU.subtract, ALU.mult)
            dve.wait_ge(ln_ready, 1)
            link(dve.scalar_tensor_tensor(LOG_F[:, :], F_ROW[:, :], 0.0, ABS_F[:, :], ALU.min, ALU.subtract))
            link(dve.tensor_tensor_scan(B_SUM[:, :], RUN_MASK[:, :], LOG_F[:, :], 0.0, ALU.mult, ALU.add))
            link(dve.tensor_tensor(A_ROW[:, :], I_ROW[:, :], B_SUM[:, :], ALU.subtract))
            link(dve.tensor_copy(A_START[:, :], A_ROW[:, :]))
            dve.tensor_scalar(A_START[:, 0:1], A_ROW[:, 0:1], 0.0, None, ALU.max)
            link(dve.tensor_tensor(A_START[:, SEQ:T:DEC_S], A_ROW[:, SEQ:T:DEC_S], M_OLD[:, :], ALU.max))
            link(dve.tensor_tensor_scan(MAX_ROW[:, :], RUN_NEG[:, :], A_START[:, :], 0.0, ALU.add, ALU.max))
            link(dve.tensor_tensor(M_ROW[:, :], B_SUM[:, :], MAX_ROW[:, :], ALU.add))
            dve.tensor_copy(M_OUT[:, 0:1], M_ROW[:, SEQ - 1:SEQ])
            dve.tensor_copy(M_OUT[:, 1:1 + DEC_B], M_ROW[:, SEQ + DEC_S - 1:T:DEC_S])
            b8 = lambda t: t.rearrange("p (b t) -> p b t", b=DEC_B)
            bc8 = lambda t: t.unsqueeze(2).broadcast_to([HEADS, DEC_B, DEC_S])
            dve.tensor_tensor(b8(OLD_W_ROW[:, :]), bc8(M_OLD[:, :]), b8(MAX_ROW[:, SEQ:T]), ALU.subtract)
            dve.tensor_scalar(KEY_W_ROW[:, 0:SEQ], A_ROW[:, 0:SEQ], MAX_ROW[:, SEQ - 1:SEQ], None, ALU.subtract)
            dve.tensor_tensor(b8(KEY_W_ROW[:, SEQ:T]), b8(A_ROW[:, SEQ:T]), bc8(MAX_ROW[:, SEQ + DEC_S - 1:T:DEC_S]),
                              ALU.subtract).then_inc(t1_ready, 1)
            dve.wait_ge(misc_done, misc.adv() + FIRST)
            dve.tensor_copy(KEY_COLS[:, 0:4, :], ps[:, 4, 0:32].rearrange("p (i g) -> p i g", g=8))
            for g in range(2):
                dve.tensor_copy(KEY_WEIGHTS[:, g], ps[0:3 * GROUP_T, 4, 40 + 4 * g:44 + 4 * g].unsqueeze(2).broadcast_to([3 * GROUP_T, HEADS, 4]))
            dve.tensor_copy(KEY_COLS[0:N_STOK, 4, :], ps[0:N_STOK, 4, 32:40]).then_inc(psum_freed[1], 1)
            dve.wait_ge(psum_freed[1], uses[1].adv())
            for g in range(2):
                ins = dve.tensor_tensor(KEY_WEIGHTS[:, g], KEY_WEIGHTS[:, g], SAMPLE_MASK[:, :].unsqueeze(1).broadcast_to([3 * GROUP_T, HEADS, 4]), ALU.mult)
            ins.then_inc(cols_ready, 1)
            dve.wait_ge(rows_ready, 1)
            dve.tensor_scalar(HEAD_SEL[:, :], ONES[0:HEADS, :], IDENT[0:HEADS, 0:1], None, ALU.mult).then_inc(sel_ready, 1)
            heads, units, kwms = Tally(), Tally(), Tally()
            with loop(dve, HEADS, {kwms: DEC_B, misc: 15, uses[0]: 7, uses[1]: 6, heads: 1, units: UNITS, step: 8, cl[0]: 3, cl[1]: 3}) as h:
                n = heads.adv()
                misc.adv(2)
                uses[0].adv(3)
                dve.wait_ge(psum_freed[1], uses[1].adv())
                for i in range(4):
                    dve.tensor_scalar(PROBS[:, PROBS_AT[i]:PROBS_AT[i + 1]], MAX_B[:, i * P:SEQ], KEY_COLS[:, i, ds(h, 1)], 0.0,
                                      ALU.subtract, ALU.max)
                dve.tensor_scalar(PROBS_S[:, :], MAX_B[0:N_STOK, SEQ:T], KEY_COLS[0:N_STOK, 4, ds(h, 1)], 0.0,
                                  ALU.subtract, ALU.max).then_inc(e_ready, 1)
                dve.tensor_scalar(HEAD_SEL[:, :], ONES[0:HEADS, :], IDENT[0:HEADS, ds(h + 1, 1)], None, ALU.mult).then_inc(sel_ready, 1)
                dve.wait_ge(psum_freed[1], uses[1].adv())
                dve.wait_ge(psum_freed[0], uses[0].now() - 1)
                qi = XM[:, ds(4 * h + 3, 1), 0:4 * N_STOK].rearrange("p o (k t) -> p (o k) t", k=4)
                nq = XM[:, ds(4 * h + 2, 1), 0:4 * N_STOK].rearrange("p o (k b t) -> p (o k) b t", k=4, b=DEC_B)
                link(dve.tensor_tensor(qi, Q_T[:, :, SEQ:T], OLD_W[:, :].unsqueeze(1).broadcast_to([P, 4, N_STOK]), ALU.mult))
                dve.tensor_tensor(nq, qi.rearrange("p k (b t) -> p k b t", b=DEC_B),
                                  N_SAMPLES[:, :, ds(h, 1), :].rearrange("p b o k -> p (o k) b").unsqueeze(3)
                                  .broadcast_to([P, 4, DEC_B, DEC_S]), ALU.mult).then_inc(nq_ready, 1)
                dve.wait_ge(vs_hi, n)
                vs = V_STACK[2 * GROUP_T:3 * GROUP_T, ds(4 * h, 2), 0:HD]
                dve.tensor_tensor(vs, ps[2 * GROUP_T:3 * GROUP_T, 0:2, :], vs.bitcast(F32), ALU.subtract).then_inc(psum_freed[0], 1)
                misc.adv(6)
                uses[0].adv(2)
                uses[1].adv()
                dve.wait_ge(misc_done, misc.adv() + FIRST)
                dve.wait_ge(masked, n)
                dve.wait_ge(kt4_done, n)
                dve.tensor_tensor(PROBS_S[:, :], PROBS_S[:, :], ps[0:N_STOK, 5, 0:N_STOK], ALU.mult).then_inc(psum_freed[1], 1)
                uses[1].adv()
                dve.wait_ge(misc_done, misc.adv() + FIRST)
                for i in range(4):
                    ins = dve.tensor_tensor(PROBS[:, PROBS_AT[i]:PROBS_AT[i + 1]], PROBS[:, PROBS_AT[i]:PROBS_AT[i + 1]],
                                            ps[:, i, i * P:SEQ], ALU.mult)
                ins.then_inc(psum_freed[0], 1)
                uses[0].adv()
                misc.adv()
                uses[1].adv()
                dve.wait_ge(misc_done, misc.adv() + FIRST)
                nt = N_SAMPLES[:, :, ds(h, 1), :].rearrange("p b o k -> p (o k) b")
                link(dve.tensor_tensor(nt, nt, OLD_W[:, DEC_S - 1:N_STOK:DEC_S].unsqueeze(1).broadcast_to([P, 4, DEC_B]), ALU.mult))
                dve.tensor_tensor(nt, nt, ps[:, 3, 8:40].rearrange("p (k b) -> p k b", k=4), ALU.add)
                def kwm_lo(b):
                    dve.wait_ge(kwm_hi, kwms.adv())
                    dve.scalar_tensor_tensor(KW_STACK[GROUP_T:2 * GROUP_T, b % 2, :], K_STACK[GROUP_T:2 * GROUP_T, b // 4, :], KEY_WEIGHTS[GROUP_T:2 * GROUP_T, b // 4, ds(h, 1), b % 4],
                                             KW_STACK[GROUP_T:2 * GROUP_T, b % 2, :].bitcast(F32), ALU.mult, ALU.subtract).then_inc(kwm_ready, 1)

                kwm_lo(0)
                kwm_lo(1)
                for v in range(UNITS):
                    dve.wait_ge(unit_done, units.adv() + 2 * FIRST)
                    bank = 4 + 2 * (v % 2)
                    c = C_HALVES[:, v % CSLOTS]
                    b, half = UNIT[v]
                    if b is None:
                        dve.wait_ge(c_loaded[v % CSLOTS], cl[half].adv(2))
                        cl[half].adv()
                        ins = dve.tensor_copy(c, ps[:, bank:bank + 2, :])
                        if half:
                            dve.tensor_copy(N_PROMPT[:, ds(h, 1), :], ps[:, 3, 0:4].unsqueeze(1)).then_inc(n_done, 1)
                    else:
                        cc = c.rearrange("p k v -> p (k v)")
                        ins = dve.scalar_tensor_tensor(cc, cc, OLD_W[:, DEC_S * b + DEC_S - 1:DEC_S * b + DEC_S],
                                                       ps[:, bank:bank + 2, :].rearrange("p k v -> p (k v)"), ALU.mult, ALU.add)
                    ins.then_inc(unit_freed, 1)
                    if b and not half and b + 1 < DEC_B:
                        kwm_lo(b + 1)
                    if v == PROMPT_UNITS[0] - 1:
                        dve.wait_ge(rd_in, n)
                        link(dve.tensor_tensor(DEN, DEN, EXP_NEG_M, ALU.max))
                        link(dve.reciprocal(DEN, DEN))
                        dve.tensor_tensor(SCALE_F, DEN, DEN, ALU.mult)
                misc.adv(2)
                uses[0].adv()
                dve.wait_ge(misc_done, misc.adv() + FIRST)
                link(dve.tensor_tensor(SCALE_F[:, 0:SEQ], SCALE_F[:, 0:SEQ], ps[:, 4, :], ALU.mult))
                dve.tensor_tensor(SCALE_F[:, SEQ:T], SCALE_F[:, SEQ:T], ps[:, 5, 0:N_STOK], ALU.mult).then_inc(psum_freed[1], 1)
                dve.wait_ge(psum_freed[1], uses[1].adv())
                link(dve.nop())
                dve.nop().then_inc(fv_ready, 1)
                dve.wait_ge(sd_ready, n)
                link(dve.reciprocal(SCALE_F, SCALE_F))
                link(dve.tensor_tensor(SCALE_F, SCALE_F, DEN, ALU.mult))
                for c in range(4):
                    hh = XC[:, ds(4 * h + c, 1), :].rearrange("p o t -> p (o t)")
                    ins = dve.scalar_tensor_tensor(hh, hh, VECS2[:, ds(C_MN + c + 4 * h, 1)], SCALE_F, ALU.mult, ALU.mult)
                ins.then_inc(h_done, 1)
            for m in range(4):
                xn_lo(2 * m, G_MIX + 8, B_HI, B_LO)

            def states():
                for s, srcs in ((0, ((RG_ROWS[:, :].rearrange("p (b n) -> p b n", b=3), ps[0:36, 0:3, :]),)),
                                (1, ((ML_ROWS[:, :].rearrange("p (b n) -> p b n", b=4), ps[0:27, 4:8, :]),)),
                                (0, ((N_ROWS[:, 0, :], ps[:, 0, 0:P]),)),
                                (1, ((N_ROWS[0:16, 1, :], ps[0:16, 4, 0:P]),))):
                    dve.wait_ge(misc_done, misc.adv() + FIRST)
                    uses[s].adv()
                    for dst, src in srcs:
                        if s == 0:
                            for slot in range(CSLOTS):
                                dve.wait_ge(c_stored[slot], 16 * HEADS * UNITS // CSLOTS + 16 * FIRST)
                        dve.tensor_copy(dst, src).then_inc(states_out, 1)
                    dve.wait_ge(states_out, 1 + so[0])
                    so[0] += 1
                    dve.nop().then_inc(psum_freed[s], 1)

            for g in range(2):
                if g:
                    states()
                with loop(dve, 2, {jobs: 8, uses[0]: 1, uses[1]: 1, blk: 2, ys: 2}) as j:
                    for m in range(2):
                        b = blk.adv()
                        y = ys.adv()
                        dve.wait_ge(slab_used, jobs.adv(4) + 2 * RING)
                        dve.wait_ge(y_ready, b - 1)
                        dve.tensor_tensor(pair5(GATE[:, :, :]), psv[:, m, :, :, 0:HALF_T], RB, ALU.mult).then_inc(psum_freed[m], 1)
                        uses[m].adv()
                        dve.wait_ge(silu_done, y)
                        dve.wait_ge(y_lo, b - 1 + FIRST)
                        dve.tensor_tensor(GATED[:, :, :], GATE[:, :, :], XC[:, ds(8 * g + 4 * j + 2 * m, 2), :], ALU.mult)\
                            .then_inc(y_ready, 1)
                with loop(dve, 2, {jobs: 8, uses[0]: 1, uses[1]: 1, **({hi_t: 2} if g else {})}) as j:
                    for m in range(2):
                        add_to_x(4, m, 4 * j + 2 * m, bool(g))
                        if g:
                            xn_lo(4 * j + 2 * m, G_FFN + 8, B_HI, B_LO)
            rstd(1)
            dve.wait_ge(std_ready, stds.adv())
            ffn(B_HI, B_LO)
            ple(1, P_HI1, P_LO1, P_PROJ1, None, None, None)
            dve.wait_ge(psum_freed[1], uses[1].adv())
            misc.adv(2)
            dve.reciprocal(RSTD_COLS[:, 0:4], RSTD_COLS[:, 0:4])
            dve.reciprocal(RSTD_COLS[0:N_STOK, 4:5], RSTD_COLS[0:N_STOK, 4:5]).then_inc(std_ready, 1)
            dve.wait_ge(std_ready, stds.adv())
            for i, (t0, n) in enumerate(TOKEN_TILES):
                s = i % 2
                if i:
                    dve.wait_ge(misc_done, misc.adv() + FIRST)
                if i >= 2:
                    dve.wait_ge(y_stored[s], 16 * (i // 2))
                dve.tensor_scalar(Y_ROWS[0:n, s, :].rearrange("p (b c) -> p b c", b=2), ps[0:n, 4 * s:4 * s + 2, :],
                                  RSTD_COLS[0:n, i:i + 1], None, ALU.mult).then_inc(out_rows, 1)
                dve.wait_ge(out_rows, i + 1)
                dve.nop().then_inc(psum_freed[s], 1)

        @block.tensor
        def _(pe):
            slabs, blk = Tally(), Tally()
            uses = [Tally(), Tally()]
            phase = [0]

            def use(s):
                before = uses[s].adv() - 1
                if not is_zero(before):
                    pe.wait_ge(psum_freed[s], before)

            def job(s, pairs, operand, before=None):
                use(s)
                for i in range(pairs):
                    if before:
                        before(i)
                    pe.wait_ge(lo_ready, slabs.adv() + RING)
                    w = phase[0] % 4
                    phase[0] += 1
                    for k in range(2):
                        hi, lo = operand(2 * i + k)
                        for m in range(2):
                            wc = slice(m * P, m * P + P)
                            for q, (a, x) in enumerate(((W_HI, hi), (W_HI, lo), (W_LO, hi))):
                                for h in range(2):
                                    ins = pe.matmul(ps[:, 4 * s + 2 * m + h, 0:HALF_T], a[:, w, k, wc], x[:, h * HALF_T:h * HALF_T + HALF_T],
                                                    start=i == 0 and k == 0 and q == 0,
                                                    stop=i == pairs - 1 and k == 1 and q == 2)
                    ins.then_inc(slab_used, 1)

            def norm(s, acc):
                use(s)
                pe.wait_ge(acc_ready, acc)
                for h in range(2):
                    for k in range(2):
                        ins = pe.matmul(ps[:, 4 * s + h, 0:HALF_T], ONES[:, :], SQUARE_SUM[:, k, h * HALF_T:h * HALF_T + HALF_T], start=k == 0, stop=k == 1)
                ins.then_inc(misc_done, 1)

            def chunks(hi, lo):
                return lambda k: (hi[:, k, :], lo[:, k, :])

            def starts(acc, xn0):
                def before(i):
                    if i == CX // 2 - 1:
                        norm(1, acc)
                    pe.wait_ge(xn_ready, xn0 + i + 1)
                return before


            give_credit(pe, slab_used, misc_done, unit_done)
            pe.wait_ge(const_ready, 1)
            for i, (t0, n) in enumerate(TOKEN_TILES):
                s = i % 2
                use(s)
                pe.wait_ge(x_loaded[i], 16)
                for c in range(CX):
                    ins = pe.transpose(ps[:, 4 * s + c // 4, (c % 4) * P:(c % 4) * P + n], X_ROWS[0:n, i, c * P:c * P + P],
                                       IDENT[0:n, 0:n])
                ins.then_inc(misc_done, 1)
            pe.wait_ge(rows_loaded, ROWS_LOADED)
            use(1)
            pe.transpose(ps[:, 4, 0:P], VEC_ROWS[:, 0, :], IDENT[:, :])
            pe.transpose(ps[:, 4, P:P + 120], VEC_ROWS[0:120, 1, :], IDENT[0:120, 0:120])
            pe.transpose(ps[:, 4, 256:384], N_IN_ROWS[:, :], IDENT[:, :])
            for c in range(CR):
                pe.transpose(ps[:, 5, c * 32:c * 32 + 32], RG_IN_ROWS[:, c * P:c * P + P], IDENT[0:32, 0:32])
            for c in range(CI):
                ins = pe.transpose(ps[:, 6, c * 24:c * 24 + 24], ML_IN_ROWS[:, c * P:c * P + P], IDENT[0:24, 0:24])
            ins.then_inc(misc_done, 1)

            def rg_block(before=None):
                job(0, 4, chunks(A_HI, A_LO), before)
                job(1, 4, chunks(A_HI, A_LO))
                pe.wait_ge(xc_ready, blk.adv())
                job(0, 1, chunks(XC_HI, XC_LO))
                job(1, 1, chunks(XC_HI, XC_LO))

            rg_block(starts(4, 0))
            rg_block()
            with loop(pe, 2, {slabs: 20, uses[0]: 4, uses[1]: 4, blk: 2}) as j:
                for jj in range(2):
                    rg_block()
            with loop(pe, 2, {slabs: 12, uses[0]: 1, uses[1]: 1}) as j:
                for m in range(2):
                    job(m, 6, chunks(Y_HI, Y_LO), lambda i: pe.wait_ge(y_lo, i + 1 + FIRST))
            y_done = [6]

            def ffn(hi, lo, gh, gl, acc, xn0):
                for g, (g0, gn) in enumerate(GROUPS):
                    if g == 0:
                        job(0, 4, chunks(hi, lo), starts(acc, xn0))
                        job(1, 4, chunks(hi, lo))
                    with loop(pe, gn // 2 - (g == 0), {slabs: 8, uses[0]: 1, uses[1]: 1}) as j:
                        for s in range(2):
                            job(s, 4, chunks(hi, lo))
                    ks = gn // 2
                    n = 4 if ks % 2 else 2
                    with loop(pe, 4 // n, {slabs: ks * n, uses[0]: n // 2, uses[1]: n // 2}) as j:
                        for m in range(n):
                            job(m % 2, ks, chunks(gh, gl), lambda i: pe.wait_ge(y_lo, y_done[0] + i + 1 + FIRST))
                    y_done[0] += ks

            def turn_out(i):
                (t0, n), s = TOKEN_TILES[i], i % 2
                use(s)
                for c in range(CX):
                    ins = pe.transpose(ps[0:n, 4 * s + c // 4, (c % 4) * P:(c % 4) * P + P], X_GAIN[:, c, t0:t0 + n], IDENT[:, :])
                ins.then_inc(misc_done, 1)

            def ple(layer, P_HI, P_LO, hi, lo, acc, xn0):
                pe.wait_ge(p_loaded, 32 * (layer + 1))
                use(0)
                for c in range(2):
                    for i, (t0, n) in enumerate(TOKEN_TILES):
                        dst = ps[:, 2 * c, t0:t0 + n] if t0 < SEQ else ps[:, 2 * c + 1, 0:n]
                        ins = pe.transpose(dst, P_ROWS[0:n, i, c * P:c * P + P], IDENT[0:n, 0:n])
                ins.then_inc(misc_done, 1)
                pe.wait_ge(pt_ready, layer + 1)
                for m in range(4):
                    job((m + 1) % 2, 1, chunks(P_HI, P_LO))
                with loop(pe, 2, {slabs: 8, uses[0]: 1, uses[1]: 1}) as j:
                    for m in range(2):
                        job((m + 1) % 2, 4, chunks(hi, lo), lambda i: pe.wait_ge(xn_ready, xn0 + i + 1))
                if layer:
                    pe.wait_ge(xf_ready, 4)
                    turn_out(0)
                    use(1)
                    pe.wait_ge(acc_ready, acc)
                    for i, (t0, n) in enumerate(TOKEN_TILES):
                        for k in range(2):
                            ins = pe.matmul(ps[0:n, 4, i:i + 1], SQUARE_SUM[:, k, t0:t0 + n], ONES[:, 0:1], start=k == 0, stop=k == 1)
                    ins.then_inc(misc_done, 1)

            ffn(A_HI, A_LO, G_HI, G_LO, 8, 4)
            ple(0, P_HI0, P_LO0, A_HI, A_LO, None, 8)
            job(0, 4, chunks(B_HI, B_LO), starts(12, 12))
            job(1, 4, chunks(B_HI, B_LO))
            with loop(pe, 3, {slabs: 8, uses[0]: 1, uses[1]: 1}) as j:
                for s in range(2):
                    job(s, 4, chunks(B_HI, B_LO))
            use(0)
            pe.wait_ge(et_ready, 2)
            pe.wait_ge(xm_copied, 8)
            order = [CI + c for c in range(CI)] + list(range(CI))
            for i, c in enumerate(order):
                if c < CI and c % 2 == 0:
                    pe.wait_ge(xc_silu, c // 2 + 1)
                for hf in range(2):
                    src = (XC if c < CI else XM)[:, c % CI, hf * HALF_T:hf * HALF_T + HALF_T]
                    ins = pe.matmul(ps[0:36, hf, 0:HALF_T], GATE_FOLD[:, c, :], src, start=i == 0, stop=i == 2 * CI - 1)
            ins.then_inc(misc_done, 1)
            use(1)
            pe.wait_ge(rows_ready, 1)
            for i, (t0, n) in enumerate(TOKEN_TILES):
                for k, t in enumerate((A_ROW, KEY_W_ROW)):
                    pe.transpose(ps[0:n, 4, i * 8 + 4 * k:i * 8 + 4 * k + 4], t[:, t0:t0 + n], IDENT[0:4, 0:4])
            for g in range(2):
                ins = pe.transpose(ps[0:3 * GROUP_T, 4, 40 + 4 * g:44 + 4 * g], KEY_W_STACK[:, g, :], IDENT[0:4, 0:4])
            ins.then_inc(misc_done, 1)
            pe.wait_ge(cols_ready, 1)
            heads, units, kws = Tally(), Tally(), Tally()
            cl = [Tally(16) for _ in range(CSLOTS)]
            with loop(pe, HEADS, {uses[0]: 7, uses[1]: 6, heads: 1, units: UNITS, kws: DEC_B,
                                  **{t: UNITS // CSLOTS for t in cl}}) as h:
                n = heads.adv()
                done = lambda ins: ins.then_inc(misc_done, 1)
                use(0)
                pe.wait_ge(ht_ready, n)
                pe.wait_ge(wbd_ready, n)

                def v_rows(i, bank):
                    t0, nt = TOKEN_TILES[i]
                    for c in range(4):
                        ins = pe.matmul(ps[0:nt, bank, c * P:c * P + P], HEAD_T[:, c, t0:t0 + nt], QKV_DIAG[:, 2, c, :],
                                        start=True, stop=True)
                    return ins

                for i in range(4):
                    ins = v_rows(i, i)
                done(ins)
                use(1)
                v_rows(4, 4)
                pe.wait_ge(sel_ready, n)
                pe.matmul(ps[:, 5, :], HEAD_SEL[:, :], MAX_ROW[:, 0:SEQ], start=True, stop=True)
                pe.matmul(ps[:, 6, :], HEAD_SEL[:, :], EXP_ROW[:, 0:SEQ], start=True, stop=True)
                for k, t in enumerate((MAX_ROW[:, SEQ:T], EXP_ROW[:, SEQ:T], OLD_W_ROW[:, :])):
                    ins = pe.matmul(ps[:, 7, k * N_STOK:k * N_STOK + N_STOK], HEAD_SEL[:, :], t, start=True, stop=True)
                done(ins)
                def project(i, order):
                    for s in order:
                        use(s)
                        for m in range(2):
                            c = 2 * s + m
                            for hf in range(2):
                                ins = pe.matmul(ps[:, 4 * s + 2 * m + hf, 0:HALF_T], QKV_DIAG[:, i, c, :],
                                                XC[:, ds(4 * h + c, 1), hf * HALF_T:hf * HALF_T + HALF_T].rearrange("p o t -> p (o t)"),
                                                start=True, stop=True)
                        done(ins)

                project(0, (0, 1))
                use(0)
                pe.wait_ge(stack_ready, 2 * n - 1)
                for g in range(2):
                    for c in range(4):
                        ins = pe.matmul(ps[0:3 * GROUP_T, g, c * P:c * P + P], X_STACK[g][:, c, :], QKV_DIAG[:, 2, c, :],
                                        start=True, stop=True)
                done(ins)
                project(1, (1, 0))
                pe.wait_ge(psum_freed[1], uses[1].now())
                use(0)

                def k_rows(i, bank):
                    t0, nt = TOKEN_TILES[i]
                    for c in range(4):
                        ins = pe.transpose(ps[0:nt, bank, c * P:c * P + P], HEAD_T[:, c, t0:t0 + nt], IDENT[:, :])
                    return ins

                for i in range(4):
                    ins = k_rows(i, i)
                done(ins)
                use(1)
                pe.wait_ge(stack_ready, 2 * n)
                for c in range(4):
                    pe.matmul(ps[0:N_STOK, 5, 0:N_STOK], HEAD_T[:, c, SEQ:T], Q_T[:, c, SEQ:T], start=c == 0, stop=c == 3)
                for g in range(2):
                    for c in range(4):
                        ins = pe.transpose(ps[0:3 * GROUP_T, 4 + 2 * g, c * P:c * P + P], X_STACK[g][:, c, :], IDENT[:, :])
                done(ins)
                use(0)
                for i in range(4):
                    for c in range(4):
                        ins = pe.matmul(ps[:, i, i * P:SEQ], HEAD_T[:, c, i * P:i * P + P], Q_T[:, c, i * P:SEQ],
                                        start=c == 0, stop=c == 3)
                done(ins)
                use(1)
                pe.wait_ge(psum_freed[0], uses[0].now())
                for vb in range(4):
                    for i in range(4):
                        ins = pe.matmul(ps[:, 4 + vb, i * P:SEQ], V_ROWS[:, i, vb * P:vb * P + P], PROBS[:, PROBS_AT[i]:PROBS_AT[i + 1]],
                                        start=i == 0, stop=i == 3)
                done(ins)
                use(0)
                for i in range(4):
                    pe.matmul(ps[:, 0, i * P:SEQ], ONES[:, :], PROBS[:, PROBS_AT[i]:PROBS_AT[i + 1]], start=i == 0, stop=i == 3)
                pe.wait_ge(nq_ready, n)
                pe.matmul(ps[:, 2, 0:N_STOK], ONES[0:N_STOK, :], PROBS_S[:, :], start=True, stop=False)
                for c in range(4):
                    pe.matmul(ps[:, 2, 0:N_STOK], ONES[:, :],
                              XM[:, ds(4 * h + 2, 1), c * N_STOK:c * N_STOK + N_STOK].rearrange("p o t -> p (o t)"), start=False, stop=c == 3)
                pe.wait_ge(kt4_done, n)
                for kb in range(4):
                    for g in range(2):
                        pe.matmul(ps[:, 3, 8 + 8 * kb + 4 * g:12 + 8 * kb + 4 * g], K_STACK[0:GROUP_T, g, kb * P:kb * P + P],
                                  KEY_WEIGHTS[0:GROUP_T, g, ds(h, 1), :].rearrange("p o b -> p (o b)"), start=True, stop=True)
                done(pe.matmul(ps[0:N_STOK, 1, :], PROBS_S[:, :], V_ROWS[0:N_STOK, 4, :], start=True, stop=False))
                pe.wait_ge(psum_freed[1], uses[1].now())
                for v in range(UNITS):
                    u = units.adv()
                    bank, slot = 4 + 2 * (v % 2), v % CSLOTS
                    pe.wait_ge(unit_freed, u - 2 + 2 * FIRST)
                    cl[slot].adv()
                    b, half = UNIT[v]
                    if b is None:
                        for kb in range(2):
                            for i in range(4):
                                kc = 2 * half + kb
                                pe.matmul(ps[:, 3, kc:kc + 1], K_WEIGHTED[:, i, kc * P:kc * P + P], ONES[:, 0:1], start=i == 0, stop=i == 3)
                                ins = pe.matmul(ps[:, bank + kb, :], K_WEIGHTED[:, i, kc * P:kc * P + P], V_ROWS[:, i, :],
                                                start=i == 0, stop=i == 3)
                    else:
                        pe.wait_ge(c_loaded[slot], cl[slot].now())
                        if v == 0:
                            pe.wait_ge(qz_ready, n)
                        for kb in range(2):
                            ins = pe.matmul(ps[0:N_STOK, 1, :], Q_T[:, 2 * half + kb, b * N_STOK:b * N_STOK + N_STOK], C_HALVES[:, slot, kb, :],
                                            start=False, stop=v == UNITS - 1 and kb == 1)
                        if v == UNITS - 1:
                            done(ins)
                        if not half:
                            pe.wait_ge(kwm_ready, kws.adv())
                        for kb in range(2):
                            kc = 2 * half + kb
                            ins = pe.matmul(ps[:, bank + kb, :], KW_STACK[:, b % 2, kc * P:kc * P + P],
                                            V_STACK[0:3 * GROUP_T, ds(4 * h + b // 4, 1), 0:HD].rearrange("p o v -> p (o v)"),
                                            start=True, stop=True)
                    ins.then_inc(unit_done, 1)
                pe.wait_ge(numt_ready, n)
                for c in range(4):
                    ins = pe.matmul(ps[:, 0, c * N_STOK:c * N_STOK + N_STOK], V_ROWS[0:N_STOK, 4, c * P:c * P + P], IDENT[0:N_STOK, 0:N_STOK], start=True, stop=True)
                done(ins)
                use(1)
                pe.wait_ge(unit_freed, units.now() + 2 * FIRST)
                for c in range(4):
                    pe.matmul(ps[:, 4, :], ONES[:, :], K_WEIGHTED[:, c, :], start=c == 0, stop=c == 3)
                pe.wait_ge(sqh_ready, n)
                for c in range(4):
                    ins = pe.matmul(ps[:, 5, 0:N_STOK], ONES[:, :], XM[:, ds(4 * h + c, 1), SEQ:T].rearrange("p o t -> p (o t)"),
                                    start=c == 0, stop=c == 3)
                done(ins)
            def states():
                use(0)
                for c in range(CR):
                    ins = pe.transpose(ps[0:36, c // 4, (c % 4) * P:(c % 4) * P + P], RG_STATE_OUT[:, c, :], IDENT[:, :])
                ins.then_inc(misc_done, 1)
                use(1)
                for c in range(CI):
                    ins = pe.transpose(ps[0:27, 4 + c // 4, (c % 4) * P:(c % 4) * P + P], ML_CONV_OUT[:, c, :], IDENT[:, :])
                ins.then_inc(misc_done, 1)
                use(0)
                pe.wait_ge(n_done, HEADS)
                pe.transpose(ps[:, 0, 0:P], N_SAMPLES[:, :, :, :].rearrange("p b h k -> p (b h k)"), IDENT[:, :]).then_inc(misc_done, 1)
                use(1)
                pe.transpose(ps[0:16, 4, 0:P], N_PROMPT[:, :, :].rearrange("p h k -> p (h k)"), IDENT[:, :]).then_inc(misc_done, 1)

            y0 = y_done[0]
            for g in range(2):
                if g:
                    states()
                with loop(pe, 2, {slabs: 8, uses[0]: 1, uses[1]: 1}) as j:
                    for s in range(2):
                        job(s, 4, chunks(B_HI, B_LO), lambda i: pe.wait_ge(xn_ready, 16 + i + 1))
                with loop(pe, 2, {slabs: 8, uses[0]: 1, uses[1]: 1}) as j:
                    for s in range(2):
                        job(s, 4, chunks(A_HI, A_LO), lambda i: pe.wait_ge(y_lo, y0 + 4 * g + i + 1 + FIRST))
            y_done[0] += 8
            ffn(B_HI, B_LO, A_HI, A_LO, 16, 20)
            ple(1, P_HI1, P_LO1, B_HI, B_LO, 20, 24)
            for i in range(1, len(TOKEN_TILES)):
                turn_out(i)



_OUTS = [("y_prompt", (1, 512, 1024)), ("y_sample", (8, 8, 1024)),
         ("rg_conv_p", (1, 1, 3, 1536)), ("rg_h_p", (1, 1, 1536)), ("ml_conv_p", (1, 1, 3, 2048)),
         ("ml_C_p", (1, 1, 4, 512, 512)), ("ml_n_p", (1, 1, 4, 512)), ("ml_m_p", (1, 1, 4)),
         ("rg_conv_s", (1, 8, 3, 1536)), ("rg_h_s", (1, 8, 1536)), ("ml_conv_s", (1, 8, 3, 2048)),
         ("ml_C_s", (1, 8, 4, 512, 512)), ("ml_n_s", (1, 8, 4, 512)), ("ml_m_s", (1, 8, 4))]


def kernel(**inputs):
    import numpy as _np
    import concourse.bacc as _bacc
    from concourse import mybir as _mybir
    from concourse.bass_utils import run_bass_kernel_spmd as _run

    nc = _bacc.Bacc("TRN2", target_bir_lowering=False, num_devices=1, dynamic_dma_scratch_size=1024)
    arrays, ins, outs = {}, {}, {}
    for name in inputs:
        a = _np.ascontiguousarray(inputs[name])
        arrays[f"in_{name}_dram"] = a
        ins[name] = nc.dram_tensor(f"in_{name}_dram", a.shape, _mybir.dt.from_np(a.dtype), kind="ExternalInput").ap()
    for name, shape in _OUTS:
        outs[name] = nc.dram_tensor(f"out_{name}_dram", shape, _mybir.dt.float32, kind="ExternalOutput").ap()
    hybrid_trunk(nc, ins, outs)
    r = _run(nc, [arrays], core_ids=[0])
    return tuple(r.results[0][f"out_{name}_dram"] for name, _ in _OUTS)
```
